# Optimizing a Trainium2 kernel written in Bass

```python
import jax, jax.numpy as jnp
from jax import lax
import numpy as np
import jax
import jax.numpy as jnp

D_MODEL = 1024
BATCH = 1
SEQ = 512
DEPTH = 1

CHUNK = 64
SUB_CHUNK = 16
HG_DK = 128
HG_HEADS = D_MODEL // HG_DK
HG_DV = D_MODEL // HG_HEADS
HG_FD = HG_HEADS * HG_DK
HG_DI = HG_HEADS * HG_DV
LB_TAIL_LOGIT = 2.0
GM_BLOCK = 128
GM_WIDTH = D_MODEL
GM_GROUPS = 8
GM_CG = GM_WIDTH // GM_GROUPS
D_FF = -(-8 * D_MODEL // (3 * 256)) * 256
IN_WIDTH = 2 * HG_FD + 2 * HG_DI + 2 * GM_WIDTH + 2 * D_MODEL
IN_SPLITS = (HG_FD, 2 * HG_FD, 2 * HG_FD + HG_DI, 2 * HG_FD + 2 * HG_DI,
             2 * HG_FD + 2 * HG_DI + GM_WIDTH, 2 * HG_FD + 2 * HG_DI + 2 * GM_WIDTH,
             2 * HG_FD + 2 * HG_DI + 2 * GM_WIDTH + D_MODEL)
DEEPNORM_ALPHA = (2.0 * DEPTH) ** 0.25
DEEPNORM_BETA = (8.0 * DEPTH) ** -0.25
LN_EPS = 1e-5
RMS_EPS = 1e-6


def _layer_norm(x):
    x = x.astype(jnp.float32)
    xc = x - jnp.mean(x, axis=-1, keepdims=True)
    return xc * lax.rsqrt(jnp.mean(xc * xc, axis=-1, keepdims=True) + LN_EPS)

def _to_chunks(t, heads):
    b, s, _ = t.shape
    return t.reshape(b, s // CHUNK, CHUNK, heads, -1).transpose(0, 3, 1, 2, 4)

def hgrn2_mixer(zq, zf, zi, zg, lower_bound, norm_w):
    b_, s_, _ = zq.shape
    n_sub = CHUNK // SUB_CHUNK
    f = lower_bound + (1.0 - lower_bound) * jax.nn.sigmoid(zf.astype(jnp.float32))
    q = _to_chunks(jax.nn.silu(zq.astype(jnp.float32)), HG_HEADS)
    k = _to_chunks(1.0 - f, HG_HEADS)
    log_f = _to_chunks(jnp.log(f), HG_HEADS)
    v = _to_chunks(zi.astype(jnp.float32), HG_HEADS)
    cum = jnp.cumsum(log_f, axis=3)
    cum_last = cum[:, :, :, -1:, :]

    u_chunk = jnp.einsum('bhnlk,bhnlv->bhnkv', k * jnp.exp(cum_last - cum), v)
    decay = jnp.exp(cum_last[:, :, :, 0, :])

    def step(state, inp):
        dec, upd = inp
        return dec[..., None] * state + upd, state

    state0 = jnp.zeros((b_, HG_HEADS, HG_DK, HG_DV), jnp.float32)
    _, s_prev = lax.scan(step, state0, (jnp.moveaxis(decay, 2, 0), jnp.moveaxis(u_chunk, 2, 0)))
    s_prev = jnp.moveaxis(s_prev, 0, 2)
    o_inter = jnp.einsum('bhnlk,bhnkv->bhnlv', q * jnp.exp(cum), s_prev)

    shp = q.shape[:3] + (n_sub, SUB_CHUNK, HG_DK)
    ref = (cum - log_f)[:, :, :, ::SUB_CHUNK, :]
    q_sub = q.reshape(shp) * jnp.exp(cum.reshape(shp) - ref[:, :, :, :, None, :])
    key_pos = jnp.arange(CHUNK)
    sub_idx = jnp.arange(n_sub)
    key_ok = key_pos[None, :] < (sub_idx[:, None] + 1) * SUB_CHUNK
    expo = ref[:, :, :, :, None, :] - cum[:, :, :, None, :, :]
    k_sub = k[:, :, :, None] * jnp.exp(jnp.where(key_ok[:, :, None], expo, -jnp.inf))
    scores = jnp.einsum('bhnimk,bhnisk->bhnims', q_sub, k_sub)
    q_pos = sub_idx[:, None] * SUB_CHUNK + jnp.arange(SUB_CHUNK)[None, :]
    causal = key_pos[None, None, :] <= q_pos[:, :, None]
    scores = jnp.where(causal, scores, 0.0)
    o_intra = jnp.einsum('bhnims,bhnsv->bhnimv', scores, v).reshape(o_inter.shape)

    o = (o_inter + o_intra).transpose(0, 2, 3, 1, 4).reshape(b_, s_, HG_HEADS, HG_DV)
    o = o * lax.rsqrt(jnp.mean(o * o, axis=-1, keepdims=True) + RMS_EPS) * norm_w
    gate = jax.nn.silu(zg.astype(jnp.float32)).reshape(b_, s_, HG_HEADS, HG_DV)
    return (o * gate).reshape(b_, s_, HG_DI)

def gmlp_mixer(zu, zv, ln_w, ln_b, w_s, b_s):
    b_, s_, _ = zu.shape
    u = jax.nn.gelu(zu.astype(jnp.float32), approximate=False)
    v = jax.nn.gelu(zv.astype(jnp.float32), approximate=False)
    v = _layer_norm(v) * ln_w + ln_b
    v = v.reshape(b_, s_ // GM_BLOCK, GM_BLOCK, GM_GROUPS, GM_CG)
    pos = jnp.arange(GM_BLOCK) // CHUNK
    mask = pos[:, None] >= pos[None, :]
    w = jnp.where(mask[None], w_s, 0.0)
    sv = jnp.einsum('gts,bnsgc->bntgc', w, v) + b_s.T[None, None, :, :, None]
    return u * sv.reshape(b_, s_, GM_WIDTH)

def first_inputs(seed: int = 0) -> dict:
    key = jax.random.key(seed)
    ks = jax.random.split(key, 24)

    def nrm(k, shape, scale):
        return jax.random.normal(k, shape, jnp.float32) * scale

    L = DEPTH
    return {
        "x": nrm(ks[0], (BATCH, SEQ, D_MODEL), 1.0),
        "c": nrm(ks[1], (BATCH, D_MODEL), 1.0),
        "w_ada": nrm(ks[2], (L, D_MODEL, 6 * D_MODEL), D_MODEL ** -0.5),
        "b_ada": nrm(ks[3], (L, 6 * D_MODEL), 0.01),
        "w_in": nrm(ks[4], (L, D_MODEL, IN_WIDTH), D_MODEL ** -0.5),
        "b_gate": nrm(ks[5], (L, 2, D_MODEL), 0.01),
        "hgrn_lb_logits": nrm(ks[6], (L + 1, HG_FD), 0.1).at[L].add(LB_TAIL_LOGIT),
        "hgrn_norm_w": 1.0 + nrm(ks[7], (L, HG_DV), 0.02),
        "w_proj_a": nrm(ks[8], (L, HG_DI, D_MODEL), HG_DI ** -0.5),
        "gmlp_ln_w": 1.0 + nrm(ks[9], (L, GM_WIDTH), 0.02),
        "gmlp_ln_b": nrm(ks[10], (L, GM_WIDTH), 0.02),
        "gmlp_ws": nrm(ks[11], (L, GM_GROUPS, GM_BLOCK, GM_BLOCK), GM_BLOCK ** -0.5),
        "gmlp_bs": 1.0 + nrm(ks[12], (L, GM_GROUPS, GM_BLOCK), 0.1),
        "w_proj_b": nrm(ks[13], (L, GM_WIDTH, D_MODEL), GM_WIDTH ** -0.5),
        "w_out": nrm(ks[14], (L, D_MODEL, D_MODEL), DEEPNORM_BETA * D_MODEL ** -0.5),
        "ln1_w": 1.0 + nrm(ks[15], (L, D_MODEL), 0.02),
        "ln1_b": nrm(ks[16], (L, D_MODEL), 0.02),
        "w_ffn_in": nrm(ks[17], (L, D_MODEL, 2 * D_FF), D_MODEL ** -0.5),
        "w_ffn_out": nrm(ks[18], (L, D_FF, D_MODEL), DEEPNORM_BETA * D_FF ** -0.5),
        "ln2_w": 1.0 + nrm(ks[19], (L, D_MODEL), 0.02),
        "ln2_b": nrm(ks[20], (L, D_MODEL), 0.02),
    }

def first_block(x, c, w_ada, b_ada, w_in, b_gate, hgrn_lb_logits, hgrn_norm_w, w_proj_a,
              gmlp_ln_w, gmlp_ln_b, gmlp_ws, gmlp_bs, w_proj_b, w_out, ln1_w, ln1_b,
              w_ffn_in, w_ffn_out, ln2_w, ln2_b):
    lower_bounds = jnp.cumsum(jax.nn.softmax(hgrn_lb_logits.astype(jnp.float32), axis=0), axis=0)
    h = x.astype(jnp.float32)
    cond = jax.nn.silu(c.astype(jnp.float32))
    for l in range(DEPTH):
        mod = cond @ w_ada[l] + b_ada[l]
        sh1, sc1, g1, sh2, sc2, g2 = [m[:, None, :] for m in jnp.split(mod, 6, axis=-1)]

        u = _layer_norm(h) * (1.0 + sc1) + sh1
        z = u @ w_in[l]
        zq, zf, zi, zg, zu, zv, zga, zgb = jnp.split(z, IN_SPLITS, axis=-1)
        y_a = hgrn2_mixer(zq, zf, zi, zg, lower_bounds[l], hgrn_norm_w[l]) @ w_proj_a[l]
        y_b = gmlp_mixer(zu, zv, gmlp_ln_w[l], gmlp_ln_b[l], gmlp_ws[l], gmlp_bs[l]) @ w_proj_b[l]
        gate_a = jax.nn.sigmoid(zga + b_gate[l, 0])
        gate_b = jax.nn.sigmoid(zgb + b_gate[l, 1])
        mix = (gate_a * y_a + gate_b * y_b) @ w_out[l]
        h = _layer_norm(DEEPNORM_ALPHA * h + g1 * mix) * ln1_w[l] + ln1_b[l]

        u2 = _layer_norm(h) * (1.0 + sc2) + sh2
        a, bb = jnp.split(u2 @ w_ffn_in[l], 2, axis=-1)
        ffn = (jax.nn.silu(a) * bb) @ w_ffn_out[l]
        h = _layer_norm(DEEPNORM_ALPHA * h + g2 * ffn) * ln2_w[l] + ln2_b[l]
    return h.astype(x.dtype)


_first_inputs = first_inputs


def first_inputs(seed=0):
    import zlib

    import numpy as np

    out = dict(_first_inputs(seed))
    spreads = {}
    factors = {'b_ada': 6.447,
     'b_gate': 8.0,
     'hgrn_norm_w': 8.0,
     'gmlp_ln_w': 8.0,
     'gmlp_ln_b': 8.0,
     'gmlp_bs': 3.77,
     'ln1_w': 2.794,
     'ln1_b': 2.771,
     'ln2_w': 2.826,
     'ln2_b': 2.949}
    for name, (base, spread) in spreads.items():
        noise = np.random.default_rng([zlib.crc32(name.encode()), seed]).standard_normal(out[name].shape)
        drawn = base * np.exp(spread * noise) if base else spread * noise
        out[name] = __import__('jax').numpy.asarray(drawn.astype(out[name].dtype))
    for name, factor in factors.items():
        out[name] = (out[name] * factor).astype(out[name].dtype)
    return out


_narrow_inputs = first_inputs


def first_inputs(seed=0):

    out = dict(_narrow_inputs(seed))
    wider = {'hgrn_norm_w': 5.21,
     'gmlp_ln_w': 5.87,
     'gmlp_ln_b': 5.86,
     'ln1_w': 3.2,
     'ln1_b': 3.23,
     'ln2_w': 3.1,
     'ln2_b': 3.18}
    for name, times in wider.items():
        mean = out[name].mean()
        out[name] = (mean + times * (out[name] - mean)).astype(out[name].dtype)
    return out


DEPTH_2 = 2

HEAD_DIM = 64
ATTN_Q_HEADS = 8
ATTN_KV_HEADS = 2
ATTN_GROUP = ATTN_Q_HEADS // ATTN_KV_HEADS
ATTN_WIDTH = ATTN_Q_HEADS * HEAD_DIM
ATTN_KV_WIDTH = ATTN_KV_HEADS * HEAD_DIM
WINDOW = 128
ATTN_BLOCK = 128
RWKV_HEADS = 8
RWKV_WIDTH = RWKV_HEADS * HEAD_DIM
DECAY_LORA = 64
ICLR_LORA = 64
GATE_LORA = 128
RWKV_SIZES = (RWKV_WIDTH, RWKV_WIDTH, RWKV_WIDTH, DECAY_LORA, ICLR_LORA, GATE_LORA)
RWKV_COLS = sum(RWKV_SIZES)
RWKV_LN_EPS = 64e-5
RET_HEADS = 8
RET_WIDTH = RET_HEADS * HEAD_DIM
RET_CHUNK = 128
ROPE_BASE = 10000.0
N_BRANCH = 3
IN_SIZES = (ATTN_WIDTH, ATTN_KV_WIDTH, ATTN_KV_WIDTH, RWKV_COLS,
            RET_WIDTH, RET_WIDTH, RET_WIDTH, RET_WIDTH, N_BRANCH * D_MODEL)
IN_WIDTH_2 = sum(IN_SIZES)
D_FF_2 = -((-8 * D_MODEL) // (3 * 256)) * 256
NORM_EPS = 1e-6


def _split(t, sizes):
    out, start = [], 0
    for s in sizes:
        out.append(t[..., start:start + s])
        start += s
    return out

def _rms(x, eps=NORM_EPS):
    xf = x.astype(jnp.float32)
    return (xf * lax.rsqrt(jnp.mean(xf * xf, axis=-1, keepdims=True) + eps)).astype(x.dtype)

def sliding_window_attention(q, k, v, sinks):
    B, T = q.shape[0], q.shape[1]
    C = ATTN_BLOCK
    NB = T // C
    qb = q.reshape(B, NB, C, ATTN_KV_HEADS, ATTN_GROUP, HEAD_DIM)

    def band(t):
        tb = t.reshape(B, NB, C, ATTN_KV_HEADS, HEAD_DIM)
        prev = jnp.concatenate([jnp.zeros_like(tb[:, :1]), tb[:, :-1]], axis=1)
        return jnp.concatenate([prev, tb], axis=2)

    kb, vb = band(k), band(v)
    s = jnp.einsum('bnqhgd,bnshd->bnhgqs', qb, kb).astype(jnp.float32) * (HEAD_DIM ** -0.5)
    qi = jnp.arange(C)[:, None]
    si = jnp.arange(2 * C)[None, :]
    rel = qi + C - si
    key_pos = jnp.arange(NB)[:, None, None] * C + si[None] - C
    mask = (rel >= 0) & (rel < WINDOW) & (key_pos >= 0)
    s = jnp.where(mask[None, :, None, None], s, -jnp.inf)
    sink = sinks.astype(jnp.float32).reshape(ATTN_KV_HEADS, ATTN_GROUP)[None, None, :, :, None, None]
    m = jnp.maximum(jnp.max(s, axis=-1, keepdims=True), sink)
    p = jnp.exp(s - m)
    p = p / (jnp.sum(p, axis=-1, keepdims=True) + jnp.exp(sink - m))
    o = jnp.einsum('bnhgqs,bnshd->bnqhgd', p.astype(v.dtype), vb)
    return o.reshape(B, T, ATTN_WIDTH)

def rwkv7_time_mix(h, shift_mu, w0, w2, a0, a2, g2, k_k, k_a, r_k, lnx_g, lnx_b):
    B, T = h.shape[0], h.shape[1]
    H, N = RWKV_HEADS, HEAD_DIM
    h_prev = jnp.pad(h, ((0, 0), (1, 0), (0, 0)))[:, :-1]
    z = h + shift_mu * (h_prev - h)
    r, k, v, wd, ad, gd = _split(z, RWKV_SIZES)
    w_log = -jax.nn.softplus(-(w0 + jnp.tanh(wd) @ w2)) - 0.5
    decay = jnp.exp(-jnp.exp(w_log.astype(jnp.float32)))
    a = jax.nn.sigmoid(a0 + ad @ a2)
    g = jax.nn.sigmoid(gd) @ g2
    kk = (k * k_k).reshape(B, T, H, N).astype(jnp.float32)
    kk = kk / jnp.maximum(jnp.linalg.norm(kk, axis=-1, keepdims=True), 1e-12)
    k = k * (1.0 + (a - 1.0) * k_a)

    def heads(t):
        return t.reshape(B, T, H, N).astype(jnp.float32)

    r_h, k_h, v_h, a_h, w_h = heads(r), heads(k), heads(v), heads(a), heads(decay)
    xs = tuple(t.transpose(1, 0, 2, 3) for t in (r_h, w_h, k_h, v_h, -kk, kk * a_h))

    def step(S, inp):
        r_t, w_t, k_t, v_t, a_t, b_t = inp
        Sa = jnp.einsum('bhvk,bhk->bhv', S, a_t)
        S = S * w_t[:, :, None, :] + Sa[..., None] * b_t[:, :, None, :] + v_t[..., None] * k_t[:, :, None, :]
        return S, jnp.einsum('bhvk,bhk->bhv', S, r_t)

    S0 = jnp.zeros((B, H, N, N), jnp.float32)
    _, y = lax.scan(step, S0, xs)
    y = y.transpose(1, 0, 2, 3)
    mu = jnp.mean(y, axis=-1, keepdims=True)
    var = jnp.mean(jnp.square(y - mu), axis=-1, keepdims=True)
    y = ((y - mu) * lax.rsqrt(var + RWKV_LN_EPS)).reshape(B, T, RWKV_WIDTH)
    y = y * lnx_g.astype(jnp.float32) + lnx_b.astype(jnp.float32)
    bonus = jnp.sum(r_h * k_h * r_k.astype(jnp.float32), axis=-1, keepdims=True) * v_h
    y = (y + bonus.reshape(B, T, RWKV_WIDTH)) * g.astype(jnp.float32)
    return y.astype(h.dtype)

def _rotary(x, pos):
    half = HEAD_DIM // 2
    inv_freq = 1.0 / (ROPE_BASE ** (jnp.arange(half, dtype=jnp.float32) * 2.0 / HEAD_DIM))
    ang = pos.astype(jnp.float32)[:, None] * inv_freq[None, :]
    cos, sin = jnp.cos(ang)[:, None, :], jnp.sin(ang)[:, None, :]
    x1, x2 = x[..., :half], x[..., half:]
    return jnp.concatenate([x1 * cos - x2 * sin, x2 * cos + x1 * sin], axis=-1)

def retention(q, k, v, gate):
    B, T = q.shape[0], q.shape[1]
    H, d, C = RET_HEADS, HEAD_DIM, RET_CHUNK
    NC = T // C
    pos = jnp.arange(T)
    qh = _rotary(q.reshape(B, T, H, d).astype(jnp.float32), pos)
    kh = _rotary(k.reshape(B, T, H, d).astype(jnp.float32), pos) * (d ** -0.5)
    vh = v.reshape(B, T, H, d).astype(jnp.float32)
    log_gamma = jnp.log1p(-jnp.power(2.0, -5.0 - jnp.arange(H, dtype=jnp.float32)))
    idx = jnp.arange(C, dtype=jnp.float32)
    diff = idx[:, None] - idx[None, :]
    dmat = jnp.where(diff >= 0, jnp.exp(log_gamma[:, None, None] * jnp.maximum(diff, 0.0)), 0.0)
    xi = jnp.exp(log_gamma[:, None] * (idx[None, :] + 1.0))
    zeta = jnp.exp(log_gamma[:, None] * (C - 1.0 - idx[None, :]))
    chunk_decay = jnp.exp(log_gamma * C)
    qc = qh.reshape(B, NC, C, H, d)
    kc = kh.reshape(B, NC, C, H, d)
    vc = vh.reshape(B, NC, C, H, d)
    s = jnp.einsum('bnihd,bnjhd->bnhij', qc, kc) * dmat
    inner = jnp.einsum('bnhij,bnjhe->bnihe', s, vc)
    kv = jnp.einsum('bnjhd,bnjhe,hj->nbhde', kc, vc, zeta)

    def step(R, kv_n):
        return R * chunk_decay[None, :, None, None] + kv_n, R

    _, r_prev = lax.scan(step, jnp.zeros((B, H, d, d), jnp.float32), kv)
    cross = jnp.einsum('bnihd,nbhde,hi->bnihe', qc, r_prev, xi)
    o = _rms((inner + cross).reshape(B, T, H, d)).reshape(B, T, RET_WIDTH)
    o = o * jax.nn.silu(gate.astype(jnp.float32))
    return o.astype(q.dtype)

def hybrid_layer(x, norm1_g, w_in, attn_q_norm_g, attn_k_norm_g, attn_sinks, w_attn_o,
                 rwkv_shift_mu, rwkv_w0, rwkv_w2, rwkv_a0, rwkv_a2, rwkv_g2, rwkv_k_k, rwkv_k_a,
                 rwkv_r_k, rwkv_lnx_g, rwkv_lnx_b, w_rwkv_o, w_ret_o, w_out,
                 norm2_g, w_ffn_gate, w_ffn_up, w_ffn_down):
    B, T, D = x.shape
    h = _rms(x) * norm1_g
    proj = h @ w_in
    aq, ak, av, rw, rq, rk, rv, rg, gates = _split(proj, IN_SIZES)
    aq = _rms(aq.reshape(B, T, ATTN_Q_HEADS, HEAD_DIM)) * attn_q_norm_g
    ak = _rms(ak.reshape(B, T, ATTN_KV_HEADS, HEAD_DIM)) * attn_k_norm_g
    av = av.reshape(B, T, ATTN_KV_HEADS, HEAD_DIM)
    o_a = sliding_window_attention(aq, ak, av, attn_sinks) @ w_attn_o
    o_b = rwkv7_time_mix(rw, rwkv_shift_mu, rwkv_w0, rwkv_w2, rwkv_a0, rwkv_a2, rwkv_g2,
                         rwkv_k_k, rwkv_k_a, rwkv_r_k, rwkv_lnx_g, rwkv_lnx_b) @ w_rwkv_o
    o_c = retention(rq, rk, rv, rg) @ w_ret_o
    g = jax.nn.sigmoid(gates).reshape(B, T, N_BRANCH, D)
    mixed = g[:, :, 0] * o_a + g[:, :, 1] * o_b + g[:, :, 2] * o_c
    x = x + mixed @ w_out
    h2 = _rms(x) * norm2_g
    x = x + (jax.nn.silu(h2 @ w_ffn_gate) * (h2 @ w_ffn_up)) @ w_ffn_down
    return x

def second_inputs(seed: int = 0) -> dict:
    key = jax.random.key(seed)
    ks = jax.random.split(key, 25)
    L = DEPTH_2

    def nrm(k, shape, scale):
        return jax.random.normal(k, shape, jnp.float32) * scale

    return {
        'x': nrm(ks[0], (BATCH, SEQ, D_MODEL), 1.0),
        'norm1_g': 1.0 + nrm(ks[1], (L, D_MODEL), 0.02),
        'w_in': nrm(ks[2], (L, D_MODEL, IN_WIDTH_2), D_MODEL ** -0.5),
        'attn_q_norm_g': 1.0 + nrm(ks[3], (L, HEAD_DIM), 0.02),
        'attn_k_norm_g': 1.0 + nrm(ks[4], (L, HEAD_DIM), 0.02),
        'attn_sinks': nrm(ks[5], (L, ATTN_Q_HEADS), 0.5),
        'w_attn_o': nrm(ks[6], (L, ATTN_WIDTH, D_MODEL), ATTN_WIDTH ** -0.5),
        'rwkv_shift_mu': jax.random.uniform(ks[7], (L, RWKV_COLS), jnp.float32),
        'rwkv_w0': jax.random.uniform(ks[8], (L, RWKV_WIDTH), jnp.float32, minval=-6.0, maxval=1.0),
        'rwkv_w2': nrm(ks[9], (L, DECAY_LORA, RWKV_WIDTH), 0.1 * DECAY_LORA ** -0.5),
        'rwkv_a0': nrm(ks[10], (L, RWKV_WIDTH), 0.1),
        'rwkv_a2': nrm(ks[11], (L, ICLR_LORA, RWKV_WIDTH), ICLR_LORA ** -0.5),
        'rwkv_g2': nrm(ks[12], (L, GATE_LORA, RWKV_WIDTH), GATE_LORA ** -0.5),
        'rwkv_k_k': 0.85 + nrm(ks[13], (L, RWKV_WIDTH), 0.02),
        'rwkv_k_a': 1.0 + nrm(ks[14], (L, RWKV_WIDTH), 0.02),
        'rwkv_r_k': nrm(ks[15], (L, RWKV_HEADS, HEAD_DIM), 0.1),
        'rwkv_lnx_g': 1.0 + nrm(ks[16], (L, RWKV_WIDTH), 0.02),
        'rwkv_lnx_b': nrm(ks[17], (L, RWKV_WIDTH), 0.02),
        'w_rwkv_o': nrm(ks[18], (L, RWKV_WIDTH, D_MODEL), RWKV_WIDTH ** -0.5),
        'w_ret_o': nrm(ks[19], (L, RET_WIDTH, D_MODEL), RET_WIDTH ** -0.5),
        'w_out': nrm(ks[20], (L, D_MODEL, D_MODEL), D_MODEL ** -0.5),
        'norm2_g': 1.0 + nrm(ks[21], (L, D_MODEL), 0.02),
        'w_ffn_gate': nrm(ks[22], (L, D_MODEL, D_FF_2), D_MODEL ** -0.5),
        'w_ffn_up': nrm(ks[23], (L, D_MODEL, D_FF_2), D_MODEL ** -0.5),
        'w_ffn_down': nrm(ks[24], (L, D_FF_2, D_MODEL), D_FF_2 ** -0.5),
    }

def second_block(x, norm1_g, w_in, attn_q_norm_g, attn_k_norm_g, attn_sinks, w_attn_o,
              rwkv_shift_mu, rwkv_w0, rwkv_w2, rwkv_a0, rwkv_a2, rwkv_g2, rwkv_k_k, rwkv_k_a,
              rwkv_r_k, rwkv_lnx_g, rwkv_lnx_b, w_rwkv_o, w_ret_o, w_out,
              norm2_g, w_ffn_gate, w_ffn_up, w_ffn_down):
    for l in range(DEPTH_2):
        x = hybrid_layer(x, norm1_g[l], w_in[l], attn_q_norm_g[l], attn_k_norm_g[l], attn_sinks[l],
                         w_attn_o[l], rwkv_shift_mu[l], rwkv_w0[l], rwkv_w2[l], rwkv_a0[l], rwkv_a2[l],
                         rwkv_g2[l], rwkv_k_k[l], rwkv_k_a[l], rwkv_r_k[l], rwkv_lnx_g[l], rwkv_lnx_b[l],
                         w_rwkv_o[l], w_ret_o[l], w_out[l], norm2_g[l], w_ffn_gate[l], w_ffn_up[l],
                         w_ffn_down[l])
    return x


def setup_inputs(seed=0):
    out = dict(first_inputs(seed))
    for name, value in second_inputs(seed + 1).items():
        if name != "x":
            out[name + "_2"] = value
    return out


def reference(
    x, c, w_ada, b_ada, w_in, b_gate, hgrn_lb_logits, hgrn_norm_w, w_proj_a, gmlp_ln_w,
    gmlp_ln_b, gmlp_ws, gmlp_bs, w_proj_b, w_out, ln1_w, ln1_b, w_ffn_in, w_ffn_out, ln2_w,
    ln2_b, norm1_g_2, w_in_2, attn_q_norm_g_2, attn_k_norm_g_2, attn_sinks_2, w_attn_o_2,
    rwkv_shift_mu_2, rwkv_w0_2, rwkv_w2_2, rwkv_a0_2, rwkv_a2_2, rwkv_g2_2, rwkv_k_k_2,
    rwkv_k_a_2, rwkv_r_k_2, rwkv_lnx_g_2, rwkv_lnx_b_2, w_rwkv_o_2, w_ret_o_2, w_out_2,
    norm2_g_2, w_ffn_gate_2, w_ffn_up_2, w_ffn_down_2,
):
    x = first_block(
        x, c, w_ada, b_ada, w_in, b_gate, hgrn_lb_logits, hgrn_norm_w, w_proj_a, gmlp_ln_w,
        gmlp_ln_b, gmlp_ws, gmlp_bs, w_proj_b, w_out, ln1_w, ln1_b, w_ffn_in, w_ffn_out, ln2_w,
        ln2_b,
    )
    return second_block(
        x, norm1_g_2, w_in_2, attn_q_norm_g_2, attn_k_norm_g_2, attn_sinks_2, w_attn_o_2,
        rwkv_shift_mu_2, rwkv_w0_2, rwkv_w2_2, rwkv_a0_2, rwkv_a2_2, rwkv_g2_2, rwkv_k_k_2,
        rwkv_k_a_2, rwkv_r_k_2, rwkv_lnx_g_2, rwkv_lnx_b_2, w_rwkv_o_2, w_ret_o_2, w_out_2,
        norm2_g_2, w_ffn_gate_2, w_ffn_up_2, w_ffn_down_2,
    )


_drawn_inputs = setup_inputs


def setup_inputs(seed=0):
    import zlib

    import numpy as np

    out = dict(_drawn_inputs(seed))
    spreads = {}
    factors = {'norm1_g_2': 5.833,
     'attn_q_norm_g_2': 200.0,
     'attn_k_norm_g_2': 200.0,
     'attn_sinks_2': 64.0,
     'rwkv_w2_2': 64.0,
     'rwkv_a0_2': 8.0,
     'rwkv_k_k_2': 200.0,
     'rwkv_k_a_2': 8.0,
     'rwkv_lnx_g_2': 200.0,
     'rwkv_lnx_b_2': 200.0,
     'norm2_g_2': 29.341}
    for name, (base, spread) in spreads.items():
        noise = np.random.default_rng([zlib.crc32(name.encode()), seed]).standard_normal(out[name].shape)
        drawn = base * np.exp(spread * noise) if base else spread * noise
        out[name] = jnp.asarray(drawn.astype(out[name].dtype))
    for name, factor in factors.items():
        out[name] = (out[name] * factor).astype(out[name].dtype)
    return out
```

```python
from contextlib import ExitStack

import numpy as np
import concourse.bass as bass
from concourse import mybir

F32, F32R = mybir.dt.float32, mybir.dt.float32r
ALU, ACT, AX = mybir.AluOpType, mybir.ActivationFunctionType, mybir.AxisListType

P = 128
T = 512
D = 1024
DT = D // P
FF = 2816
FT = FF // P
LAYERS = 2
HEADS = 8
CHUNK = 64
NCH = T // CHUNK
SUB = 16
BLK = 128
NBLK = T // BLK
PAIRS = 4
ALPHA = 2.0 ** 0.25
RWKV_DECAY = float(np.exp(np.float32(-0.5)))
KB = 256

FILLS_1 = 32 + 16 + 4 * 8 + 8 + 44 + 24
FILLS_L = 16 + 32 + 4 + 12 + 4 + 4 + 8 + 44 + 24
LEAD = 4
FILLS = FILLS_1 + LAYERS * FILLS_L + LEAD
CHUNKS_1 = 32 + 16 + 4 * 8 + 8 + 44 + 8
CHUNKS_L = 16 + 32 + 8 + 12 + 8 + 8 + 8 + 44 + 8

def columns(sizes):
    at, out = 0, {}
    for name, n in sizes:
        out[name] = at
        at += n
    return out, at

CONST, N_CONST = columns([("ident", 128), ("ones", 128), ("blk1", 128), ("chunk_start", T), ("upper", 64), ("incl", 64),
                          ("lower0", 64), ("level", 6 * 64), ("band", 256),
                          ("dup", 256), ("cd", 4), ("eps", 4)])
TABLE, N_TABLE = columns([("cos", T), ("sin", T), ("dmat", 8 * 128), ("xi", 4 * 128), ("zeta", 4 * 128), ("rot", 128)])
PAR1, N_PAR1 = columns([("c", 8), ("b_ada", 48), ("lb0", 8), ("lb1", 8), ("hg_w", 1), ("gm_w", 8), ("gm_b", 8),
                        ("b_gate", 16), ("ln1_w", 8), ("ln1_b", 8), ("ln2_w", 8), ("ln2_b", 8)])
PAR2, N_PAR2 = columns([("norm1", 8), ("norm2", 8), ("qg", 1), ("kg", 1), ("sinks", 8), ("mu", 14), ("w0", 4), ("a0", 4),
                        ("k_k", 4), ("k_a", 4), ("r_k", 4), ("ln_g", 4), ("ln_b", 4)])
MASKED = -1.0e30

HG = {"ks": 76, "state": 84, "val_t": 88, "kdec_t": 90, "k": 32, "lf": 34, "cum": 36, "qs": 38, "e1": 40, "qi": 42,
      "kdec": 104.5, "st": 106.5, "val": 34, "o": 38, "sq": 32, "rstd": 36}
RP = {"cs": 0, "cx": 2, "kk": 4, "rn": 6, "e": 8, "ei": 10, "ex": 84, "sq": 86, "rk": 94}
RC = {"a": 0, "b": 2, "k": 4, "v": 6, "ak": 8, "b_t": 10, "k_t": 40, "v_t": 42, "u": 44, "t": 46, "p": 48, "us": 50,
      "state": 92, "al0": 94, "al1": 96, "rbk": 98, "el": 100, "spill": 101}
AT = {"sq": 0, "rs": 2, "kn": 4, "vt": 6, "kd": 8, "sc": 40, "pb": 44, "pt": 48, "kj": 104.5, "qs": 106.5, "vj": 108.5}
RT = {"qr": 0, "kr": 2, "qx": 4, "kz": 6, "vs": 8, "t1": 10, "t2": 12, "rs": 14, "kz_t": 40, "v_t": 42, "st": 44, "state": 48, "sq": 50}
ARENA_KB = 109.5


def build(nc, dram, out, scratch):
    ctx = ExitStack()
    with ctx:
        def sb(name, cols, dt=F32):
            return ctx.enter_context(nc.sbuf_tensor(name, [P, cols], dt))

        sems = {}

        def sem(name):
            if name not in sems:
                sems[name] = ctx.enter_context(nc.semaphore(name))
            return sems[name]

        FILL = 8 * 128
        w_raw = sb("w_raw", 2 * FILL)
        w_hi = sb("w_hi", 4 * FILL, F32R)
        w_lo = sb("w_lo", 4 * FILL, F32R)
        H = sb("H", DT * T)
        XH = sb("XH", DT * T, F32R)
        XL = sb("XL", DT * T, F32R)
        con = sb("con", N_CONST)
        par1 = sb("par1", N_PAR1)
        par2 = sb("par2", LAYERS * N_PAR2)
        mod = sb("mod", 48)
        cond = sb("cond", 8)
        lbs = sb("lbs", 16)
        lbt = sb("lbt", 32)
        small = sb("small", 64)
        arena = sb("arena", int(ARENA_KB * KB))
        arena_at = nc.sbuf_base - int(ARENA_KB * KB) * 4
        HH = nc.alloc_sbuf_tensor_at("HH", [P, FT * T], F32R, offset=arena_at)
        HL = nc.alloc_sbuf_tensor_at("HL", [P, FT * T], F32R, offset=arena_at + 4 * FT * T)
        psum = ctx.enter_context(nc.psum_tensor("psum", [P, 8 * 512], F32))

        def A(kb, n=T, at=0):
            lo = int(kb * KB)
            if isinstance(at, int):
                return arena[:, lo + at:lo + at + n]
            return arena[:, bass.ds(lo + at, n)]

        def tile(t, n, at):
            return t[:, at:at + n] if isinstance(at, int) else t[:, bass.ds(at, n)]

        def C(name, n, at=0):
            return tile(con, n, CONST[name] + at)

        def TB(name, n, at=0):
            return A(92, n, TABLE[name] + at)

        def P1(name, at=0, n=1):
            return tile(par1, n, PAR1[name] + at)

        def P2(l, name, at=0, n=1):
            return tile(par2, n, l * N_PAR2 + PAR2[name] + at)

        def bank(b, n=512, at=0):
            return psum[:, 512 * b + at:512 * b + at + n]

        def region(table):
            return lambda name, n, at=0: A(table[name], n, at)

        hg, rp, rc, at, rt = (region(table) for table in (HG, RP, RC, AT, RT))

        def chunks(ap, c=CHUNK):
            return ap.rearrange("p (a c) -> p a c", c=c)

        def bc(ap, n):
            return ap.unsqueeze(1).broadcast_to([ap.shape[0], n, ap.shape[1]])

        def each(ap, n):
            return ap.unsqueeze(2).broadcast_to([ap.shape[0], ap.shape[1], n])

        w_loaded = [sem(f"w_loaded{s}") for s in range(2)]
        hi_ready = sem("hi_ready")
        lo_ready = sem("lo_ready")
        fill_done = sem("fill_done")
        half_done = sem("half_done")
        chunk_out = [sem(f"chunk_out{b}") for b in range(4)]

        spilled = [sem(f"spilled{j}") for j in range(4)]

        def quarter(c):
            return c // 4 if isinstance(c, int) else c

        def arrived(f, k):
            return 8 * f + 16 * (k // 2) + 16

        block = ctx.enter_context(nc.Block())

        @block.sync
        def _(sp):
            sp.dma_start(con[:], dram["con"]).then_inc(sem("const_in"), 16)
            sp.dma_start(par1[:], dram["par1"]).then_inc(sem("const_in"), 16)
            sp.dma_start(par2[:], dram["par2"]).then_inc(sem("const_in"), 16)
            sp.dma_start(H[:], dram["x"]).then_inc(sem("x_in"), 16)
            for k in range(2):
                sp.dma_start(A(16 * k, 16 * KB), dram["w_ada"][k]).then_inc(sem(f"ada_in{k}"), 16)
            for f in range(2):
                sp.dma_start(w_raw[:, f * FILL:(f + 1) * FILL], dram["fills"][f]).then_inc(w_loaded[f], 16)
            with sp.Fori(0, 5) as i:
                for k in range(2):
                    sp.wait_ge(sem("ada_used"), 2 * i + k + 1)
                    sp.dma_start(A(16 * k, 16 * KB),
                                 dram["w_ada"][bass.ds(2 * i + k + 2, 1)].rearrange("a p n -> (a p) n")).then_inc(sem(f"ada_in{k}"), 16)
            with sp.Fori(0, FILLS // 2 - 1) as i:
                for s in range(2):
                    sp.wait_ge(lo_ready, 2 * i + s + 1)
                    sp.dma_start(w_raw[:, s * FILL:(s + 1) * FILL],
                                 dram["fills"][bass.ds(2 * i + s + 2, 1)].rearrange("a p n -> (a p) n")).then_inc(w_loaded[s], 16)
            for b in range(4):
                sp.wait_ge(chunk_out[b], (CHUNKS_1 + LAYERS * CHUNKS_L) // 4)
            sp.dma_start(out, H[:]).then_inc(sem("stored"), 16)
            sp.wait_ge(sem("stored"), 16)

        @block.gpsimd
        def _(pool):
            def lo_part(f, j):
                pool.wait_ge(hi_ready, f + 1)
                nc.gpsimd.tensor_tensor(w_lo[:, j * FILL:(j + 1) * FILL], w_raw[:, (j % 2) * FILL:(j % 2 + 1) * FILL],
                                        w_hi[:, j * FILL:(j + 1) * FILL].bitcast(F32), ALU.subtract).then_inc(lo_ready, 1)

            def lo_parts(f, n):
                with pool.Fori(0, n // 4) as i:
                    for k in range(4):
                        lo_part(f + 4 * i + k, (3 + k) % 4)

            for f in range(3):
                lo_part(f, f)
            lo_parts(3, FILLS_1)
            mask = C("blk1", 128).rearrange("p (k t) -> p k t", k=2).unsqueeze(1).broadcast_to([P, PAIRS, 2, 64])
            with pool.Fori(0, LAYERS) as l:
                f0 = l * FILLS_L + FILLS_1
                lo_parts(f0 + 3, 16)
                pool.wait_ge(sem("rp_done"), l * PAIRS + PAIRS)
                nc.gpsimd.tensor_tensor(small[:, 62:63], small[:, 61:62], small[:, 61:62], ALU.add)
                with pool.Fori(0, NCH) as c:
                    n = l * NCH + c + 1
                    for name, kb, step in (("b", 76, 1), ("k", 24, 1), ("v", 32, 1), ("a", 60, 2)):
                        src = A(kb, 4 * step * T).rearrange("p (a t) -> p a t", a=PAIRS)[:, :, bass.ds(c * step * CHUNK, CHUNK)]
                        ins = nc.gpsimd.tensor_tensor(rc(name, 512).rearrange("p (a k t) -> p a k t", a=PAIRS, k=2),
                                                      src.unsqueeze(2).broadcast_to([P, PAIRS, 2, CHUNK]), mask, ALU.mult)
                    ins.then_inc(sem("rc_in"), 1)
                    for k in range(4):
                        lo_part(f0 + 19 + 4 * c + k, (3 + k) % 4)
                    pool.wait_ge(sem("rc_w"), n)
                    nc.gpsimd.tensor_tensor(small[:, 62:63], small[:, 61:62], small[:, 61:62], ALU.add)
                lo_parts(f0 + 51, FILLS_L - 48)

        @block.tensor
        def _(pe):
            mm = nc.tensor.matmul

            def blocks(slot, xh, xl, out_ap, cols, tiles, first, last):
                n = len(cols)
                for k in range(n):
                    w = slot * FILL + cols[k] * 128
                    x0 = tiles[k] * T
                    ops = [(w_hi, xh), (w_lo, xh), (w_hi, xl)]
                    for o, (wt, xt) in enumerate(ops):
                        ins = mm(out_ap, wt[:, w:w + 128], xt[:, x0:x0 + T],
                                 start=first and k == 0 and o == 0, stop=last and k == n - 1 and o == 2)
                return ins

            def gemm(f, c, n, xh=XH, xl=XL, ready=None, value=0):
                if isinstance(c, int) and c == 0:
                    for j in range(4):
                        pe.wait_ge(lo_ready, j + 1)
                        blocks(j, xh, xl, bank(j), range(8), range(8), True, True).then_inc(fill_done, 1)
                    f, c, n = 4, 4, n - 4
                with pe.Fori(0, n // 4) as i:
                    for j in range(4):
                        if ready and j == 0:
                            pe.wait_ge(ready, value)
                        pe.wait_ge(lo_ready, f + 4 * i + j + 1)
                        pe.wait_ge(chunk_out[j], quarter(c) + i)
                        blocks(j, xh, xl, bank(j), range(8), range(8), True, True).then_inc(fill_done, 1)

            def gemm512(f, c, tile0):
                for j in range(4):
                    pe.wait_ge(lo_ready, f + j + 1)
                    for h in range(2):
                        b = (2 * j + h) % 4
                        pe.wait_ge(chunk_out[b], quarter(c) + j // 2)
                        blocks(j, HH, HL, bank(b), range(4 * h, 4 * h + 4), range(tile0, tile0 + 4), True, True)\
                            .then_inc(fill_done if h else half_done, 1)

            def gemm2816(f, c, value):
                with pe.Fori(0, 2) as i:
                    for j in range(12):
                        q, part = divmod(j, 3)
                        if j == 0:
                            pe.wait_ge(sem("ffn_lo"), value)
                        pe.wait_ge(lo_ready, f + 12 * i + j + 1)
                        if part == 0:
                            pe.wait_ge(chunk_out[q], quarter(c) + i)
                        n = min(8, FT - 8 * part)
                        blocks(j % 4, HH, HL, bank(q), range(n), range(8 * part, 8 * part + n), part == 0, part == 2)\
                            .then_inc(fill_done, 1)

            def mean_of_squares(n, name, src):
                for t in range(DT):
                    if t % 2 == 0:
                        pe.wait_ge(sem(name + "_sq"), 4 * n + t // 2 + 1)
                    ins = mm(bank(5), C("ones", 128), src(t), start=t == 0, stop=t == DT - 1)
                ins.then_inc(sem(name + "_var"), 1)

            def layer_norm(n, src, sq):
                for t in range(DT):
                    ins = mm(bank(4), C("ones", 128), src(t), start=t == 0, stop=t == DT - 1)
                ins.then_inc(sem("ln_sum"), 1)
                mean_of_squares(n, "ln", sq)

            def all_out(c):
                for b in range(4):
                    pe.wait_ge(chunk_out[b], quarter(c))

            def transposes(b, src, n=4):
                for k in range(n):
                    ins = nc.tensor.transpose(bank(b, 128, 128 * k), src(k), C("ident", 128))
                return ins

            pe.wait_ge(sem("cond"), 1)
            with pe.Fori(0, 6) as i:
                for k in range(2):
                    pe.wait_ge(sem(f"ada_in{k}"), 16 * i + 16)
                    for t in range(4):
                        for kt in range(DT):
                            ins = mm(psum[:, bass.ds(512 * 6 + 8 * i + 4 * k + t, 1)],
                                     A(16 * k, 128, (t * DT + kt) * 128), cond[:, kt:kt + 1], start=kt == 0, stop=kt == DT - 1)
                    ins.then_inc(sem("ada_used"), 1)
            pe.wait_ge(sem("x_in"), 16)
            layer_norm(0, lambda t: H[:, t * T:(t + 1) * T], lambda t: A(16, T, t * T))
            pe.wait_ge(sem("ln_x"), 4)
            gemm(0, 0, 32)
            with pe.Fori(0, HEADS) as h:
                pe.wait_ge(sem("hg_q"), h + 1)
                transposes(4, lambda k: hg("kdec", 128, 128 * k))
                transposes(5, lambda k: hg("val", 128, 128 * k)).then_inc(sem("hg_tr"), 1)
                pe.wait_ge(sem("hg_k"), h + 1)
                for c in range(NCH):
                    for s in range(4):
                        ins = mm(bank(6, SUB, 64 * (c // 2) + SUB * s)[64 * (c % 2):64 * (c % 2) + 64],
                                 hg("ks", 64, (4 * c + s) * 64), hg("qs", SUB, c * CHUNK + s * SUB), start=True, stop=True)
                ins.then_inc(sem("hg_sc"), 1)
                pe.wait_ge(sem("hg_tm"), h + 1)
                for c in range(NCH - 1):
                    p0, t0 = 64 * (c % 2), 128 * (c // 2)
                    ins = mm(bank(4 if c % 2 else 7, 128, t0), hg("kdec_t", 128, t0)[p0:p0 + 64], hg("val_t", 128, t0)[p0:p0 + 64],
                             start=True, stop=True)
                ins.then_inc(sem("hg_u"), 1)
                pe.wait_ge(sem("hg_st"), h + 1)
                pe.wait_ge(sem("hg_s"), h + 1)
                for b in range(NBLK):
                    mm(bank(5, 128, 128 * b), hg("val_t", 128, 128 * b), hg("st", 128, 128 * b), start=True, stop=False)
                    for c in (2 * b, 2 * b + 1):
                        ins = mm(bank(5, 64, 64 * c), hg("state", 128, 128 * c), hg("qi", 64, 64 * c), start=False, stop=c % 2 == 1)
                ins.then_inc(sem("hg_o"), 1)
                pe.wait_ge(sem("hg_sq"), h + 1)
                mm(bank(6), C("ones", 128), hg("sq", T), start=True, stop=True).then_inc(sem("hg_var"), 1)
            gemm(32, 32, 16)
            all_out(48)
            layer_norm(1, lambda t: A(60, T, t * T), lambda t: A(76, T, t * T))
            pe.wait_ge(sem("ln_h"), 4)
            pe.wait_ge(sem("gm_mask"), 1)
            with pe.Fori(0, 8) as g:
                pe.wait_ge(sem("gm_vs"), g + 1)
                transposes(4, lambda k: A(40, 128, 128 * k)).then_inc(sem("gm_tr"), 1)
                pe.wait_ge(sem("gm_vt"), g + 1)
                for b in range(NBLK):
                    ins = mm(bank(5, 128, 128 * b), A(42, 128, 128 * b), A(32, 128, 128 * g), start=True, stop=True)
                ins.then_inc(sem("gm_sv"), 1)
            gemm(48, 48, 8)
            pe.wait_ge(sem("hg_y"), HEADS)
            gemm(56, 56, 8, HH, HL)
            gemm(64, 64, 8)
            pe.wait_ge(sem("gm_lo"), 4)
            gemm(72, 72, 8, HH, HL)
            pe.wait_ge(sem("mix_lo"), 8)
            gemm(80, 80, 8)
            all_out(88)
            layer_norm(2, lambda t: H[:, t * T:(t + 1) * T], lambda t: A(16, T, t * T))
            pe.wait_ge(sem("ln_h"), 8)
            layer_norm(3, lambda t: H[:, t * T:(t + 1) * T], lambda t: A(16, T, t * T))
            pe.wait_ge(sem("ln_x"), 8)
            gemm(88, 88, 44)
            gemm2816(132, 132, FT)
            all_out(140)
            layer_norm(4, lambda t: H[:, t * T:(t + 1) * T], lambda t: A(16, T, t * T))

            with pe.Fori(0, LAYERS) as l:
                f0, c0 = l * FILLS_L + FILLS_1, l * (CHUNKS_L // 4) + CHUNKS_1 // 4
                mean_of_squares(2 * l, "rms", lambda t: A(16, T, t * T))
                gemm(f0, c0, 16, ready=sem("rms_x"), value=8 * l + 4)
                pe.wait_ge(sem("rw_act"), l + 1)
                pe.wait_ge(sem("lora_in"), 16 * l + 16)
                for n in range(4):
                    mm(bank(n), A(88, 128, 128 * n)[0:64], A(16, T, 12 * T)[0:64], start=True, stop=True).then_inc(sem("rw_lora"), 1)
                for n in range(4):
                    mm(bank(4 + n), A(88, 128, 128 * n)[64:128], A(16, T, 12 * T)[64:128], start=True, stop=True).then_inc(sem("rw_lora"), 1)
                for n in range(4):
                    pe.wait_ge(sem("rw_lev"), 12 * l + n + 1)
                    mm(bank(n), A(88, 128, 512 + 128 * n), A(16, T, 13 * T), start=True, stop=True).then_inc(sem("rw_lora"), 1)
                with pe.Fori(0, PAIRS) as p:
                    pe.wait_ge(sem("rp_k2"), 4 * l + p + 1)
                    mm(bank(4), C("blk1", 128), rp("sq", T), start=True, stop=True).then_inc(sem("rp_ss"), 1)
                    pe.wait_ge(sem("rp_rk"), 4 * l + p + 1)
                    mm(bank(5), C("blk1", 128), rp("rk", T), start=True, stop=True).then_inc(sem("rp_bn"), 1)
                with pe.Fori(0, NCH) as c:
                    n = l * NCH + c + 1
                    pairs = range(PAIRS)

                    def half_fill(k):
                        j, h = divmod(k, 2)
                        if h == 0:
                            pe.wait_ge(lo_ready, f0 + 16 + 4 * c + j + 1)
                            pe.wait_ge(chunk_out[j], c0 + 4 + c)
                        ins = blocks(j, XH, XL, bank(j), range(4 * h, 4 * h + 4), range(4 * h, 4 * h + 4), h == 0, h == 1)
                        if h:
                            ins.then_inc(fill_done, 1)

                    def bd(name, p):
                        return rc(name, 128, 128 * p)

                    def product(b, *terms):
                        for p in pairs:
                            for k, (left, right) in enumerate(terms):
                                ins = mm(bank(b, 128, 128 * p), bd(left, p), C("ident", 128) if right is None else bd(right, p),
                                         start=k == 0, stop=k == len(terms) - 1)
                        return ins

                    def r(p):
                        return A(60, 64, 2 * T * p + 64 + c * 128)

                    pe.wait_ge(sem("rc_in"), n)
                    product(5, ("a", "b"))
                    product(6, ("k", "a")).then_inc(sem("rc_s1"), 1)
                    pe.wait_ge(sem("rc_st"), n + l)
                    product(4, ("b", "a"))
                    for p in pairs:
                        mm(bank(7, 64, 128 * p), bd("b", p), r(p), start=True, stop=True)
                        ins = mm(bank(7, 64, 128 * p + 64), bd("k", p), r(p), start=True, stop=True)
                    ins.then_inc(sem("rc_s2"), 1)
                    half_fill(0)
                    pe.wait_ge(sem("rc_out"), n)
                    product(5, ("b", None))
                    product(6, ("k", None))
                    product(7, ("v", None)).then_inc(sem("rc_tr"), 1)
                    pe.wait_ge(sem("rc_trc"), n)
                    for v in range(1, 6):
                        pe.wait_ge(sem("rc_al"), 5 * n - 5 + v)
                        product(5, (f"al{v % 2}", "t")).then_inc(sem("rc_p"), 1)
                        half_fill(v)
                        pe.wait_ge(sem("rc_pc"), 5 * n - 5 + v)
                        if v > 1:
                            pe.wait_ge(sem("rc_uu"), 5 * n - 6 + v)
                        if v < 5:
                            product(6, ("u", "p")).then_inc(sem("rc_d"), 1)
                        product(7, ("p", "u")).then_inc(sem("rc_e"), 1)
                    product(5, ("a", "state"), ("ak", "v_t")).then_inc(sem("rc_w"), 1)
                    half_fill(6)
                    pe.wait_ge(sem("rc_wc"), n)
                    pe.wait_ge(sem("rc_uu"), 5 * n)
                    product(6, ("u", "p")).then_inc(sem("rc_u"), 1)
                    half_fill(7)
                    pe.wait_ge(sem("rc_uc"), n)
                    for p in pairs:
                        y = bank(7, 64, 64 * p)
                        mm(y, bd("state", p), r(p), start=True, stop=False)
                        mm(y, bd("us", p), rc("rbk", 64, 128 * p), start=False, stop=False)
                        ins = mm(y, bd("v_t", p), rc("rbk", 64, 128 * p + 64), start=False, stop=True)
                    ins.then_inc(sem("rc_y"), 1)
                    product(4, ("b_t", "us"), ("k_t", "v_t")).then_inc(sem("rc_n"), 1)
                with pe.Fori(0, PAIRS) as p:
                    n = l * PAIRS + p
                    pe.wait_ge(sem("rc_st"), (l + 1) * (NCH + 1))
                    mm(bank(4), C("blk1", 128), A(84, T, p * T), start=True, stop=True).then_inc(sem("ro_m"), 1)
                    pe.wait_ge(sem("ro_s"), n + 1)
                    mm(bank(5), C("blk1", 128), A(94, T), start=True, stop=True).then_inc(sem("ro_v"), 1)
                pe.wait_ge(sem("ro_l"), l * PAIRS + PAIRS)
                gemm512(f0 + 48, c0 + 12, 0)
                gemm(f0 + 52, c0 + 14, 12)
                pe.wait_ge(sem("ak_sq"), l + 1)
                mm(bank(4), C("blk1", 128), at("sq", T), start=True, stop=True).then_inc(sem("ak_ss"), 1)
                transposes(5, lambda k: A(14, 128, 128 * k)).then_inc(sem("av_tr"), 1)
                pe.wait_ge(sem("ak_n"), l + 1)
                for j in range(2):
                    ins = mm(bank(6 + j), C("dup", 128, 128 * j), at("kn", T), start=True, stop=True)
                ins.then_inc(sem("ak_dup"), 1)
                with pe.Fori(0, PAIRS) as p:
                    n = l * PAIRS + p
                    pe.wait_ge(sem("at_sq"), n + 1)
                    mm(bank(4), C("blk1", 128), at("sq", T), start=True, stop=True).then_inc(sem("at_ss"), 1)
                    pe.wait_ge(sem("at_q"), n + 1)
                    for hh in range(2):
                        r = slice(64 * hh, 64 * hh + 64)
                        for b in range(NBLK):
                            k0, k1 = max(0, BLK * (b - 1)), BLK * (b + 1)
                            ins = mm(bank(4 + 2 * hh, k1 - k0, 256 * b + 256 - (k1 - k0)), at("qs", 128, 128 * b)[r],
                                     at("kj", k1 - k0, k0)[r], start=True, stop=True)
                        ins.then_inc(sem("at_sc"), 1)
                    for hh in range(2):
                        pe.wait_ge(sem("at_pn"), 2 * n + hh + 1)
                        for s in range(1, 8):
                            ins = nc.tensor.transpose(bank(0, 128, 128 * s), at("pb", 128, 128 * s), C("ident", 128))
                        ins.then_inc(sem("at_pt"), 1)
                        pe.wait_ge(sem("at_ptc"), 2 * n + hh + 1)
                        for b in range(NBLK):
                            o = psum[64 * hh:64 * hh + 64, 1024 + 128 * b:1024 + 128 * b + 128]
                            if b:
                                mm(o, at("vj", 64, 64 * (b - 1)), at("pt", 128, 256 * b), start=True, stop=False)
                            ins = mm(o, at("vj", 64, 64 * b), at("pt", 128, 256 * b + 128), start=b == 0, stop=True)
                        ins.then_inc(sem("at_o"), 1)
                with pe.Fori(0, PAIRS) as p:
                    n = l * PAIRS + p
                    pe.wait_ge(sem("table_in"), 16 * l + 16)
                    pe.wait_ge(sem("rq_in"), 16 * l + 16)
                    pe.wait_ge(sem("rt_in"), n + 1)
                    mm(bank(4), TB("rot", 128), A(60, T, p * T), start=True, stop=True)
                    mm(bank(5), TB("rot", 128), A(68, T, p * T), start=True, stop=True).then_inc(sem("rt_rot"), 1)
                    pe.wait_ge(sem("rt_qk"), n + 1)
                    transposes(6, lambda k: rt("kz", 128, 128 * k))
                    transposes(7, lambda k: rt("vs", 128, 128 * k)).then_inc(sem("rt_tr"), 1)
                    for hh in range(2):
                        r = slice(64 * hh, 64 * hh + 64)
                        for b in range(NBLK):
                            ins = mm(bank(4 + hh, 128, 128 * b), rt("kr", 128, 128 * b)[r], rt("qr", 128, 128 * b)[r], start=True, stop=True)
                    ins.then_inc(sem("rt_sc"), 1)
                    pe.wait_ge(sem("rt_tm"), n + 1)
                    for b in range(NBLK - 1):
                        ins = mm(bank(7, 128, 128 * b), rt("kz_t", 128, 128 * b), rt("v_t", 128, 128 * b), start=True, stop=True)
                    ins.then_inc(sem("rt_kv"), 1)
                    pe.wait_ge(sem("rt_r"), n + 1)
                    for b in range(NBLK):
                        mm(bank(6, 128, 128 * b), rt("state", 128, 128 * b), rt("qx", 128, 128 * b), start=True, stop=False)
                        for hh in range(2):
                            ins = mm(psum[64 * hh:64 * hh + 64, 512 * 6 + 128 * b:512 * 6 + 128 * b + 128],
                                     rt("v_t", 64, 128 * b + 64 * hh), rt("st", 128, 512 * hh + 128 * b), start=False, stop=True)
                    ins.then_inc(sem("rt_o"), 1)
                    pe.wait_ge(sem("rt_sq"), n + 1)
                    mm(bank(4), C("blk1", 128), rt("sq", T), start=True, stop=True).then_inc(sem("rt_var"), 1)
                pe.wait_ge(sem("at_y"), 2 * l + 2)
                gemm512(f0 + 64, c0 + 17, 0)
                gemm512(f0 + 68, c0 + 19, 4)
                gemm(f0 + 72, c0 + 21, 8, ready=sem("mix_lo"), value=8 * l + 16)
                mean_of_squares(2 * l + 1, "rms", lambda t: A(16, T, t * T))
                gemm(f0 + 80, c0 + 23, 44, ready=sem("rms_x"), value=8 * l + 8)
                gemm2816(f0 + 124, c0 + 34, l * FT + 2 * FT)

        @block.scalar
        def _(act):
            fn = nc.scalar.activation

            def hi(f, j):
                s = (j + LEAD) % 4
                act.wait_ge(w_loaded[s % 2], arrived(f, j + LEAD))
                act.wait_ge(fill_done, f + j + 1)
                fn(w_hi[:, s * FILL:(s + 1) * FILL], w_raw[:, (s % 2) * FILL:(s % 2 + 1) * FILL], ACT.Copy).then_inc(hi_ready, 1)

            def gemm(f, c, n, take=None):
                with act.Fori(0, n // 4) as i:
                    for j in range(4):
                        if take:
                            act.wait_ge(fill_done, f + 4 * i + j + 1)
                            take(i, j, chunk_out[j])
                        hi(f + 4 * i, j)

            def gemm512(f):
                for j in range(4):
                    hi(f, j)

            def gemm2816(f):
                with act.Fori(0, 2) as i:
                    for j in range(12):
                        hi(f + 12 * i, j)

            def rstd(name, b, scale, eps, out_ap, done):
                fn(out_ap, bank(b), ACT.Ln, scale=scale, bias=C("eps", 1, eps))
                nc.scalar.drain()
                fn(out_ap, out_ap, ACT.Exp, scale=-0.5).then_inc(sem(done), 1)

            def norm_tail(n, name, eps):
                act.wait_ge(sem(name + "_var"), n + 1)
                rstd(name, 5, 1.0 / D, eps, A(34), name + "_rstd")

            def norm_hi(n, name):
                for q in range(4):
                    act.wait_ge(sem(name + "_u"), 4 * n + q + 1)
                    fn(XH[:, 2 * q * T:(2 * q + 2) * T], A(0, 2 * T, 2 * q * T), ACT.Copy).then_inc(sem(name + "_hi"), 1)

            def layer_norm(n, xc, sq):
                for q in range(4):
                    act.wait_ge(sem("ln_xc"), 4 * n + q + 1)
                    fn(sq(2 * q), xc(2 * q), ACT.Square).then_inc(sem("ln_sq"), 1)
                norm_tail(n, "ln", 0)

            def ffn(f, c, n0):
                with act.Fori(0, FT // 2) as i:
                    for j in range(4):
                        if j % 2 == 0:
                            act.wait_ge(fill_done, f + 4 * i + j + 1)
                            fn(A(88, T, j // 2 * T), bank(j), ACT.Silu).then_inc(chunk_out[j], 1)
                        else:
                            act.wait_ge(chunk_out[j], quarter(c) + i + 1)
                            fn(HH[:, bass.ds((2 * i + j // 2) * T, T)], A(105, T, j // 2 * T), ACT.Copy).then_inc(sem("ffn_hi"), 1)
                        hi(f + 4 * i, j)

            def all_out(c):
                for b in range(4):
                    act.wait_ge(chunk_out[b], quarter(c))

            def first_hi(f):
                act.wait_ge(w_loaded[f % 2], 16 * (f // 2) + 16)
                fn(w_hi[:, f * FILL:(f + 1) * FILL], w_raw[:, (f % 2) * FILL:(f % 2 + 1) * FILL], ACT.Copy).then_inc(hi_ready, 1)

            act.wait_ge(sem("const_in"), 48)
            fn(cond[:], P1("c", 0, 8), ACT.Silu).then_inc(sem("cond"), 1)
            act.wait_ge(sem("lb_max"), 1)
            fn(lbt[:, 8:24], lbt[:, 8:24], ACT.Exp).then_inc(sem("lb_exp"), 1)
            two = lambda kb: (lambda t: A(kb, 2 * T, t * T))
            first_hi(0)
            first_hi(1)
            layer_norm(0, two(0), two(16))
            first_hi(2)
            first_hi(3)
            norm_hi(0, "ln")
            def take_hgrn(i, j, done):
                kb, func = ((0, ACT.Silu), (16, ACT.Silu), (44, ACT.Sigmoid), (60, ACT.Copy))[j]
                fn(A(kb, T, i * T), bank(j), func).then_inc(done, 1)
            gemm(0, 0, 32, take_hgrn)
            with act.Fori(0, HEADS) as h:
                act.wait_ge(sem("hg_f"), h + 1)
                fn(hg("lf", T), hg("lf", T), ACT.Ln).then_inc(sem("hg_lf"), 1)
                act.wait_ge(sem("hg_ex"), h + 1)
                fn(hg("qs", T), hg("qs", T), ACT.Exp)
                fn(hg("kdec", T), hg("kdec", T), ACT.Exp)
                fn(hg("e1", T), hg("cum", T), ACT.Exp).then_inc(sem("hg_exp"), 1)
                act.wait_ge(sem("hg_ks"), h + 1)
                ks = hg("ks", 2048).rearrange("p (c i s) -> p c i s", c=NCH, i=4)
                for s in range(4):
                    n = SUB * (s + 1)
                    ins = fn(ks[:, :, s, :n], ks[:, :, s, :n], ACT.Exp)
                ins.then_inc(sem("hg_kse"), 1)
                act.wait_ge(sem("hg_tr"), h + 1)
                fn(hg("kdec_t", T), bank(4), ACT.Copy)
                fn(hg("val_t", T), bank(5), ACT.Copy).then_inc(sem("hg_tm"), 1)
                act.wait_ge(sem("hg_o"), h + 1)
                fn(hg("sq", T), bank(5), ACT.Square).then_inc(sem("hg_sq"), 1)
                act.wait_ge(sem("hg_var"), h + 1)
                rstd("hg", 6, 1.0 / 128, 1, hg("rstd", T), "hg_rstd")
                act.wait_ge(sem("hg_out"), h + 1)
                fn(HH[:, bass.ds(h * T, T)], hg("o", T), ACT.Copy).then_inc(sem("hg_hi"), 1)
            act.wait_ge(sem("hg_y"), HEADS)
            act.dma_start(A(32, 8 * 128), dram["gm_ws"]).then_inc(sem("gm_in"), 16)
            act.dma_start(A(36, 8 * 128), dram["gm_bs"].broadcast_to([P, 8 * 128])).then_inc(sem("gm_in"), 16)
            def take_gmlp(i, j, done):
                fn(A(16 if j < 2 else 60, T, (2 * i + j % 2) * T), bank(j), ACT.Gelu).then_inc(done, 1)
            gemm(32, 32, 16, take_gmlp)
            for q in range(4):
                act.wait_ge(sem("ln_xc"), 4 + q + 1)
                fn(A(76, 2 * T, 2 * q * T), A(60, 2 * T, 2 * q * T), ACT.Square).then_inc(sem("ln_sq"), 1)
            act.wait_ge(sem("ln_var"), 2)
            rstd("ln", 5, 1.0 / D, 0, A(105), "ln_rstd")
            with act.Fori(0, 8) as g:
                act.wait_ge(sem("gm_tr"), g + 1)
                fn(A(42), bank(4), ACT.Copy).then_inc(sem("gm_vt"), 1)
            act.wait_ge(sem("gm_u"), 8)
            gemm(48, 48, 8, lambda i, j, done: fn(A(60, T, (4 * i + j) * T), bank(j), ACT.Sigmoid, bias=P1("b_gate", 4 * i + j)).then_inc(done, 1))
            gemm(56, 56, 8)
            gemm(64, 64, 8, lambda i, j, done: fn(A(76, T, (4 * i + j) * T), bank(j), ACT.Sigmoid, bias=P1("b_gate", 4 * i + j + 8)).then_inc(done, 1))
            all_out(64)
            for q in range(4):
                fn(HH[:, 2 * q * T:(2 * q + 2) * T], A(16, 2 * T, 2 * q * T), ACT.Copy).then_inc(sem("gm_hi"), 1)
            def sum_hi(n0):
                def take(i, j):
                    act.wait_ge(sem("mix_sum"), n0 + 4 * i + j + 1)
                    fn(XH[:, bass.ds((4 * i + j) * T, T)], A(60, T, (4 * i + j) * T), ACT.Copy).then_inc(sem("mix_hi"), 1)
                return take
            take = sum_hi(0)
            with act.Fori(0, 2) as i:
                for j in range(4):
                    hi(72 + 4 * i, j)
                    take(i, j)
            gemm(80, 80, 8)
            layer_norm(2, two(0), two(16))
            layer_norm(3, two(0), two(16))
            norm_hi(1, "ln")
            ffn(88, 88, 0)
            gemm2816(132)
            layer_norm(4, two(0), two(16))
            act.wait_ge(sem("ln_h"), 12)

            with act.Fori(0, LAYERS) as l:
                f0, c0 = l * FILLS_L + FILLS_1, l * (CHUNKS_L // 4) + CHUNKS_1 // 4

                def rms_norm(k, c):
                    all_out(c)
                    for q in range(4):
                        fn(A(16, 2 * T, 2 * q * T), H[:, 2 * q * T:(2 * q + 2) * T], ACT.Square).then_inc(sem("rms_sq"), 1)
                    norm_tail(2 * l + k, "rms", 1)
                    norm_hi(2 * l + k, "rms")

                def take_at(kb):
                    return lambda i, j, done: fn(A(kb, T, (4 * i + j) * T), bank(j), ACT.Copy).then_inc(done, 1)

                rms_norm(0, c0)
                act.dma_start(A(88, 1024), dram["lora"][bass.ds(l, 1)].rearrange("a p n -> (a p) n")).then_inc(sem("lora_in"), 16)
                gemm(f0, c0, 16, take_at(12))
                act.wait_ge(sem("rw_mix"), 14 * l + 14)
                fn(A(16, T, 12 * T)[0:64], A(16, T, 12 * T)[0:64], ACT.Tanh)
                fn(A(16, T, 13 * T), A(16, T, 13 * T), ACT.Sigmoid).then_inc(sem("rw_act"), 1)
                for n in range(12):
                    act.wait_ge(sem("rw_lora"), 12 * l + n + 1)
                    if n < 4:
                        ins = fn(A(76, T, n * T), bank(n), ACT.Sigmoid, bias=P2(l, "w0", n))
                    elif n < 8:
                        ins = fn(A(44, T, (n - 4) * T), bank(n), ACT.Sigmoid, bias=P2(l, "a0", n - 4))
                    else:
                        ins = fn(A(52, T, (n - 8) * T), bank(n - 8), ACT.Copy)
                    ins.then_inc(sem("rw_lev"), 1)
                with act.Fori(0, PAIRS) as p:
                    n = l * PAIRS + p + 1
                    act.wait_ge(sem("rp_cs"), n)
                    fn(rp("e", T), rp("cs", T), ACT.Exp, scale=-RWKV_DECAY)
                    fn(rp("ei", T), rp("cs", T), ACT.Exp, scale=RWKV_DECAY)
                    fn(rp("ex", T), rp("cx", T), ACT.Exp, scale=-RWKV_DECAY).then_inc(sem("rp_e"), 1)
                    act.wait_ge(sem("rp_kk"), n)
                    fn(rp("sq", T), rp("kk", T), ACT.Square).then_inc(sem("rp_k2"), 1)
                    act.wait_ge(sem("rp_mx"), n)
                    fn(rp("rn", T), rp("rn", T), ACT.Sqrt).then_inc(sem("rp_rn"), 1)
                with act.Fori(0, NCH) as c:
                    n = l * NCH + c + 1

                    def take(j):
                        act.wait_ge(fill_done, f0 + 16 + 4 * c + j + 1)
                        fn(rc("spill", T, T * j), bank(j), ACT.Copy if j == 3 else ACT.Sigmoid).then_inc(chunk_out[j], 1)
                        hi(f0 + 16 + 4 * c, j)
                        act.wait_ge(chunk_out[j], c0 + 4 + c + 1)
                        act.dma_start(scratch[bass.ds(l * 32 + 8 * j + c, 1)].rearrange("a p n -> (a p) n"),
                                      rc("spill", T, T * j)).then_inc(spilled[j], 16)

                    act.wait_ge(sem("rc_tr"), n)
                    fn(rc("b_t", T), bank(5), ACT.Copy)
                    fn(rc("k_t", T), bank(6), ACT.Copy)
                    fn(rc("v_t", T), bank(7), ACT.Copy).then_inc(sem("rc_trc"), 1)
                    for v in range(1, 6):
                        act.wait_ge(sem("rc_p"), 5 * n - 5 + v)
                        fn(rc("p", T), bank(5), ACT.Copy).then_inc(sem("rc_pc"), 1)
                        if v in (2, 4):
                            take(v // 2 - 1)
                    take(2)
                    act.wait_ge(sem("rc_w"), n)
                    fn(rc("p", T), bank(5), ACT.Copy).then_inc(sem("rc_wc"), 1)
                    act.wait_ge(sem("rc_u"), n)
                    fn(rc("us", T), bank(6), ACT.Copy).then_inc(sem("rc_uc"), 1)
                    take(3)
                    act.wait_ge(sem("rc_y"), n)
                    fn(A(84, 4 * T).rearrange("p (a t) -> p a t", a=PAIRS)[:, :, bass.ds(c * CHUNK, CHUNK)],
                       chunks(bank(7, 256)), ACT.Copy).then_inc(sem("rc_yc"), 1)
                    for j in range(4):
                        act.wait_ge(spilled[j], 16 * n)

                def from_scratch(dst, tile, tiles, done):
                    act.dma_start(dst.rearrange("p (a n) -> p a n", n=T),
                                  scratch[bass.ds(l * 32 + tile, tiles)].rearrange("a p n -> p a n")).then_inc(sem(done), 16)

                act.wait_ge(sem("rc_y"), l * NCH + NCH)
                from_scratch(A(60, 8 * T), 8, 8, "gate_b_in")
                with act.Fori(0, PAIRS) as p:
                    n = l * PAIRS + p + 1
                    act.wait_ge(sem("ro_c"), n)
                    fn(A(94), A(92), ACT.Square).then_inc(sem("ro_s"), 1)
                    act.wait_ge(sem("ro_v"), n)
                    rstd("ro", 5, 1.0 / 64, 2, A(96), "ro_r")
                    act.wait_ge(sem("ro_y"), n)
                    fn(HH[:, bass.ds(p * T, T)], A(92), ACT.Copy).then_inc(sem("ro_h"), 1)
                act.wait_ge(sem("ro_l"), l * PAIRS + PAIRS)
                act.dma_start(A(92, N_TABLE), dram["table"]).then_inc(sem("table_in"), 16)
                from_scratch(A(52, 4 * T), 24, 4, "aq_in")
                gemm512(f0 + 48)
                all_out(c0 + 14)
                from_scratch(A(60, 4 * T), 28, 4, "rq_in")
                gemm(f0 + 52, c0 + 14, 12, take_at(68))
                act.wait_ge(sem("aq_in"), 16 * l + 16)
                fn(at("sq", T), A(12), ACT.Square).then_inc(sem("ak_sq"), 1)
                act.wait_ge(sem("ak_ss"), l + 1)
                rstd("ak", 4, 1.0 / 64, 1, at("rs", T), "ak_rs")
                act.wait_ge(sem("av_tr"), l + 1)
                fn(at("vt", T), bank(5), ACT.Copy)
                act.wait_ge(sem("ak_dup"), l + 1)
                fn(at("kd", 2 * T), bank(6, 2 * T), ACT.Copy).then_inc(sem("ak_kv"), 1)
                with act.Fori(0, PAIRS) as p:
                    n = l * PAIRS + p
                    act.wait_ge(sem("at_in"), n + 1)
                    fn(at("sq", T), A(52, T, p * T), ACT.Square).then_inc(sem("at_sq"), 1)
                    act.wait_ge(sem("at_ss"), n + 1)
                    rstd("at", 4, 1.0 / 64, 1, at("rs", T), "at_rs")
                    for hh in range(2):
                        act.wait_ge(sem("at_m"), 2 * n + hh + 1)
                        for b in range(NBLK):
                            fn(at("pb", 256, 256 * b), at("sc", 256, 256 * b), ACT.Exp, bias=small[:, b:b + 1], accum_out=small[:, 8 + b:9 + b])
                        fn(small[:, 16:20], small[:, 0:4], ACT.Exp, bias=P2(l, "sinks", 2 * p + hh)).then_inc(sem("at_p"), 1)
                        act.wait_ge(sem("at_pt"), 2 * n + hh + 1)
                        fn(at("pt", 896, 128), bank(0, 896, 128), ACT.Copy).then_inc(sem("at_ptc"), 1)
                    act.wait_ge(sem("at_o"), 2 * n + 2)
                    fn(small[:, 60:61], small[:, 60:61], ACT.Copy)
                    fn(A(52, T, p * T), bank(2), ACT.Copy).then_inc(sem("at_ao"), 1)
                with act.Fori(0, PAIRS) as p:
                    n = l * PAIRS + p
                    act.wait_ge(sem("rt_tr"), n + 1)
                    fn(rt("kz_t", T), bank(6), ACT.Copy)
                    fn(rt("v_t", T), bank(7), ACT.Copy).then_inc(sem("rt_tm"), 1)
                    act.wait_ge(sem("rt_o"), n + 1)
                    fn(rt("sq", T), bank(6), ACT.Square).then_inc(sem("rt_sq"), 1)
                    fn(A(84, T, p * T), A(84, T, p * T), ACT.Silu)
                    act.wait_ge(sem("rt_var"), n + 1)
                    rstd("rt", 4, 1.0 / 64, 1, rt("rs", T), "rt_rs")
                fn(HH[:, 0:4 * T], A(52, 4 * T), ACT.Copy).then_inc(sem("at_yh"), 1)
                act.wait_ge(sem("rt_done"), l * PAIRS + PAIRS)
                fn(HH[:, 4 * T:8 * T], A(60, 4 * T), ACT.Copy).then_inc(sem("at_yh"), 1)
                from_scratch(A(68, 8 * T), 0, 8, "gate_a_in")
                from_scratch(A(84, 8 * T), 16, 8, "gate_c_in")
                gemm512(f0 + 64)
                gemm512(f0 + 68)
                for j in range(8):
                    act.wait_ge(sem("mix_sum"), 16 * l + 16 + j + 1)
                    fn(XH[:, j * T:(j + 1) * T], A(16, T, j * T), ACT.Copy).then_inc(sem("mix_hi"), 1)
                gemm(f0 + 72, c0 + 21, 8)
                rms_norm(1, c0 + 23)
                ffn(f0 + 80, c0 + 23, l * FT + FT)
                gemm2816(f0 + 124)

        @block.vector
        def _(dve):
            tt, ts, stt, cp = nc.vector.tensor_tensor, nc.vector.tensor_scalar, nc.vector.scalar_tensor_tensor, nc.vector.tensor_copy

            def drain():
                nc.vector.drain()

            def lo(dst, src, hi_part):
                return tt(dst, src, hi_part.bitcast(F32), ALU.subtract)

            def all_out(c):
                for b in range(4):
                    dve.wait_ge(chunk_out[b], quarter(c))

            def norm_lo(n, name):
                for q in range(4):
                    dve.wait_ge(sem(name + "_hi"), 4 * n + q + 1)
                    s = slice(2 * q * T, (2 * q + 2) * T)
                    lo(XL[:, s], A(0, 2 * T, 2 * q * T), XH[:, s]).then_inc(sem(name + "_x"), 1)

            def layer_norm(n, src, xc, rs, scale, bias, dst, done):
                dve.wait_ge(sem("ln_sum"), n + 1)
                for q in range(4):
                    stt(chunks(xc(2 * q, 2), T), bc(bank(4), 2), -1.0 / D, chunks(src(2 * q, 2), T), ALU.mult, ALU.add).then_inc(sem("ln_xc"), 1)
                dve.wait_ge(sem("ln_rstd"), n + 1)
                for q in range(4):
                    tt(chunks(xc(2 * q, 2), T), chunks(xc(2 * q, 2), T), bc(rs, 2), ALU.mult)
                drain()
                for t in range(DT):
                    ins = ts(dst(t, 1), xc(t, 1), scale(t), bias(t), ALU.mult, ALU.add)
                    if t % 2:
                        ins.then_inc(sem(done), 1)

            def ffn(f, c, n0):
                with dve.Fori(0, FT // 2) as i:
                    for j in (1, 3):
                        k = j // 2
                        dve.wait_ge(chunk_out[j - 1], quarter(c) + i + 1)
                        dve.wait_ge(fill_done, f + 4 * i + j + 1)
                        tt(A(105, T, k * T), bank(j), A(88, T, k * T), ALU.mult).then_inc(chunk_out[j], 1)
                        dve.wait_ge(sem("ffn_hi"), n0 + 2 * i + k + 1)
                        at_ = bass.ds((2 * i + k) * T, T)
                        lo(HL[:, at_], A(105, T, k * T), HH[:, at_]).then_inc(sem("ffn_lo"), 1)

            def residual(f, c, n, step, scale=None):
                with dve.Fori(0, 2) as i:
                    for j in range(4):
                        dve.wait_ge(fill_done, f + step * (4 * i + j + 1))
                        h = H[:, bass.ds((4 * i + j) * T, T)]
                        if scale:
                            stt(h, bank(j), scale(4 * i + j), h, ALU.mult, ALU.add).then_inc(chunk_out[j], 1)
                        else:
                            tt(h, bank(j), h, ALU.add).then_inc(chunk_out[j], 1)

            def Ht(t, n):
                return H[:, t * T:(t + n) * T]

            def at_kb(kb):
                return lambda t, n: A(kb, n * T, t * T)

            nc.vector.memset(small[:], 0.0)
            dve.wait_ge(sem("const_in"), 48)
            tt(lbt[:, 0:8], P1("lb0", 0, 8), P1("lb1", 0, 8), ALU.max)
            drain()
            tt(lbt[:, 8:16], P1("lb0", 0, 8), lbt[:, 0:8], ALU.subtract)
            tt(lbt[:, 16:24], P1("lb1", 0, 8), lbt[:, 0:8], ALU.subtract).then_inc(sem("lb_max"), 1)
            dve.wait_ge(sem("lb_exp"), 1)
            tt(lbt[:, 0:8], lbt[:, 8:16], lbt[:, 16:24], ALU.add)
            drain()
            nc.vector.reciprocal(lbt[:, 24:32], lbt[:, 0:8])
            drain()
            tt(lbs[:, 0:8], lbt[:, 8:16], lbt[:, 24:32], ALU.mult)
            drain()
            ts(lbs[:, 8:16], lbs[:, 0:8], -1.0, 1.0, ALU.mult, ALU.add)
            dve.wait_ge(sem("ada_used"), 12)
            tt(mod[:], bank(6, 48), P1("b_ada", 0, 48), ALU.add)
            drain()
            for k in (8, 32):
                ts(mod[:, k:k + 8], mod[:, k:k + 8], 1.0, None, ALU.add)
            drain()
            layer_norm(0, Ht, at_kb(0), A(34), lambda t: mod[:, 8 + t:9 + t], lambda t: mod[:, t:t + 1], at_kb(0), "ln_u")
            norm_lo(0, "ln")
            ts(H[:], H[:], ALPHA, None, ALU.mult)
            nc.vector.memset(hg("ks", 2048), 0.0)
            nc.vector.memset(hg("state", 128), 0.0)
            nc.vector.memset(hg("st", 512), 0.0)
            all_out(32)
            with dve.Fori(0, HEADS) as h:
                drain()
                ts(hg("lf", T), A(44, T, h * T), lbs[:, bass.ds(h + 8, 1)], lbs[:, bass.ds(h, 1)], ALU.mult, ALU.add)
                drain()
                ts(hg("k", T), hg("lf", T), -1.0, 1.0, ALU.mult, ALU.add).then_inc(sem("hg_f"), 1)
                dve.wait_ge(sem("hg_lf"), h + 1)
                nc.vector.tensor_tensor_scan(hg("cum", T), C("chunk_start", T), hg("lf", T), 0.0, ALU.mult, ALU.add)
                drain()
                tt(hg("lf", T), hg("cum", T), hg("lf", T), ALU.subtract)
                drain()
                ref = chunks(hg("lf", T), SUB)[:, :, 0]
                tt(chunks(hg("qs", T), SUB), chunks(hg("cum", T), SUB), each(ref, SUB), ALU.subtract)
                last = chunks(hg("cum", T))[:, :, CHUNK - 1]
                tt(chunks(hg("kdec", T)), each(last, CHUNK), chunks(hg("cum", T)), ALU.subtract).then_inc(sem("hg_ex"), 1)
                ks = hg("ks", 2048).rearrange("p (c i s) -> p c i s", c=NCH, i=4)
                for s in range(4):
                    n = SUB * (s + 1)
                    ins = tt(ks[:, :, s, :n], each(chunks(hg("lf", T))[:, :, SUB * s], n), chunks(hg("cum", T))[:, :, :n], ALU.subtract)
                ins.then_inc(sem("hg_ks"), 1)
                dve.wait_ge(sem("hg_exp"), h + 1)
                q = A(0, T, h * T)
                tt(hg("qs", T), hg("qs", T), q, ALU.mult)
                tt(hg("qi", T), hg("e1", T), q, ALU.mult)
                tt(hg("kdec", T), hg("kdec", T), hg("k", T), ALU.mult)
                drain()
                cp(hg("val", T), A(60, T, h * T)).then_inc(sem("hg_q"), 1)
                dve.wait_ge(sem("hg_kse"), h + 1)
                kb = chunks(hg("k", T)).unsqueeze(2).broadcast_to([P, NCH, 4, CHUNK])
                tt(ks, ks, kb, ALU.mult).then_inc(sem("hg_k"), 1)
                dve.wait_ge(sem("hg_sc"), h + 1)
                for p0 in (0, 64):
                    r = slice(p0, p0 + 64)
                    ins = tt(chunks(hg("st", T), 128)[r, :, p0:p0 + 64], chunks(bank(6, 256))[r], bc(C("incl", 64)[r], 4), ALU.mult)
                ins.then_inc(sem("hg_st"), 1)
                dve.wait_ge(sem("hg_u"), h + 1)
                for c in range(NCH - 1):
                    e = hg("e1", T)[:, c * CHUNK + CHUNK - 1:c * CHUNK + CHUNK]
                    ins = stt(hg("state", 128, 128 * c + 128), hg("state", 128, 128 * c), e, bank(4 if c % 2 else 7, 128, 128 * (c // 2)), ALU.mult, ALU.add)
                    if c < NCH - 2:
                        drain()
                ins.then_inc(sem("hg_s"), 1)
                dve.wait_ge(sem("hg_rstd"), h + 1)
                tt(hg("o", T), bank(5), hg("rstd", T), ALU.mult)
                drain()
                stt(hg("o", T), hg("o", T), P1("hg_w"), A(16, T, h * T), ALU.mult, ALU.mult).then_inc(sem("hg_out"), 1)
                dve.wait_ge(sem("hg_hi"), h + 1)
                lo(HL[:, bass.ds(h * T, T)], hg("o", T), HH[:, bass.ds(h * T, T)]).then_inc(sem("hg_y"), 1)
            dve.wait_ge(sem("gm_in"), 32)
            nc.vector.memset(chunks(A(32, 1024), 128)[64:128, :, 0:64], 0.0).then_inc(sem("gm_mask"), 1)
            all_out(48)
            layer_norm(1, at_kb(60), at_kb(60), A(105), lambda t: P1("gm_w", t), lambda t: P1("gm_b", t), at_kb(60), "ln_h")
            with dve.Fori(0, 8) as g:
                drain()
                cp(A(40), A(60, T, g * T)).then_inc(sem("gm_vs"), 1)
                dve.wait_ge(sem("gm_sv"), g + 1)
                tt(chunks(A(40), 128), chunks(bank(5), 128), bc(A(36, 128, g * 128), 4), ALU.add)
                drain()
                tt(A(16, T, g * T), A(16, T, g * T), A(40), ALU.mult).then_inc(sem("gm_u"), 1)
            all_out(56)
            with dve.Fori(0, 2) as i:
                for j in range(4):
                    dve.wait_ge(fill_done, 56 + 4 * i + j + 1)
                    m = A(60, T, (4 * i + j) * T)
                    tt(m, bank(j), m, ALU.mult).then_inc(chunk_out[j], 1)
            for q in range(4):
                dve.wait_ge(sem("gm_hi"), q + 1)
                s = slice(2 * q * T, (2 * q + 2) * T)
                lo(HL[:, s], A(16, 2 * T, 2 * q * T), HH[:, s]).then_inc(sem("gm_lo"), 1)
            all_out(72)
            with dve.Fori(0, 2) as i:
                for j in range(4):
                    dve.wait_ge(fill_done, 72 + 4 * i + j + 1)
                    k = (4 * i + j) * T
                    tt(A(76, T, k), bank(j), A(76, T, k), ALU.mult).then_inc(chunk_out[j], 1)
                    drain()
                    tt(A(60, T, k), A(60, T, k), A(76, T, k), ALU.add).then_inc(sem("mix_sum"), 1)
                for j in range(4):
                    k = (4 * i + j) * T
                    dve.wait_ge(sem("mix_hi"), 4 * i + j + 1)
                    lo(XL[:, bass.ds(k, T)], A(60, T, k), XH[:, bass.ds(k, T)]).then_inc(sem("mix_lo"), 1)
            residual(80, 80, 8, 1, lambda c: mod[:, bass.ds(c + 16, 1)])
            drain()
            layer_norm(2, Ht, at_kb(0), A(34), lambda t: P1("ln1_w", t), lambda t: P1("ln1_b", t), Ht, "ln_h")
            layer_norm(3, Ht, at_kb(0), A(34), lambda t: mod[:, 32 + t:33 + t], lambda t: mod[:, 24 + t:25 + t], at_kb(0), "ln_u")
            norm_lo(1, "ln")
            ts(H[:], H[:], ALPHA, None, ALU.mult)
            ffn(88, 88, 0)
            residual(132, 132, 8, 3, lambda c: mod[:, bass.ds(c + 40, 1)])
            drain()
            layer_norm(4, Ht, at_kb(0), A(34), lambda t: P1("ln2_w", t), lambda t: P1("ln2_b", t), Ht, "ln_h")

            with dve.Fori(0, LAYERS) as l:
                f0, c0 = l * FILLS_L + FILLS_1, l * (CHUNKS_L // 4) + CHUNKS_1 // 4

                def rms_norm(k, name):
                    n = 2 * l + k
                    dve.wait_ge(sem("rms_rstd"), n + 1)
                    for t in range(DT):
                        ins = stt(A(0, T, t * T), Ht(t, 1), P2(l, name, t), A(34), ALU.mult, ALU.mult)
                        if t % 2:
                            ins.then_inc(sem("rms_u"), 1)
                    norm_lo(n, "rms")

                rms_norm(0, "norm1")
                all_out(c0 + 4)
                z, d = (A(kb, 14 * T).rearrange("p (a t) -> p a t", t=T) for kb in (16, 60))
                tt(d[:, :, 1:T], z[:, :, 0:T - 1], z[:, :, 1:T], ALU.subtract)
                ts(d[:, :, 0:1], z[:, :, 0:1], -1.0, None, ALU.mult)
                drain()
                with dve.Fori(0, 14) as t:
                    stt(A(16, T, t * T), A(60, T, t * T), P2(l, "mu", t), A(16, T, t * T), ALU.mult, ALU.add).then_inc(sem("rw_mix"), 1)
                with dve.Fori(0, PAIRS) as p:
                    n = l * PAIRS + p + 1
                    R, K, V = A(16, T, p * T), A(24, T, p * T), A(32, T, p * T)
                    SG, AA = A(76, T, p * T), A(44, T, p * T)
                    drain()
                    dve.wait_ge(sem("rw_lev"), 12 * l + 12)
                    nc.vector.tensor_tensor_scan(rp("cs", T), C("chunk_start", T), SG, 0.0, ALU.mult, ALU.add)
                    drain()
                    tt(rp("cx", T), rp("cs", T), SG, ALU.subtract).then_inc(sem("rp_cs"), 1)
                    ts(rp("kk", T), K, P2(l, "k_k", p), None, ALU.mult).then_inc(sem("rp_kk"), 1)
                    dve.wait_ge(sem("rp_ss"), n)
                    ts(rp("rn", T), bank(4), 1e-24, None, ALU.max).then_inc(sem("rp_mx"), 1)
                    dve.wait_ge(sem("rp_rn"), n)
                    nc.vector.reciprocal(rp("rn", T), rp("rn", T))
                    drain()
                    tt(rp("kk", T), rp("kk", T), rp("rn", T), ALU.mult)
                    drain()
                    ar = A(60, 2 * T, p * 2 * T).rearrange("p (c k t) -> p c k t", c=NCH, k=2)
                    dve.wait_ge(sem("rp_e"), n)
                    stt(ar[:, :, 0, :], chunks(rp("kk", T)), -1.0, chunks(rp("ex", T)), ALU.mult, ALU.mult)
                    tt(ar[:, :, 1, :], chunks(R), chunks(rp("e", T)), ALU.mult)
                    cp(rc("el", 8, 8 * p),
                       chunks(rp("e", T))[:, :, CHUNK - 1])
                    tt(rp("kk", T), rp("kk", T), AA, ALU.mult)
                    ts(AA, AA, -1.0, P2(l, "k_a", p), ALU.add, ALU.mult)
                    drain()
                    tt(SG, rp("kk", T), rp("ei", T), ALU.mult)
                    stt(AA, AA, 1.0, K, ALU.add, ALU.mult)
                    drain()
                    tt(K, AA, rp("ei", T), ALU.mult)
                    stt(rp("rk", T), R, P2(l, "r_k", p), AA, ALU.mult, ALU.mult).then_inc(sem("rp_rk"), 1)
                    dve.wait_ge(sem("rp_bn"), n)
                    tt(R, bank(5), V, ALU.mult).then_inc(sem("rp_done"), 1)
                nc.vector.memset(rc("state", 512), 0.0).then_inc(sem("rc_st"), 1)
                with dve.Fori(0, NCH) as c:
                    n = l * NCH + c + 1

                    def level(dst, b, mask):
                        return tt(chunks(dst), chunks(bank(b)), bc(mask, 2 * PAIRS), ALU.mult)

                    def plus_identity(name):
                        return tt(chunks(rc(name, 512), 128), chunks(rc(name, 512), 128), bc(C("ident", 128), PAIRS), ALU.add)

                    dve.wait_ge(sem("rc_s1"), n)
                    level(rc("t", 512), 5, C("lower0", 64))
                    level(rc("ak", 512), 6, C("upper", 64))
                    dve.wait_ge(sem("rc_s2"), n)
                    level(rc("u", 512), 4, C("level", 64))
                    level(rc("rbk", 512), 7, C("incl", 64)).then_inc(sem("rc_out"), 1)
                    level(rc("al1", 512), 4, C("level", 64, 64))
                    drain()
                    plus_identity("u")
                    plus_identity("t").then_inc(sem("rc_al"), 1)
                    for v in range(1, 6):
                        if v < 5:
                            level(rc(f"al{(v + 1) % 2}", 512), 4, C("level", 64, 64 * (v + 1)))
                            dve.wait_ge(sem("rc_d"), 4 * n - 4 + v)
                            tt(rc("t", 512), rc("t", 512), bank(6), ALU.add).then_inc(sem("rc_al"), 1)
                        dve.wait_ge(sem("rc_e"), 5 * n - 5 + v)
                        tt(rc("u", 512), rc("u", 512), bank(7), ALU.add).then_inc(sem("rc_uu"), 1)
                    dve.wait_ge(sem("rc_n"), n)
                    tt(rc("state", 512), rc("state", 512), bank(4), ALU.add)
                    drain()
                    dve.wait_ge(sem("rc_yc"), n)
                    el = chunks(rc("el", 32), 8)[:, :, bass.ds(c, 1)].broadcast_to([P, PAIRS, 128])
                    tt(chunks(rc("state", 512), 128), chunks(rc("state", 512), 128), el, ALU.mult).then_inc(sem("rc_st"), 1)
                with dve.Fori(0, PAIRS) as p:
                    n = l * PAIRS + p + 1
                    drain()
                    dve.wait_ge(sem("ro_m"), n)
                    stt(A(92), bank(4), -1.0 / 64, A(84, T, p * T), ALU.mult, ALU.add).then_inc(sem("ro_c"), 1)
                    dve.wait_ge(sem("ro_r"), n)
                    tt(A(92), A(92), A(96), ALU.mult)
                    drain()
                    ts(A(92), A(92), P2(l, "ln_g", p), P2(l, "ln_b", p), ALU.mult, ALU.add)
                    drain()
                    tt(A(92), A(92), A(16, T, p * T), ALU.add)
                    drain()
                    tt(A(92), A(92), A(52, T, p * T), ALU.mult).then_inc(sem("ro_y"), 1)
                    dve.wait_ge(sem("ro_h"), n)
                    lo(HL[:, bass.ds(p * T, T)], A(92), HH[:, bass.ds(p * T, T)]).then_inc(sem("ro_l"), 1)

                def gated(f, c, gate, first, h0):
                    for j in range(8):
                        if j % 2:
                            dve.wait_ge(fill_done, f + j // 2 + 1)
                        else:
                            dve.wait_ge(half_done, l * 12 + h0 + j // 2 + 1)
                        m, g = A(16, T, j * T), A(gate, T, j * T)
                        if first:
                            tt(m, bank(j % 4), g, ALU.mult).then_inc(chunk_out[j % 4], 1)
                        else:
                            tt(g, bank(j % 4), g, ALU.mult).then_inc(chunk_out[j % 4], 1)
                            drain()
                            tt(m, m, g, ALU.add).then_inc(sem("mix_sum"), 1)

                dve.wait_ge(sem("ro_h"), l * PAIRS + PAIRS)
                dve.wait_ge(sem("gate_b_in"), 16 * l + 16)
                gated(f0 + 48, c0 + 12, 60, True, 0)
                all_out(c0 + 17)
                dve.wait_ge(sem("ak_rs"), l + 1)
                stt(at("kn", T), A(12), P2(l, "kg"), at("rs", T), ALU.mult, ALU.mult).then_inc(sem("ak_n"), 1)
                nc.vector.memset(at("sc", 128), MASKED)
                with dve.Fori(0, 2) as j:
                    with dve.Fori(0, 2) as i:
                        n = l * PAIRS + 2 * j + i
                        p = 2 * j + i
                        dve.wait_ge(sem("ak_kv"), l + 1)
                        cp(at("kj", T), at("kd", T, j * T))
                        cp(chunks(at("vj", 256)), chunks(at("vt", T), 128)[:, :, bass.ds(64 * j, 64)]).then_inc(sem("at_in"), 1)
                        dve.wait_ge(sem("at_rs"), n + 1)
                        stt(at("qs", T), A(52, T, p * T), P2(l, "qg"), at("rs", T), ALU.mult, ALU.mult).then_inc(sem("at_q"), 1)
                        for hh in range(2):
                            dve.wait_ge(sem("at_sc"), 2 * n + hh + 1)
                            b = 4 + 2 * hh
                            stt(at("sc", 128, 128), bank(b, 128, 128), 0.125, C("band", 128, 128), ALU.mult, ALU.add)
                            stt(chunks(at("sc", 768, 256), 256), chunks(bank(b, 768, 256), 256), 0.125, bc(C("band", 256), 3), ALU.mult, ALU.add)
                            drain()
                            nc.vector.reduce_max(small[:, 24:28], chunks(at("sc", 1024), 256), AX.X)
                            drain()
                            ts(small[:, 0:4], small[:, 24:28], P2(l, "sinks", 2 * p + hh), -1.0, ALU.max, ALU.mult).then_inc(sem("at_m"), 1)
                            dve.wait_ge(sem("at_p"), 2 * n + hh + 1)
                            tt(small[:, 32:36], small[:, 8:12], small[:, 16:20], ALU.add)
                            drain()
                            nc.vector.reciprocal(small[:, 36:40], small[:, 32:36])
                            drain()
                            pb = chunks(at("pb", 1024), 256)
                            tt(pb, pb, each(small[:, 36:40], 256), ALU.mult).then_inc(sem("at_pn"), 1)
                            dve.wait_ge(sem("at_ptc"), 2 * n + hh + 1)
                        dve.wait_ge(sem("at_o"), 2 * n + 2)
                dve.wait_ge(sem("at_ao"), l * PAIRS + PAIRS)
                nc.vector.memset(rt("state", 128), 0.0)
                with dve.Fori(0, PAIRS) as p:
                    n = l * PAIRS + p + 1
                    drain()
                    dve.wait_ge(sem("table_in"), 16 * l + 16)
                    dve.wait_ge(sem("rq_in"), 16 * l + 16)
                    cp(rt("vs", T), A(76, T, p * T)).then_inc(sem("rt_in"), 1)
                    q, k = A(60, T, p * T), A(68, T, p * T)
                    tt(rt("qr", T), q, TB("cos", T), ALU.mult)
                    stt(rt("kr", T), k, 0.125, TB("cos", T), ALU.mult, ALU.mult)
                    dve.wait_ge(sem("rt_rot"), n)
                    tt(rt("t1", T), bank(4), TB("sin", T), ALU.mult)
                    stt(rt("t2", T), bank(5), 0.125, TB("sin", T), ALU.mult, ALU.mult)
                    drain()
                    tt(rt("qr", T), rt("qr", T), rt("t1", T), ALU.add)
                    tt(rt("kr", T), rt("kr", T), rt("t2", T), ALU.add)
                    drain()
                    tt(chunks(rt("qx", T), 128), chunks(rt("qr", T), 128), bc(TB("xi", 128, 128 * p), 4), ALU.mult)
                    tt(chunks(rt("kz", T), 128), chunks(rt("kr", T), 128), bc(TB("zeta", 128, 128 * p), 4), ALU.mult).then_inc(sem("rt_qk"), 1)
                    dve.wait_ge(sem("rt_sc"), n)
                    for hh in range(2):
                        tt(chunks(rt("st", T, T * hh), 128), chunks(bank(4 + hh), 128), bc(TB("dmat", 128, 128 * (2 * p + hh)), 4), ALU.mult)
                    dve.wait_ge(sem("rt_kv"), n)
                    tt(chunks(rt("t1", 384), 128), chunks(bank(7, 384), 128), bc(C("blk1", 128), 3), ALU.mult)
                    drain()
                    for b in range(NBLK - 1):
                        ins = stt(rt("state", 128, 128 * b + 128), rt("state", 128, 128 * b), C("cd", 1, p), rt("t1", 128, 128 * b), ALU.mult, ALU.add)
                        if b < NBLK - 2:
                            drain()
                    ins.then_inc(sem("rt_r"), 1)
                    dve.wait_ge(sem("rt_rs"), n)
                    tt(rt("t2", T), bank(6), rt("rs", T), ALU.mult)
                    drain()
                    tt(q, rt("t2", T), A(84, T, p * T), ALU.mult).then_inc(sem("rt_done"), 1)
                dve.wait_ge(sem("at_yh"), 2 * l + 1)
                lo(HL[:, 0:4 * T], A(52, 4 * T), HH[:, 0:4 * T]).then_inc(sem("at_y"), 1)
                drain()
                dve.wait_ge(sem("at_yh"), 2 * l + 2)
                lo(HL[:, 4 * T:8 * T], A(60, 4 * T), HH[:, 4 * T:8 * T]).then_inc(sem("at_y"), 1)
                dve.wait_ge(sem("gate_a_in"), 16 * l + 16)
                gated(f0 + 64, c0 + 17, 68, False, 4)
                dve.wait_ge(sem("gate_c_in"), 16 * l + 16)
                gated(f0 + 68, c0 + 19, 84, False, 8)
                for j in range(8):
                    dve.wait_ge(sem("mix_hi"), 8 * l + 8 + j + 1)
                    lo(XL[:, j * T:(j + 1) * T], A(16, T, j * T), XH[:, j * T:(j + 1) * T]).then_inc(sem("mix_lo"), 1)
                residual(f0 + 72, c0 + 21, 8, 1)
                rms_norm(1, "norm2")
                ffn(f0 + 80, c0 + 23, l * FT + FT)
                residual(f0 + 124, c0 + 34, 8, 3)


def columns_of(v):
    return v.reshape(-1, P).T


def shape_constants():
    con = np.zeros((P, N_CONST), np.float32)

    def put(name, a):
        con[:, CONST[name]:CONST[name] + a.shape[1]] = a

    r = np.arange(P)
    half, i64 = r % 64, np.arange(64)
    put("ident", np.eye(P))
    put("ones", np.ones((P, P)))
    put("blk1", (r[:, None] // 64 == r[None, :] // 64))
    put("chunk_start", np.broadcast_to(np.arange(T)[None] % CHUNK != 0, (P, T)))
    put("upper", half[:, None] < i64[None])
    put("incl", half[:, None] <= i64[None])
    put("lower0", (half[:, None] // 2 == i64[None] // 2) & (half[:, None] % 2 == 1) & (i64[None] % 2 == 0))
    levels = [(half[:, None] // (2 * b) == i64[None] // (2 * b)) & (half[:, None] // b % 2 == 0) & (i64[None] // b % 2 == 1)
              for b in (1, 2, 4, 8, 16, 32)]
    put("level", np.concatenate(levels, axis=1))
    key = np.arange(2 * BLK)
    seen = (key[None] > r[:, None]) & (key[None] <= r[:, None] + BLK)
    put("band", np.where(seen, 0.0, MASKED))
    put("dup", np.concatenate([r[:, None] == 64 * j + half[None] for j in range(2)], axis=1))
    put("eps", np.broadcast_to(np.float32([[1e-5, 1e-6, 64e-5, 0.0]]), (P, 4)))

    table = np.zeros((P, N_TABLE), np.float32)

    def put_t(name, a):
        table[:, TABLE[name]:TABLE[name] + a.shape[1]] = a

    inv = np.float32(1.0) / np.power(np.float32(10000.0), np.arange(32, dtype=np.float32) * np.float32(2.0) / np.float32(64))
    angle = np.arange(T, dtype=np.float32)[None] * inv[r % 32][:, None].astype(np.float32)
    put_t("cos", np.cos(angle))
    put_t("sin", np.sin(angle))
    lg = np.log1p(-np.power(2.0, -5.0 - np.arange(HEADS)))
    pos = np.arange(BLK)
    diff = pos[None] - pos[:, None]
    put_t("dmat", np.concatenate([np.where(diff >= 0, np.exp(g * np.maximum(diff, 0)), 0.0) for g in lg], axis=1))
    of = lambda p: lg[2 * p + r // 64][:, None]
    put_t("xi", np.concatenate([np.exp(of(p) * (pos[None] + 1.0)) for p in range(PAIRS)], axis=1))
    put_t("zeta", np.concatenate([np.exp(of(p) * (BLK - 1.0 - pos[None])) for p in range(PAIRS)], axis=1))
    put("cd", np.concatenate([np.exp(of(p) * BLK) for p in range(PAIRS)], axis=1))
    rot = np.zeros((P, P))
    for m in range(P):
        rot[m + 32 if m % 64 < 32 else m - 32, m] = -1.0 if m % 64 < 32 else 1.0
    put_t("rot", rot)
    return con, table


def kernel(**inputs):
    import concourse.bacc as bacc
    from concourse.bass_utils import run_bass_kernel_spmd

    a = {k: np.asarray(v) for k, v in inputs.items()}

    def fills_of(w):
        k, n = w.shape
        t = w.reshape(k // P, P, n // P, P).transpose(2, 1, 0, 3)
        if k == D:
            return t.reshape(n // P, P, 8 * P)
        if k == D // 2:
            return t.reshape(n // P // 2, 2, P, 4 * P).transpose(0, 2, 1, 3).reshape(n // P // 2, P, 8 * P)
        t = np.pad(t, ((0, 0), (0, 0), (0, 24 - k // P), (0, 0)))
        return t.reshape(n // P, P, 3, 8 * P).transpose(0, 2, 1, 3).reshape(n // P * 3, P, 8 * P)

    def turns(parts, order):
        out, at = [], [0] * len(parts)
        while at[0] < len(parts[0]):
            for k, m in enumerate(order):
                out.append(parts[k][at[k]:at[k] + m])
                at[k] += m
        return np.concatenate(out)

    w_in = fills_of(a["w_in"][0])
    zq, zf, zi, zg, zu, zv, ga, gb = (w_in[8 * k:8 * k + 8] for k in range(8))
    ffn = fills_of(a["w_ffn_in"][0])
    fills = [turns([zq, zg, zf, zi], [1, 1, 1, 1]), turns([zu, zv], [2, 2]), ga, fills_of(a["w_proj_a"][0]), gb,
             fills_of(a["w_proj_b"][0]), fills_of(a["w_out"][0]), turns([ffn[:FT], ffn[FT:]], [1, 1]), fills_of(a["w_ffn_out"][0])]
    for l in range(LAYERS):
        w = fills_of(a["w_in_2"][l])
        aq, ak, av, rw, ret = w[0:4], w[4:5], w[5:6], w[6:20], w[20:36]
        gates = [w[36 + 8 * k:44 + 8 * k] for k in range(3)]
        gated = turns([gates[0], gates[1], gates[2], np.concatenate([aq, ret[:4]])], [1, 1, 1, 1])
        fills += [ak, av, rw, gated, fills_of(a["w_rwkv_o_2"][l]), ret[4:], fills_of(a["w_attn_o_2"][l]),
                  fills_of(a["w_ret_o_2"][l]), fills_of(a["w_out_2"][l]),
                  turns([fills_of(a["w_ffn_gate_2"][l]), fills_of(a["w_ffn_up_2"][l])], [1, 1]), fills_of(a["w_ffn_down_2"][l])]
    fills.append(np.zeros((LEAD, P, 8 * P), np.float32))
    fills = np.concatenate(fills)
    assert fills.shape[0] == FILLS

    con, table = shape_constants()
    ln = lambda name: columns_of(a[name][0])
    par1 = np.concatenate([columns_of(a["c"][0]), ln("b_ada"), columns_of(a["hgrn_lb_logits"][0]), columns_of(a["hgrn_lb_logits"][1]),
                           ln("hgrn_norm_w"), ln("gmlp_ln_w"), ln("gmlp_ln_b"), columns_of(a["b_gate"][0].reshape(-1)),
                           ln("ln1_w"), ln("ln1_b"), ln("ln2_w"), ln("ln2_b")], axis=1)
    twice = lambda v: np.concatenate([v, v])[:, None]
    par2 = np.concatenate([np.concatenate(
        [columns_of(a["norm1_g_2"][l]), columns_of(a["norm2_g_2"][l]), twice(a["attn_q_norm_g_2"][l]), twice(a["attn_k_norm_g_2"][l]),
         np.broadcast_to(a["attn_sinks_2"][l][None], (P, HEADS)), columns_of(a["rwkv_shift_mu_2"][l])]
        + [columns_of(a[f"rwkv_{n}_2"][l].reshape(-1)) for n in ("w0", "a0", "k_k", "k_a", "r_k", "lnx_g", "lnx_b")], axis=1)
        for l in range(LAYERS)], axis=1)
    arrays = {
        "x": a["x"][0].reshape(T, DT, P).transpose(2, 1, 0).reshape(P, DT * T),
        "w_ada": a["w_ada"][0].reshape(DT, P, 12, 4, P).transpose(2, 1, 3, 0, 4).reshape(12, P, 16 * KB),
        "fills": fills, "con": con, "table": table, "par1": par1, "par2": par2,
        "gm_ws": a["gmlp_ws"][0].transpose(2, 0, 1).reshape(P, 8 * P),
        "gm_bs": a["gmlp_bs"][0].reshape(1, 8 * P),
        "lora": np.concatenate([np.concatenate([a["rwkv_w2_2"], a["rwkv_a2_2"]], axis=1), a["rwkv_g2_2"]], axis=2),
    }
    arrays = {k: np.ascontiguousarray(v) for k, v in arrays.items()}
    nc = bacc.Bacc("TRN2", target_bir_lowering=False, num_devices=1)
    dram = {k: nc.dram_tensor("in_" + k, v.shape, F32, kind="ExternalInput").ap() for k, v in arrays.items()}
    out = nc.dram_tensor("out", (P, DT * T), F32, kind="ExternalOutput").ap()
    scratch = nc.dram_tensor("scratch", (LAYERS * 32, P, T), F32, kind="Internal").ap()
    build(nc, dram, out, scratch)
    r = run_bass_kernel_spmd(nc, [{"in_" + k: v for k, v in arrays.items()}], core_ids=[0])
    got = np.asarray(r.results[0]["out"])
    return np.ascontiguousarray(got.reshape(P, DT, T).transpose(2, 1, 0).reshape(1, T, D))
```

```python
from contextlib import ExitStack

import numpy as np
import concourse.bass as bass
from concourse import mybir

F32, F32R = mybir.dt.float32, mybir.dt.float32r
ALU, ACT, AX = mybir.AluOpType, mybir.ActivationFunctionType, mybir.AxisListType

P = 128
T = 512
D = 1024
DT = D // P
FF = 2816
FT = FF // P
LAYERS = 2
HEADS = 8
CHUNK = 64
NCH = T // CHUNK
SUB = 16
BLK = 128
NBLK = T // BLK
PAIRS = 4
ALPHA = 2.0 ** 0.25
RWKV_DECAY = float(np.exp(np.float32(-0.5)))
KB = 256

FILLS_1 = 32 + 16 + 4 * 8 + 8 + 44 + 24
FILLS_L = 16 + 32 + 4 + 12 + 4 + 4 + 8 + 44 + 24
LEAD = 4
FILLS = FILLS_1 + LAYERS * FILLS_L + LEAD
CHUNKS_1 = 32 + 16 + 4 * 8 + 8 + 44 + 8
CHUNKS_L = 16 + 32 + 8 + 12 + 8 + 8 + 8 + 44 + 8

def columns(sizes):
    at, out = 0, {}
    for name, n in sizes:
        out[name] = at
        at += n
    return out, at

CONST, N_CONST = columns([("ident", 128), ("ones", 128), ("blk1", 128), ("chunk_start", T), ("upper", 64), ("incl", 64),
                          ("lower0", 64), ("level", 6 * 64), ("band", 256),
                          ("dup", 256), ("cd", 4), ("eps", 4)])
TABLE, N_TABLE = columns([("cos", T), ("sin", T), ("dmat", 8 * 128), ("xi", 4 * 128), ("zeta", 4 * 128), ("rot", 128)])
PAR1, N_PAR1 = columns([("c", 8), ("b_ada", 48), ("lb0", 8), ("lb1", 8), ("hg_w", 1), ("gm_w", 8), ("gm_b", 8),
                        ("b_gate", 16), ("ln1_w", 8), ("ln1_b", 8), ("ln2_w", 8), ("ln2_b", 8)])
PAR2, N_PAR2 = columns([("norm1", 8), ("norm2", 8), ("qg", 1), ("kg", 1), ("sinks", 8), ("mu", 14), ("w0", 4), ("a0", 4),
                        ("k_k", 4), ("k_a", 4), ("r_k", 4), ("ln_g", 4), ("ln_b", 4)])
MASKED = -1.0e30

HG = {"ks": 76, "state": 84, "val_t": 88, "kdec_t": 90, "k": 32, "lf": 34, "cum": 36, "qs": 38, "e1": 40, "qi": 42,
      "kdec": 104.5, "st": 106.5, "val": 34, "o": 38, "sq": 32, "rstd": 36}
RP = {"rn": 0, "kk": 8, "kb": 10, "cs": 40, "cx": 42, "ei": 84, "ex": 86, "e": 92, "rk": 94}
RC = {"a": 0, "b": 2, "k": 4, "v": 6, "ak": 8, "b_t": 10, "k_t": 40, "v_t": 42, "u": 44, "t": 46, "p": 48, "us": 50,
      "state": 92, "al0": 94, "al1": 96, "rbk": 98, "el": 100, "spill": 101}
AT = {"sq": 0, "rs": 2, "kn": 4, "vt": 6, "kd": 8, "sc": 40, "pb": 44, "pt": 48, "kj": 104.5, "qs": 106.5, "vj": 108.5}
RT = {"qr": 0, "kr": 2, "qx": 4, "kz": 6, "vs": 8, "t1": 10, "t2": 12, "rs": 14, "kz_t": 16, "v_t": 18, "st": 20, "state": 24, "sq": 26}
ARENA_KB = 109.5


def build(nc, dram, out, scratch):
    ctx = ExitStack()
    with ctx:
        def sb(name, cols, dt=F32):
            return ctx.enter_context(nc.sbuf_tensor(name, [P, cols], dt))

        sems = {}

        def sem(name):
            if name not in sems:
                sems[name] = ctx.enter_context(nc.semaphore(name))
            return sems[name]

        FILL = 8 * 128
        w_raw = sb("w_raw", 2 * FILL)
        w_hi = sb("w_hi", 4 * FILL, F32R)
        w_lo = sb("w_lo", 4 * FILL, F32R)
        H = sb("H", DT * T)
        x_at = nc.sbuf_base
        XH = sb("XH", DT * T, F32R)
        XL = sb("XL", DT * T, F32R)
        con = sb("con", N_CONST)
        par1 = sb("par1", N_PAR1)
        par2 = sb("par2", LAYERS * N_PAR2)
        mod = sb("mod", 48)
        cond = sb("cond", 8)
        lbs = sb("lbs", 16)
        lbt = sb("lbt", 32)
        small = sb("small", 64)
        arena = sb("arena", int(ARENA_KB * KB))
        arena_at = nc.sbuf_base - int(ARENA_KB * KB) * 4
        HH = nc.alloc_sbuf_tensor_at("HH", [P, FT * T], F32R, offset=arena_at)
        HL = nc.alloc_sbuf_tensor_at("HL", [P, FT * T], F32R, offset=arena_at + 4 * FT * T)
        X32 = nc.alloc_sbuf_tensor_at("X32", [P, 2 * DT * T], F32, offset=x_at)
        psum = ctx.enter_context(nc.psum_tensor("psum", [P, 8 * 512], F32))

        def A(kb, n=T, at=0):
            lo = int(kb * KB)
            if isinstance(at, int):
                return arena[:, lo + at:lo + at + n]
            return arena[:, bass.ds(lo + at, n)]

        def tile(t, n, at):
            return t[:, at:at + n] if isinstance(at, int) else t[:, bass.ds(at, n)]

        def C(name, n, at=0):
            return tile(con, n, CONST[name] + at)

        def TB(name, n, at=0):
            return A(92, n, TABLE[name] + at)

        def P1(name, at=0, n=1):
            return tile(par1, n, PAR1[name] + at)

        def P2(l, name, at=0, n=1):
            return tile(par2, n, l * N_PAR2 + PAR2[name] + at)

        def bank(b, n=512, at=0):
            return psum[:, 512 * b + at:512 * b + at + n]

        def region(table):
            return lambda name, n, at=0: A(table[name], n, at)

        hg, rp, rc, at = (region(table) for table in (HG, RP, RC, AT))

        def rt(name, n, at=0):
            lo = RT[name] * KB + at
            return X32[:, lo:lo + n]

        def chunks(ap, c=CHUNK):
            return ap.rearrange("p (a c) -> p a c", c=c)

        def bc(ap, n):
            return ap.unsqueeze(1).broadcast_to([ap.shape[0], n, ap.shape[1]])

        def each(ap, n):
            return ap.unsqueeze(2).broadcast_to([ap.shape[0], ap.shape[1], n])

        w_loaded = [sem(f"w_loaded{s}") for s in range(2)]
        hi_ready = sem("hi_ready")
        lo_ready = sem("lo_ready")
        fill_done = sem("fill_done")
        half_done = sem("half_done")
        chunk_out = [sem(f"chunk_out{b}") for b in range(4)]

        spilled = [sem(f"spilled{j}") for j in range(4)]

        def quarter(c):
            return c // 4 if isinstance(c, int) else c

        def arrived(f, k):
            return 8 * f + 16 * (k // 2) + 16

        block = ctx.enter_context(nc.Block())

        @block.sync
        def _(sp):
            sp.dma_start(con[:], dram["con"]).then_inc(sem("const_in"), 16)
            sp.dma_start(par1[:], dram["par1"]).then_inc(sem("const_in"), 16)
            sp.dma_start(par2[:], dram["par2"]).then_inc(sem("const_in"), 16)
            sp.dma_start(H[:], dram["x"]).then_inc(sem("x_in"), 16)
            for k in range(2):
                sp.dma_start(A(16 * k, 16 * KB), dram["w_ada"][k]).then_inc(sem(f"ada_in{k}"), 16)
            for f in range(2):
                sp.dma_start(w_raw[:, f * FILL:(f + 1) * FILL], dram["fills"][f]).then_inc(w_loaded[f], 16)
            with sp.Fori(0, 5) as i:
                for k in range(2):
                    sp.wait_ge(sem("ada_used"), 2 * i + k + 1)
                    sp.dma_start(A(16 * k, 16 * KB),
                                 dram["w_ada"][bass.ds(2 * i + k + 2, 1)].rearrange("a p n -> (a p) n")).then_inc(sem(f"ada_in{k}"), 16)
            with sp.Fori(0, FILLS // 2 - 1) as i:
                for s in range(2):
                    sp.wait_ge(lo_ready, 2 * i + s + 1)
                    sp.dma_start(w_raw[:, s * FILL:(s + 1) * FILL],
                                 dram["fills"][bass.ds(2 * i + s + 2, 1)].rearrange("a p n -> (a p) n")).then_inc(w_loaded[s], 16)
            for b in range(4):
                sp.wait_ge(chunk_out[b], (CHUNKS_1 + LAYERS * CHUNKS_L) // 4)
            sp.dma_start(out, H[:]).then_inc(sem("stored"), 16)
            sp.wait_ge(sem("stored"), 16)

        @block.gpsimd
        def _(pool):
            def lo_part(f, j):
                pool.wait_ge(hi_ready, f + 1)
                nc.gpsimd.tensor_tensor(w_lo[:, j * FILL:(j + 1) * FILL], w_raw[:, (j % 2) * FILL:(j % 2 + 1) * FILL],
                                        w_hi[:, j * FILL:(j + 1) * FILL].bitcast(F32), ALU.subtract).then_inc(lo_ready, 1)

            def lo_parts(f, n):
                with pool.Fori(0, n // 4) as i:
                    for k in range(4):
                        lo_part(f + 4 * i + k, (3 + k) % 4)

            for f in range(3):
                lo_part(f, f)
            lo_parts(3, FILLS_1)
            mask = C("blk1", 128).rearrange("p (k t) -> p k t", k=2).unsqueeze(1).broadcast_to([P, PAIRS, 2, 64])
            with pool.Fori(0, LAYERS) as l:
                f0 = l * FILLS_L + FILLS_1
                lo_parts(f0 + 3, 16)
                pool.wait_ge(sem("rp_done"), l * PAIRS + PAIRS)
                nc.gpsimd.tensor_tensor(small[:, 62:63], small[:, 61:62], small[:, 61:62], ALU.add)
                with pool.Fori(0, NCH) as c:
                    n = l * NCH + c + 1
                    for name, kb, step in (("b", 76, 1), ("k", 24, 1), ("v", 32, 1), ("a", 60, 2)):
                        src = A(kb, 4 * step * T).rearrange("p (a t) -> p a t", a=PAIRS)[:, :, bass.ds(c * step * CHUNK, CHUNK)]
                        ins = nc.gpsimd.tensor_tensor(rc(name, 512).rearrange("p (a k t) -> p a k t", a=PAIRS, k=2),
                                                      src.unsqueeze(2).broadcast_to([P, PAIRS, 2, CHUNK]), mask, ALU.mult)
                    ins.then_inc(sem("rc_in"), 1)
                    for k in range(4):
                        lo_part(f0 + 19 + 4 * c + k, (3 + k) % 4)
                    pool.wait_ge(sem("rc_w"), n)
                    nc.gpsimd.tensor_tensor(small[:, 62:63], small[:, 61:62], small[:, 61:62], ALU.add)
                lo_parts(f0 + 51, FILLS_L - 48)

        @block.tensor
        def _(pe):
            mm = nc.tensor.matmul

            def blocks(slot, xh, xl, out_ap, cols, tiles, first, last):
                n = len(cols)
                for k in range(n):
                    w = slot * FILL + cols[k] * 128
                    x0 = tiles[k] * T
                    ops = [(w_hi, xh), (w_lo, xh), (w_hi, xl)]
                    for o, (wt, xt) in enumerate(ops):
                        ins = mm(out_ap, wt[:, w:w + 128], xt[:, x0:x0 + T],
                                 start=first and k == 0 and o == 0, stop=last and k == n - 1 and o == 2)
                return ins

            def gemm(f, c, n, xh=XH, xl=XL, ready=None, value=0):
                if isinstance(c, int) and c == 0:
                    for j in range(4):
                        pe.wait_ge(lo_ready, j + 1)
                        blocks(j, xh, xl, bank(j), range(8), range(8), True, True).then_inc(fill_done, 1)
                    f, c, n = 4, 4, n - 4
                with pe.Fori(0, n // 4) as i:
                    for j in range(4):
                        if ready and j == 0:
                            pe.wait_ge(ready, value)
                        pe.wait_ge(lo_ready, f + 4 * i + j + 1)
                        pe.wait_ge(chunk_out[j], quarter(c) + i)
                        blocks(j, xh, xl, bank(j), range(8), range(8), True, True).then_inc(fill_done, 1)

            def gemm512(f, c, tile0):
                for j in range(4):
                    pe.wait_ge(lo_ready, f + j + 1)
                    for h in range(2):
                        b = (2 * j + h) % 4
                        pe.wait_ge(chunk_out[b], quarter(c) + j // 2)
                        blocks(j, HH, HL, bank(b), range(4 * h, 4 * h + 4), range(tile0, tile0 + 4), True, True)\
                            .then_inc(fill_done if h else half_done, 1)

            def gemm2816(f, c, value):
                with pe.Fori(0, 2) as i:
                    for j in range(12):
                        q, part = divmod(j, 3)
                        if j == 0:
                            pe.wait_ge(sem("ffn_lo"), value)
                        pe.wait_ge(lo_ready, f + 12 * i + j + 1)
                        if part == 0:
                            pe.wait_ge(chunk_out[q], quarter(c) + i)
                        n = min(8, FT - 8 * part)
                        blocks(j % 4, HH, HL, bank(q), range(n), range(8 * part, 8 * part + n), part == 0, part == 2)\
                            .then_inc(fill_done, 1)

            def mean_of_squares(n, name, src):
                for t in range(DT):
                    if t % 2 == 0:
                        pe.wait_ge(sem(name + "_sq"), 4 * n + t // 2 + 1)
                    ins = mm(bank(5), C("ones", 128), src(t), start=t == 0, stop=t == DT - 1)
                ins.then_inc(sem(name + "_var"), 1)

            def layer_norm(n, src, sq):
                for t in range(DT):
                    ins = mm(bank(4), C("ones", 128), src(t), start=t == 0, stop=t == DT - 1)
                ins.then_inc(sem("ln_sum"), 1)
                mean_of_squares(n, "ln", sq)

            def all_out(c):
                for b in range(4):
                    pe.wait_ge(chunk_out[b], quarter(c))

            def transposes(b, src, n=4):
                for k in range(n):
                    ins = nc.tensor.transpose(bank(b, 128, 128 * k), src(k), C("ident", 128))
                return ins

            pe.wait_ge(sem("cond"), 1)
            with pe.Fori(0, 6) as i:
                for k in range(2):
                    pe.wait_ge(sem(f"ada_in{k}"), 16 * i + 16)
                    for t in range(4):
                        for kt in range(DT):
                            ins = mm(psum[:, bass.ds(512 * 6 + 8 * i + 4 * k + t, 1)],
                                     A(16 * k, 128, (t * DT + kt) * 128), cond[:, kt:kt + 1], start=kt == 0, stop=kt == DT - 1)
                    ins.then_inc(sem("ada_used"), 1)
            pe.wait_ge(sem("x_in"), 16)
            layer_norm(0, lambda t: H[:, t * T:(t + 1) * T], lambda t: A(16, T, t * T))
            pe.wait_ge(sem("ln_x"), 4)
            gemm(0, 0, 32)
            with pe.Fori(0, HEADS) as h:
                pe.wait_ge(sem("hg_q"), h + 1)
                transposes(4, lambda k: hg("kdec", 128, 128 * k))
                transposes(5, lambda k: hg("val", 128, 128 * k)).then_inc(sem("hg_tr"), 1)
                pe.wait_ge(sem("hg_k"), h + 1)
                for c in range(NCH):
                    for s in range(4):
                        ins = mm(bank(6, SUB, 64 * (c // 2) + SUB * s)[64 * (c % 2):64 * (c % 2) + 64],
                                 hg("ks", 64, (4 * c + s) * 64), hg("qs", SUB, c * CHUNK + s * SUB), start=True, stop=True)
                ins.then_inc(sem("hg_sc"), 1)
                pe.wait_ge(sem("hg_tm"), h + 1)
                for c in range(NCH - 1):
                    p0, t0 = 64 * (c % 2), 128 * (c // 2)
                    ins = mm(bank(4 if c % 2 else 7, 128, t0), hg("kdec_t", 128, t0)[p0:p0 + 64], hg("val_t", 128, t0)[p0:p0 + 64],
                             start=True, stop=True)
                ins.then_inc(sem("hg_u"), 1)
                pe.wait_ge(sem("hg_st"), h + 1)
                pe.wait_ge(sem("hg_s"), h + 1)
                for b in range(NBLK):
                    mm(bank(5, 128, 128 * b), hg("val_t", 128, 128 * b), hg("st", 128, 128 * b), start=True, stop=False)
                    for c in (2 * b, 2 * b + 1):
                        ins = mm(bank(5, 64, 64 * c), hg("state", 128, 128 * c), hg("qi", 64, 64 * c), start=False, stop=c % 2 == 1)
                ins.then_inc(sem("hg_o"), 1)
                pe.wait_ge(sem("hg_sq"), h + 1)
                mm(bank(6), C("ones", 128), hg("sq", T), start=True, stop=True).then_inc(sem("hg_var"), 1)
            gemm(32, 32, 16)
            all_out(48)
            layer_norm(1, lambda t: A(60, T, t * T), lambda t: A(76, T, t * T))
            pe.wait_ge(sem("ln_h"), 4)
            pe.wait_ge(sem("gm_mask"), 1)
            with pe.Fori(0, 8) as g:
                pe.wait_ge(sem("gm_vs"), g + 1)
                transposes(4, lambda k: A(40, 128, 128 * k)).then_inc(sem("gm_tr"), 1)
                pe.wait_ge(sem("gm_vt"), g + 1)
                for b in range(NBLK):
                    ins = mm(bank(5, 128, 128 * b), A(42, 128, 128 * b), A(32, 128, 128 * g), start=True, stop=True)
                ins.then_inc(sem("gm_sv"), 1)
            gemm(48, 48, 8)
            pe.wait_ge(sem("hg_y"), HEADS)
            gemm(56, 56, 8, HH, HL)
            gemm(64, 64, 8)
            pe.wait_ge(sem("gm_lo"), 4)
            gemm(72, 72, 8, HH, HL)
            pe.wait_ge(sem("mix_lo"), 8)
            gemm(80, 80, 8)
            all_out(88)
            layer_norm(2, lambda t: H[:, t * T:(t + 1) * T], lambda t: A(16, T, t * T))
            pe.wait_ge(sem("ln_h"), 8)
            layer_norm(3, lambda t: H[:, t * T:(t + 1) * T], lambda t: A(16, T, t * T))
            pe.wait_ge(sem("ln_x"), 8)
            gemm(88, 88, 44)
            gemm2816(132, 132, FT)
            all_out(140)
            layer_norm(4, lambda t: H[:, t * T:(t + 1) * T], lambda t: A(16, T, t * T))

            with pe.Fori(0, LAYERS) as l:
                f0, c0 = l * FILLS_L + FILLS_1, l * (CHUNKS_L // 4) + CHUNKS_1 // 4
                mean_of_squares(2 * l, "rms", lambda t: A(16, T, t * T))
                gemm(f0, c0, 16, ready=sem("rms_x"), value=8 * l + 4)
                pe.wait_ge(sem("rp_k2"), l + 1)
                for p in range(PAIRS):
                    ins = mm(bank(4 + p), C("blk1", 128), rp("rn", T, p * T), start=True, stop=True)
                ins.then_inc(sem("rp_ss"), 1)
                pe.wait_ge(sem("rw_act"), l + 1)
                pe.wait_ge(sem("lora_in"), 16 * l + 16)
                for n in range(4):
                    mm(bank(n), A(88, 128, 128 * n)[0:64], A(16, T, 12 * T)[0:64], start=True, stop=True).then_inc(sem("rw_lora"), 1)
                pe.wait_ge(sem("rp_mx"), l + 1)
                for n in range(4):
                    mm(bank(4 + n), A(88, 128, 128 * n)[64:128], A(16, T, 12 * T)[64:128], start=True, stop=True).then_inc(sem("rw_lora"), 1)
                for n in range(4):
                    pe.wait_ge(sem("rw_lev"), 12 * l + n + 1)
                    mm(bank(n), A(88, 128, 512 + 128 * n), A(16, T, 13 * T), start=True, stop=True).then_inc(sem("rw_lora"), 1)
                with pe.Fori(0, PAIRS) as p:
                    pe.wait_ge(sem("rp_rk"), 4 * l + p + 1)
                    mm(bank(5), C("blk1", 128), rp("rk", T), start=True, stop=True).then_inc(sem("rp_bn"), 1)
                with pe.Fori(0, NCH) as c:
                    n = l * NCH + c + 1
                    pairs = range(PAIRS)

                    def half_fill(k):
                        j, h = divmod(k, 2)
                        if h == 0:
                            pe.wait_ge(lo_ready, f0 + 16 + 4 * c + j + 1)
                            pe.wait_ge(chunk_out[j], c0 + 4 + c)
                        ins = blocks(j, XH, XL, bank(j), range(4 * h, 4 * h + 4), range(4 * h, 4 * h + 4), h == 0, h == 1)
                        if h:
                            ins.then_inc(fill_done, 1)

                    def bd(name, p):
                        return rc(name, 128, 128 * p)

                    def product(b, *terms):
                        for p in pairs:
                            for k, (left, right) in enumerate(terms):
                                ins = mm(bank(b, 128, 128 * p), bd(left, p), C("ident", 128) if right is None else bd(right, p),
                                         start=k == 0, stop=k == len(terms) - 1)
                        return ins

                    def r(p):
                        return A(60, 64, 2 * T * p + 64 + c * 128)

                    pe.wait_ge(sem("rc_in"), n)
                    product(5, ("a", "b"))
                    product(6, ("k", "a")).then_inc(sem("rc_s1"), 1)
                    pe.wait_ge(sem("rc_st"), n + l)
                    product(4, ("b", "a"))
                    for p in pairs:
                        mm(bank(7, 64, 128 * p), bd("b", p), r(p), start=True, stop=True)
                        ins = mm(bank(7, 64, 128 * p + 64), bd("k", p), r(p), start=True, stop=True)
                    ins.then_inc(sem("rc_s2"), 1)
                    half_fill(0)
                    pe.wait_ge(sem("rc_out"), n)
                    product(5, ("b", None))
                    product(6, ("k", None))
                    product(7, ("v", None)).then_inc(sem("rc_tr"), 1)
                    pe.wait_ge(sem("rc_trc"), n)
                    for v in range(1, 6):
                        pe.wait_ge(sem("rc_al"), 5 * n - 5 + v)
                        product(5, (f"al{v % 2}", "t")).then_inc(sem("rc_p"), 1)
                        half_fill(v)
                        pe.wait_ge(sem("rc_pc"), 5 * n - 5 + v)
                        if v > 1:
                            pe.wait_ge(sem("rc_uu"), 5 * n - 6 + v)
                        if v < 5:
                            product(6, ("u", "p")).then_inc(sem("rc_d"), 1)
                        product(7, ("p", "u")).then_inc(sem("rc_e"), 1)
                    product(5, ("a", "state"), ("ak", "v_t")).then_inc(sem("rc_w"), 1)
                    half_fill(6)
                    pe.wait_ge(sem("rc_wc"), n)
                    pe.wait_ge(sem("rc_uu"), 5 * n)
                    product(6, ("u", "p")).then_inc(sem("rc_u"), 1)
                    half_fill(7)
                    pe.wait_ge(sem("rc_uc"), n)
                    for p in pairs:
                        y = bank(7, 64, 64 * p)
                        mm(y, bd("state", p), r(p), start=True, stop=False)
                        mm(y, bd("us", p), rc("rbk", 64, 128 * p), start=False, stop=False)
                        ins = mm(y, bd("v_t", p), rc("rbk", 64, 128 * p + 64), start=False, stop=True)
                    ins.then_inc(sem("rc_y"), 1)
                    product(4, ("b_t", "us"), ("k_t", "v_t")).then_inc(sem("rc_n"), 1)
                pe.wait_ge(sem("rc_st"), (l + 1) * (NCH + 1))
                for h in range(2):
                    for p in (2 * h, 2 * h + 1):
                        ins = mm(bank(4 + p), C("blk1", 128), A(84, T, p * T), start=True, stop=True)
                    ins.then_inc(sem("ro_m"), 1)
                all_out(c0 + 12)
                for h in range(2):
                    pe.wait_ge(sem("ro_s"), 2 * l + h + 1)
                    for p in (2 * h, 2 * h + 1):
                        ins = mm(bank(p), C("blk1", 128), A(100, T, p * T), start=True, stop=True)
                    ins.then_inc(sem("ro_v"), 1)
                pe.wait_ge(sem("ro_l"), 2 * l + 2)
                gemm512(f0 + 48, c0 + 12, 0)
                gemm(f0 + 52, c0 + 14, 12)
                pe.wait_ge(sem("ak_sq"), l + 1)
                mm(bank(4), C("blk1", 128), at("sq", T), start=True, stop=True).then_inc(sem("ak_ss"), 1)
                transposes(5, lambda k: A(14, 128, 128 * k)).then_inc(sem("av_tr"), 1)
                pe.wait_ge(sem("ak_n"), l + 1)
                for j in range(2):
                    ins = mm(bank(6 + j), C("dup", 128, 128 * j), at("kn", T), start=True, stop=True)
                ins.then_inc(sem("ak_dup"), 1)
                with pe.Fori(0, PAIRS) as p:
                    n = l * PAIRS + p
                    halves = (slice(0, 64), slice(64, 128))

                    def scores(hh):
                        for b in range(NBLK):
                            k0, k1 = max(0, BLK * (b - 1)), BLK * (b + 1)
                            ins = mm(bank(4, k1 - k0, 256 * b + 256 - (k1 - k0)), at("qs", 128, 128 * b)[halves[hh]],
                                     at("kj", k1 - k0, k0)[halves[hh]], start=True, stop=True)
                        ins.then_inc(sem("at_sc"), 1)

                    def probs_t(hh):
                        for s in range(1, 8):
                            ins = nc.tensor.transpose(bank(6 - 2 * hh, 128, 128 * s), at("pb", 128, 128 * s), C("ident", 128))
                        ins.then_inc(sem("at_pt"), 1)

                    def weighted(hh):
                        for b in range(NBLK):
                            o = bank(6, 128, 128 * b)[halves[hh]]
                            if b:
                                mm(o, at("vj", 64, 64 * (b - 1)), at("pt", 128, 256 * b), start=True, stop=False)
                            ins = mm(o, at("vj", 64, 64 * b), at("pt", 128, 256 * b + 128), start=b == 0, stop=True)
                        ins.then_inc(sem("at_o"), 1)

                    pe.wait_ge(sem("table_in"), 16 * l + 16)
                    pe.wait_ge(sem("rq_in"), 16 * l + 16)
                    pe.wait_ge(sem("at_sq"), n + 1)
                    mm(bank(7), C("blk1", 128), at("sq", T), start=True, stop=True).then_inc(sem("at_ss"), 1)
                    pe.wait_ge(sem("rt_in"), n + 1)
                    mm(bank(0), TB("rot", 128), A(60, T, p * T), start=True, stop=True)
                    mm(bank(1), TB("rot", 128), A(68, T, p * T), start=True, stop=True).then_inc(sem("rt_rot"), 1)
                    pe.wait_ge(sem("at_q"), n + 1)
                    scores(0)
                    pe.wait_ge(sem("rt_qk"), n + 1)
                    transposes(2, lambda k: rt("kz", 128, 128 * k))
                    transposes(3, lambda k: rt("vs", 128, 128 * k)).then_inc(sem("rt_tr"), 1)
                    for hh in range(2):
                        for b in range(NBLK):
                            ins = mm(bank(hh, 128, 128 * b), rt("kr", 128, 128 * b)[halves[hh]], rt("qr", 128, 128 * b)[halves[hh]], start=True, stop=True)
                    ins.then_inc(sem("rt_sc"), 1)
                    pe.wait_ge(sem("at_m"), 2 * n + 1)
                    scores(1)
                    pe.wait_ge(sem("rt_tm"), n + 1)
                    for b in range(NBLK - 1):
                        ins = mm(bank(3, 128, 128 * b), rt("kz_t", 128, 128 * b), rt("v_t", 128, 128 * b), start=True, stop=True)
                    ins.then_inc(sem("rt_kv"), 1)
                    pe.wait_ge(sem("at_pn"), 2 * n + 1)
                    probs_t(0)
                    pe.wait_ge(sem("rt_r"), n + 1)
                    for b in range(NBLK):
                        mm(bank(2, 128, 128 * b), rt("state", 128, 128 * b), rt("qx", 128, 128 * b), start=True, stop=False)
                        for hh in range(2):
                            ins = mm(bank(2, 128, 128 * b)[halves[hh]], rt("v_t", 64, 128 * b + 64 * hh), rt("st", 128, 512 * hh + 128 * b),
                                     start=False, stop=True)
                    ins.then_inc(sem("rt_o"), 1)
                    pe.wait_ge(sem("at_ptc"), 2 * n + 1)
                    weighted(0)
                    pe.wait_ge(sem("rt_sq"), n + 1)
                    mm(bank(0), C("blk1", 128), rt("sq", T), start=True, stop=True).then_inc(sem("rt_var"), 1)
                    pe.wait_ge(sem("at_pn"), 2 * n + 2)
                    probs_t(1)
                    pe.wait_ge(sem("at_ptc"), 2 * n + 2)
                    weighted(1)
                pe.wait_ge(sem("at_y"), 2 * l + 2)
                gemm512(f0 + 64, c0 + 17, 0)
                gemm512(f0 + 68, c0 + 19, 4)
                gemm(f0 + 72, c0 + 21, 8, ready=sem("mix_lo"), value=8 * l + 16)
                mean_of_squares(2 * l + 1, "rms", lambda t: A(16, T, t * T))
                gemm(f0 + 80, c0 + 23, 44, ready=sem("rms_x"), value=8 * l + 8)
                gemm2816(f0 + 124, c0 + 34, l * FT + 2 * FT)

        @block.scalar
        def _(act):
            fn = nc.scalar.activation

            def hi(f, j):
                s = (j + LEAD) % 4
                act.wait_ge(w_loaded[s % 2], arrived(f, j + LEAD))
                act.wait_ge(fill_done, f + j + 1)
                fn(w_hi[:, s * FILL:(s + 1) * FILL], w_raw[:, (s % 2) * FILL:(s % 2 + 1) * FILL], ACT.Copy).then_inc(hi_ready, 1)

            def gemm(f, c, n, take=None):
                with act.Fori(0, n // 4) as i:
                    for j in range(4):
                        if take:
                            act.wait_ge(fill_done, f + 4 * i + j + 1)
                            take(i, j, chunk_out[j])
                        hi(f + 4 * i, j)

            def gemm512(f):
                for j in range(4):
                    hi(f, j)

            def gemm2816(f):
                with act.Fori(0, 2) as i:
                    for j in range(12):
                        hi(f + 12 * i, j)

            def ln_exp_tables():
                act.preload_act_table_set("natural_log_exp_and_others")

            def rstd(name, b, scale, eps, out_ap, done):
                fn(out_ap, bank(b), ACT.Ln, scale=scale, bias=C("eps", 1, eps))
                nc.scalar.drain()
                fn(out_ap, out_ap, ACT.Exp, scale=-0.5).then_inc(sem(done), 1)

            def norm_tail(n, name, eps):
                act.wait_ge(sem(name + "_var"), n + 1)
                rstd(name, 5, 1.0 / D, eps, A(34), name + "_rstd")

            def norm_hi(n, name):
                for q in range(4):
                    act.wait_ge(sem(name + "_u"), 4 * n + q + 1)
                    fn(XH[:, 2 * q * T:(2 * q + 2) * T], A(0, 2 * T, 2 * q * T), ACT.Copy).then_inc(sem(name + "_hi"), 1)

            def layer_norm(n, xc, sq):
                ln_exp_tables()
                for q in range(4):
                    act.wait_ge(sem("ln_xc"), 4 * n + q + 1)
                    fn(sq(2 * q), xc(2 * q), ACT.Square).then_inc(sem("ln_sq"), 1)
                norm_tail(n, "ln", 0)

            def ffn(f, c, n0):
                act.preload_act_table(ACT.Silu)
                with act.Fori(0, FT // 2) as i:
                    for j in range(4):
                        if j % 2 == 0:
                            act.wait_ge(fill_done, f + 4 * i + j + 1)
                            fn(A(88, T, j // 2 * T), bank(j), ACT.Silu).then_inc(chunk_out[j], 1)
                        else:
                            act.wait_ge(chunk_out[j], quarter(c) + i + 1)
                            fn(HH[:, bass.ds((2 * i + j // 2) * T, T)], A(105, T, j // 2 * T), ACT.Copy).then_inc(sem("ffn_hi"), 1)
                        hi(f + 4 * i, j)

            def all_out(c):
                for b in range(4):
                    act.wait_ge(chunk_out[b], quarter(c))

            def first_hi(f):
                act.wait_ge(w_loaded[f % 2], 16 * (f // 2) + 16)
                fn(w_hi[:, f * FILL:(f + 1) * FILL], w_raw[:, (f % 2) * FILL:(f % 2 + 1) * FILL], ACT.Copy).then_inc(hi_ready, 1)

            act.wait_ge(sem("const_in"), 48)
            fn(cond[:], P1("c", 0, 8), ACT.Silu).then_inc(sem("cond"), 1)
            act.wait_ge(sem("lb_max"), 1)
            fn(lbt[:, 8:24], lbt[:, 8:24], ACT.Exp).then_inc(sem("lb_exp"), 1)
            two = lambda kb: (lambda t: A(kb, 2 * T, t * T))
            first_hi(0)
            first_hi(1)
            layer_norm(0, two(0), two(16))
            first_hi(2)
            first_hi(3)
            norm_hi(0, "ln")
            def take_hgrn(i, j, done):
                kb, func = ((0, ACT.Silu), (16, ACT.Silu), (44, ACT.Sigmoid), (60, ACT.Copy))[j]
                fn(A(kb, T, i * T), bank(j), func).then_inc(done, 1)
            gemm(0, 0, 32, take_hgrn)
            ln_exp_tables()
            with act.Fori(0, HEADS) as h:
                act.wait_ge(sem("hg_f"), h + 1)
                fn(hg("lf", T), hg("lf", T), ACT.Ln).then_inc(sem("hg_lf"), 1)
                act.wait_ge(sem("hg_ex"), h + 1)
                fn(hg("qs", T), hg("qs", T), ACT.Exp)
                fn(hg("kdec", T), hg("kdec", T), ACT.Exp)
                fn(hg("e1", T), hg("cum", T), ACT.Exp).then_inc(sem("hg_exp"), 1)
                act.wait_ge(sem("hg_ks"), h + 1)
                ks = hg("ks", 2048).rearrange("p (c i s) -> p c i s", c=NCH, i=4)
                for s in range(4):
                    n = SUB * (s + 1)
                    ins = fn(ks[:, :, s, :n], ks[:, :, s, :n], ACT.Exp)
                ins.then_inc(sem("hg_kse"), 1)
                act.wait_ge(sem("hg_tr"), h + 1)
                fn(hg("kdec_t", T), bank(4), ACT.Copy)
                fn(hg("val_t", T), bank(5), ACT.Copy).then_inc(sem("hg_tm"), 1)
                act.wait_ge(sem("hg_o"), h + 1)
                fn(hg("sq", T), bank(5), ACT.Square).then_inc(sem("hg_sq"), 1)
                act.wait_ge(sem("hg_var"), h + 1)
                rstd("hg", 6, 1.0 / 128, 1, hg("rstd", T), "hg_rstd")
                act.wait_ge(sem("hg_out"), h + 1)
                fn(HH[:, bass.ds(h * T, T)], hg("o", T), ACT.Copy).then_inc(sem("hg_hi"), 1)
            act.wait_ge(sem("hg_y"), HEADS)
            act.dma_start(A(32, 8 * 128), dram["gm_ws"]).then_inc(sem("gm_in"), 16)
            act.dma_start(A(36, 8 * 128), dram["gm_bs"].broadcast_to([P, 8 * 128])).then_inc(sem("gm_in"), 16)
            def take_gmlp(i, j, done):
                fn(A(16 if j < 2 else 60, T, (2 * i + j % 2) * T), bank(j), ACT.Gelu).then_inc(done, 1)
            gemm(32, 32, 16, take_gmlp)
            ln_exp_tables()
            for q in range(4):
                act.wait_ge(sem("ln_xc"), 4 + q + 1)
                fn(A(76, 2 * T, 2 * q * T), A(60, 2 * T, 2 * q * T), ACT.Square).then_inc(sem("ln_sq"), 1)
            act.wait_ge(sem("ln_var"), 2)
            rstd("ln", 5, 1.0 / D, 0, A(105), "ln_rstd")
            with act.Fori(0, 8) as g:
                act.wait_ge(sem("gm_tr"), g + 1)
                fn(A(42), bank(4), ACT.Copy).then_inc(sem("gm_vt"), 1)
            act.wait_ge(sem("gm_u"), 8)
            gemm(48, 48, 8, lambda i, j, done: fn(A(60, T, (4 * i + j) * T), bank(j), ACT.Sigmoid, bias=P1("b_gate", 4 * i + j)).then_inc(done, 1))
            gemm(56, 56, 8)
            gemm(64, 64, 8, lambda i, j, done: fn(A(76, T, (4 * i + j) * T), bank(j), ACT.Sigmoid, bias=P1("b_gate", 4 * i + j + 8)).then_inc(done, 1))
            all_out(64)
            for q in range(4):
                fn(HH[:, 2 * q * T:(2 * q + 2) * T], A(16, 2 * T, 2 * q * T), ACT.Copy).then_inc(sem("gm_hi"), 1)
            def sum_hi(n0):
                def take(i, j):
                    act.wait_ge(sem("mix_sum"), n0 + 4 * i + j + 1)
                    fn(XH[:, bass.ds((4 * i + j) * T, T)], A(60, T, (4 * i + j) * T), ACT.Copy).then_inc(sem("mix_hi"), 1)
                return take
            take = sum_hi(0)
            with act.Fori(0, 2) as i:
                for j in range(4):
                    hi(72 + 4 * i, j)
                    take(i, j)
            gemm(80, 80, 8)
            layer_norm(2, two(0), two(16))
            layer_norm(3, two(0), two(16))
            norm_hi(1, "ln")
            ffn(88, 88, 0)
            gemm2816(132)
            layer_norm(4, two(0), two(16))
            act.wait_ge(sem("ln_h"), 12)

            with act.Fori(0, LAYERS) as l:
                f0, c0 = l * FILLS_L + FILLS_1, l * (CHUNKS_L // 4) + CHUNKS_1 // 4

                def rms_norm(k, c):
                    ln_exp_tables()
                    all_out(c)
                    for q in range(4):
                        fn(A(16, 2 * T, 2 * q * T), H[:, 2 * q * T:(2 * q + 2) * T], ACT.Square).then_inc(sem("rms_sq"), 1)
                    norm_tail(2 * l + k, "rms", 1)
                    norm_hi(2 * l + k, "rms")

                def take_at(kb):
                    return lambda i, j, done: fn(A(kb, T, (4 * i + j) * T), bank(j), ACT.Copy).then_inc(done, 1)

                rms_norm(0, c0)
                act.dma_start(A(88, 1024), dram["lora"][bass.ds(l, 1)].rearrange("a p n -> (a p) n")).then_inc(sem("lora_in"), 16)
                gemm(f0, c0, 16, take_at(12))
                act.wait_ge(sem("rw_mix"), 14 * l + 8)
                for p in range(PAIRS):
                    ins = fn(rp("rn", T, p * T), A(24, T, p * T), ACT.Square, scale=P2(l, "k_k", p))
                ins.then_inc(sem("rp_k2"), 1)
                act.wait_ge(sem("rw_mix"), 14 * l + 14)
                fn(A(16, T, 12 * T)[0:64], A(16, T, 12 * T)[0:64], ACT.Tanh)
                fn(A(16, T, 13 * T), A(16, T, 13 * T), ACT.Sigmoid).then_inc(sem("rw_act"), 1)
                act.wait_ge(sem("rp_mx"), l + 1)
                fn(rp("rn", 4 * T), rp("rn", 4 * T), ACT.Sqrt).then_inc(sem("rp_rn"), 1)
                for n in range(12):
                    act.wait_ge(sem("rw_lora"), 12 * l + n + 1)
                    if n < 4:
                        ins = fn(A(76, T, n * T), bank(n), ACT.Sigmoid, bias=P2(l, "w0", n))
                    elif n < 8:
                        ins = fn(A(44, T, (n - 4) * T), bank(n), ACT.Sigmoid, bias=P2(l, "a0", n - 4))
                    else:
                        ins = fn(A(52, T, (n - 8) * T), bank(n - 8), ACT.Copy)
                    ins.then_inc(sem("rw_lev"), 1)
                ln_exp_tables()
                with act.Fori(0, PAIRS) as p:
                    n = l * PAIRS + p + 1
                    act.wait_ge(sem("rp_cs"), n)
                    fn(rp("e", T), rp("cs", T), ACT.Exp, scale=-RWKV_DECAY)
                    fn(rp("ei", T), rp("cs", T), ACT.Exp, scale=RWKV_DECAY)
                    fn(rp("ex", T), rp("cx", T), ACT.Exp, scale=-RWKV_DECAY).then_inc(sem("rp_e"), 1)
                act.preload_act_table(ACT.Sigmoid)
                with act.Fori(0, NCH) as c:
                    n = l * NCH + c + 1

                    def take(j):
                        act.wait_ge(fill_done, f0 + 16 + 4 * c + j + 1)
                        fn(rc("spill", T, T * j), bank(j), ACT.Copy if j == 3 else ACT.Sigmoid).then_inc(chunk_out[j], 1)
                        hi(f0 + 16 + 4 * c, j)
                        act.wait_ge(chunk_out[j], c0 + 4 + c + 1)
                        act.dma_start(scratch[bass.ds(l * 32 + 8 * j + c, 1)].rearrange("a p n -> (a p) n"),
                                      rc("spill", T, T * j)).then_inc(spilled[j], 16)

                    act.wait_ge(sem("rc_tr"), n)
                    fn(rc("b_t", T), bank(5), ACT.Copy)
                    fn(rc("k_t", T), bank(6), ACT.Copy)
                    fn(rc("v_t", T), bank(7), ACT.Copy).then_inc(sem("rc_trc"), 1)
                    for v in range(1, 6):
                        act.wait_ge(sem("rc_p"), 5 * n - 5 + v)
                        fn(rc("p", T), bank(5), ACT.Copy).then_inc(sem("rc_pc"), 1)
                        if v in (2, 4):
                            take(v // 2 - 1)
                    take(2)
                    act.wait_ge(sem("rc_w"), n)
                    fn(rc("p", T), bank(5), ACT.Copy).then_inc(sem("rc_wc"), 1)
                    act.wait_ge(sem("rc_u"), n)
                    fn(rc("us", T), bank(6), ACT.Copy).then_inc(sem("rc_uc"), 1)
                    take(3)
                    act.wait_ge(sem("rc_y"), n)
                    fn(A(84, 4 * T).rearrange("p (a t) -> p a t", a=PAIRS)[:, :, bass.ds(c * CHUNK, CHUNK)],
                       chunks(bank(7, 256)), ACT.Copy).then_inc(sem("rc_yc"), 1)
                    for j in range(4):
                        act.wait_ge(spilled[j], 16 * n)

                def from_scratch(dst, tile, tiles, done):
                    act.dma_start(dst.rearrange("p (a n) -> p a n", n=T),
                                  scratch[bass.ds(l * 32 + tile, tiles)].rearrange("a p n -> p a n")).then_inc(sem(done), 16)

                act.wait_ge(sem("rc_y"), l * NCH + NCH)
                from_scratch(A(60, 8 * T), 8, 8, "gate_b_in")
                ln_exp_tables()
                two_pairs = lambda kb, h: A(kb, 2 * T, 2 * h * T)
                for h in range(2):
                    act.wait_ge(sem("ro_c"), 2 * l + h + 1)
                    fn(two_pairs(100, h), two_pairs(92, h), ACT.Square).then_inc(sem("ro_s"), 1)
                for h in range(2):
                    act.wait_ge(sem("ro_v"), 2 * l + h + 1)
                    fn(two_pairs(24, h), bank(2 * h, 2 * T), ACT.Ln, scale=1.0 / 64, bias=C("eps", 1, 2))
                    nc.scalar.drain()
                    fn(two_pairs(24, h), two_pairs(24, h), ACT.Exp, scale=-0.5).then_inc(sem("ro_r"), 1)
                for h in range(2):
                    act.wait_ge(sem("ro_y"), 2 * l + h + 1)
                    fn(HH[:, 2 * h * T:(2 * h + 2) * T], two_pairs(92, h), ACT.Copy).then_inc(sem("ro_h"), 1)
                act.wait_ge(sem("ro_l"), 2 * l + 2)
                act.dma_start(A(92, N_TABLE), dram["table"]).then_inc(sem("table_in"), 16)
                from_scratch(A(52, 4 * T), 24, 4, "aq_in")
                gemm512(f0 + 48)
                all_out(c0 + 14)
                from_scratch(A(60, 4 * T), 28, 4, "rq_in")
                gemm(f0 + 52, c0 + 14, 12, take_at(68))
                all_out(c0 + 17)
                fn(A(84, 4 * T), A(84, 4 * T), ACT.Silu)
                ln_exp_tables()
                act.wait_ge(sem("aq_in"), 16 * l + 16)
                fn(at("sq", T), A(12), ACT.Square).then_inc(sem("ak_sq"), 1)
                act.wait_ge(sem("ak_ss"), l + 1)
                rstd("ak", 4, 1.0 / 64, 1, at("rs", T), "ak_rs")
                act.wait_ge(sem("av_tr"), l + 1)
                fn(at("vt", T), bank(5), ACT.Copy)
                act.wait_ge(sem("ak_dup"), l + 1)
                fn(at("kd", 2 * T), bank(6, 2 * T), ACT.Copy).then_inc(sem("ak_kv"), 1)
                with act.Fori(0, PAIRS) as p:
                    n = l * PAIRS + p

                    def exps(hh):
                        act.wait_ge(sem("at_m"), 2 * n + hh + 1)
                        for b in range(NBLK):
                            fn(at("pb", 256, 256 * b), at("sc", 256, 256 * b), ACT.Exp, bias=small[:, b:b + 1], accum_out=small[:, 8 + b:9 + b])
                        fn(small[:, 16:20], small[:, 0:4], ACT.Exp, bias=P2(l, "sinks", 2 * p + hh)).then_inc(sem("at_p"), 1)

                    def probs_out(hh):
                        act.wait_ge(sem("at_pt"), 2 * n + hh + 1)
                        fn(at("pt", 896, 128), bank(6 - 2 * hh, 896, 128), ACT.Copy).then_inc(sem("at_ptc"), 1)

                    act.wait_ge(sem("at_in"), n + 1)
                    fn(at("sq", T), A(52, T, p * T), ACT.Square).then_inc(sem("at_sq"), 1)
                    act.wait_ge(sem("at_ss"), n + 1)
                    rstd("at", 7, 1.0 / 64, 1, at("rs", T), "at_rs")
                    act.wait_ge(sem("rt_tr"), n + 1)
                    fn(rt("kz_t", T), bank(2), ACT.Copy)
                    fn(rt("v_t", T), bank(3), ACT.Copy).then_inc(sem("rt_tm"), 1)
                    exps(0)
                    probs_out(0)
                    act.wait_ge(sem("rt_o"), n + 1)
                    fn(rt("sq", T), bank(2), ACT.Square).then_inc(sem("rt_sq"), 1)
                    exps(1)
                    act.wait_ge(sem("rt_var"), n + 1)
                    rstd("rt", 0, 1.0 / 64, 1, rt("rs", T), "rt_rs")
                    probs_out(1)
                    act.wait_ge(sem("at_o"), 2 * n + 2)
                    fn(small[:, 60:61], small[:, 60:61], ACT.Copy)
                    fn(A(52, T, p * T), bank(6), ACT.Copy).then_inc(sem("at_ao"), 1)
                act.wait_ge(sem("at_ao"), l * PAIRS + PAIRS)
                fn(HH[:, 0:4 * T], A(52, 4 * T), ACT.Copy).then_inc(sem("at_yh"), 1)
                act.wait_ge(sem("rt_done"), l * PAIRS + PAIRS)
                fn(HH[:, 4 * T:8 * T], A(60, 4 * T), ACT.Copy).then_inc(sem("at_yh"), 1)
                from_scratch(A(68, 8 * T), 0, 8, "gate_a_in")
                from_scratch(A(84, 8 * T), 16, 8, "gate_c_in")
                gemm512(f0 + 64)
                gemm512(f0 + 68)
                for j in range(8):
                    act.wait_ge(sem("mix_sum"), 16 * l + 16 + j + 1)
                    fn(XH[:, j * T:(j + 1) * T], A(16, T, j * T), ACT.Copy).then_inc(sem("mix_hi"), 1)
                gemm(f0 + 72, c0 + 21, 8)
                rms_norm(1, c0 + 23)
                ffn(f0 + 80, c0 + 23, l * FT + FT)
                gemm2816(f0 + 124)

        @block.vector
        def _(dve):
            tt, ts, stt, cp = nc.vector.tensor_tensor, nc.vector.tensor_scalar, nc.vector.scalar_tensor_tensor, nc.vector.tensor_copy

            def drain():
                nc.vector.drain()

            def lo(dst, src, hi_part):
                return tt(dst, src, hi_part.bitcast(F32), ALU.subtract)

            def all_out(c):
                for b in range(4):
                    dve.wait_ge(chunk_out[b], quarter(c))

            def norm_lo(n, name):
                for q in range(4):
                    dve.wait_ge(sem(name + "_hi"), 4 * n + q + 1)
                    s = slice(2 * q * T, (2 * q + 2) * T)
                    lo(XL[:, s], A(0, 2 * T, 2 * q * T), XH[:, s]).then_inc(sem(name + "_x"), 1)

            def layer_norm(n, src, xc, rs, scale, bias, dst, done):
                dve.wait_ge(sem("ln_sum"), n + 1)
                for q in range(4):
                    stt(chunks(xc(2 * q, 2), T), bc(bank(4), 2), -1.0 / D, chunks(src(2 * q, 2), T), ALU.mult, ALU.add).then_inc(sem("ln_xc"), 1)
                dve.wait_ge(sem("ln_rstd"), n + 1)
                for q in range(4):
                    tt(chunks(xc(2 * q, 2), T), chunks(xc(2 * q, 2), T), bc(rs, 2), ALU.mult)
                drain()
                for t in range(DT):
                    ins = ts(dst(t, 1), xc(t, 1), scale(t), bias(t), ALU.mult, ALU.add)
                    if t % 2:
                        ins.then_inc(sem(done), 1)

            def ffn(f, c, n0):
                with dve.Fori(0, FT // 2) as i:
                    for j in (1, 3):
                        k = j // 2
                        dve.wait_ge(chunk_out[j - 1], quarter(c) + i + 1)
                        dve.wait_ge(fill_done, f + 4 * i + j + 1)
                        tt(A(105, T, k * T), bank(j), A(88, T, k * T), ALU.mult).then_inc(chunk_out[j], 1)
                        dve.wait_ge(sem("ffn_hi"), n0 + 2 * i + k + 1)
                        at_ = bass.ds((2 * i + k) * T, T)
                        lo(HL[:, at_], A(105, T, k * T), HH[:, at_]).then_inc(sem("ffn_lo"), 1)

            def residual(f, c, n, step, scale=None):
                with dve.Fori(0, 2) as i:
                    for j in range(4):
                        dve.wait_ge(fill_done, f + step * (4 * i + j + 1))
                        h = H[:, bass.ds((4 * i + j) * T, T)]
                        if scale:
                            stt(h, bank(j), scale(4 * i + j), h, ALU.mult, ALU.add).then_inc(chunk_out[j], 1)
                        else:
                            tt(h, bank(j), h, ALU.add).then_inc(chunk_out[j], 1)

            def Ht(t, n):
                return H[:, t * T:(t + n) * T]

            def at_kb(kb):
                return lambda t, n: A(kb, n * T, t * T)

            nc.vector.memset(small[:], 0.0)
            dve.wait_ge(sem("const_in"), 48)
            tt(lbt[:, 0:8], P1("lb0", 0, 8), P1("lb1", 0, 8), ALU.max)
            drain()
            tt(lbt[:, 8:16], P1("lb0", 0, 8), lbt[:, 0:8], ALU.subtract)
            tt(lbt[:, 16:24], P1("lb1", 0, 8), lbt[:, 0:8], ALU.subtract).then_inc(sem("lb_max"), 1)
            dve.wait_ge(sem("lb_exp"), 1)
            tt(lbt[:, 0:8], lbt[:, 8:16], lbt[:, 16:24], ALU.add)
            drain()
            nc.vector.reciprocal(lbt[:, 24:32], lbt[:, 0:8])
            drain()
            tt(lbs[:, 0:8], lbt[:, 8:16], lbt[:, 24:32], ALU.mult)
            drain()
            ts(lbs[:, 8:16], lbs[:, 0:8], -1.0, 1.0, ALU.mult, ALU.add)
            dve.wait_ge(sem("ada_used"), 12)
            tt(mod[:], bank(6, 48), P1("b_ada", 0, 48), ALU.add)
            drain()
            for k in (8, 32):
                ts(mod[:, k:k + 8], mod[:, k:k + 8], 1.0, None, ALU.add)
            drain()
            layer_norm(0, Ht, at_kb(0), A(34), lambda t: mod[:, 8 + t:9 + t], lambda t: mod[:, t:t + 1], at_kb(0), "ln_u")
            norm_lo(0, "ln")
            ts(H[:], H[:], ALPHA, None, ALU.mult)
            nc.vector.memset(hg("ks", 2048), 0.0)
            nc.vector.memset(hg("state", 128), 0.0)
            nc.vector.memset(hg("st", 512), 0.0)
            all_out(32)
            with dve.Fori(0, HEADS) as h:
                drain()
                ts(hg("lf", T), A(44, T, h * T), lbs[:, bass.ds(h + 8, 1)], lbs[:, bass.ds(h, 1)], ALU.mult, ALU.add)
                drain()
                ts(hg("k", T), hg("lf", T), -1.0, 1.0, ALU.mult, ALU.add).then_inc(sem("hg_f"), 1)
                dve.wait_ge(sem("hg_lf"), h + 1)
                nc.vector.tensor_tensor_scan(hg("cum", T), C("chunk_start", T), hg("lf", T), 0.0, ALU.mult, ALU.add)
                drain()
                tt(hg("lf", T), hg("cum", T), hg("lf", T), ALU.subtract)
                drain()
                ref = chunks(hg("lf", T), SUB)[:, :, 0]
                tt(chunks(hg("qs", T), SUB), chunks(hg("cum", T), SUB), each(ref, SUB), ALU.subtract)
                last = chunks(hg("cum", T))[:, :, CHUNK - 1]
                tt(chunks(hg("kdec", T)), each(last, CHUNK), chunks(hg("cum", T)), ALU.subtract).then_inc(sem("hg_ex"), 1)
                ks = hg("ks", 2048).rearrange("p (c i s) -> p c i s", c=NCH, i=4)
                for s in range(4):
                    n = SUB * (s + 1)
                    ins = tt(ks[:, :, s, :n], each(chunks(hg("lf", T))[:, :, SUB * s], n), chunks(hg("cum", T))[:, :, :n], ALU.subtract)
                ins.then_inc(sem("hg_ks"), 1)
                dve.wait_ge(sem("hg_exp"), h + 1)
                q = A(0, T, h * T)
                tt(hg("qs", T), hg("qs", T), q, ALU.mult)
                tt(hg("qi", T), hg("e1", T), q, ALU.mult)
                tt(hg("kdec", T), hg("kdec", T), hg("k", T), ALU.mult)
                drain()
                cp(hg("val", T), A(60, T, h * T)).then_inc(sem("hg_q"), 1)
                dve.wait_ge(sem("hg_kse"), h + 1)
                kb = chunks(hg("k", T)).unsqueeze(2).broadcast_to([P, NCH, 4, CHUNK])
                tt(ks, ks, kb, ALU.mult).then_inc(sem("hg_k"), 1)
                dve.wait_ge(sem("hg_sc"), h + 1)
                for p0 in (0, 64):
                    r = slice(p0, p0 + 64)
                    ins = tt(chunks(hg("st", T), 128)[r, :, p0:p0 + 64], chunks(bank(6, 256))[r], bc(C("incl", 64)[r], 4), ALU.mult)
                ins.then_inc(sem("hg_st"), 1)
                dve.wait_ge(sem("hg_u"), h + 1)
                for c in range(NCH - 1):
                    e = hg("e1", T)[:, c * CHUNK + CHUNK - 1:c * CHUNK + CHUNK]
                    ins = stt(hg("state", 128, 128 * c + 128), hg("state", 128, 128 * c), e, bank(4 if c % 2 else 7, 128, 128 * (c // 2)), ALU.mult, ALU.add)
                    if c < NCH - 2:
                        drain()
                ins.then_inc(sem("hg_s"), 1)
                dve.wait_ge(sem("hg_rstd"), h + 1)
                tt(hg("o", T), bank(5), hg("rstd", T), ALU.mult)
                drain()
                stt(hg("o", T), hg("o", T), P1("hg_w"), A(16, T, h * T), ALU.mult, ALU.mult).then_inc(sem("hg_out"), 1)
                dve.wait_ge(sem("hg_hi"), h + 1)
                lo(HL[:, bass.ds(h * T, T)], hg("o", T), HH[:, bass.ds(h * T, T)]).then_inc(sem("hg_y"), 1)
            dve.wait_ge(sem("gm_in"), 32)
            nc.vector.memset(chunks(A(32, 1024), 128)[64:128, :, 0:64], 0.0).then_inc(sem("gm_mask"), 1)
            all_out(48)
            layer_norm(1, at_kb(60), at_kb(60), A(105), lambda t: P1("gm_w", t), lambda t: P1("gm_b", t), at_kb(60), "ln_h")
            with dve.Fori(0, 8) as g:
                drain()
                cp(A(40), A(60, T, g * T)).then_inc(sem("gm_vs"), 1)
                dve.wait_ge(sem("gm_sv"), g + 1)
                tt(chunks(A(40), 128), chunks(bank(5), 128), bc(A(36, 128, g * 128), 4), ALU.add)
                drain()
                tt(A(16, T, g * T), A(16, T, g * T), A(40), ALU.mult).then_inc(sem("gm_u"), 1)
            all_out(56)
            with dve.Fori(0, 2) as i:
                for j in range(4):
                    dve.wait_ge(fill_done, 56 + 4 * i + j + 1)
                    m = A(60, T, (4 * i + j) * T)
                    tt(m, bank(j), m, ALU.mult).then_inc(chunk_out[j], 1)
            for q in range(4):
                dve.wait_ge(sem("gm_hi"), q + 1)
                s = slice(2 * q * T, (2 * q + 2) * T)
                lo(HL[:, s], A(16, 2 * T, 2 * q * T), HH[:, s]).then_inc(sem("gm_lo"), 1)
            all_out(72)
            with dve.Fori(0, 2) as i:
                for j in range(4):
                    dve.wait_ge(fill_done, 72 + 4 * i + j + 1)
                    k = (4 * i + j) * T
                    tt(A(76, T, k), bank(j), A(76, T, k), ALU.mult).then_inc(chunk_out[j], 1)
                    drain()
                    tt(A(60, T, k), A(60, T, k), A(76, T, k), ALU.add).then_inc(sem("mix_sum"), 1)
                for j in range(4):
                    k = (4 * i + j) * T
                    dve.wait_ge(sem("mix_hi"), 4 * i + j + 1)
                    lo(XL[:, bass.ds(k, T)], A(60, T, k), XH[:, bass.ds(k, T)]).then_inc(sem("mix_lo"), 1)
            residual(80, 80, 8, 1, lambda c: mod[:, bass.ds(c + 16, 1)])
            drain()
            layer_norm(2, Ht, at_kb(0), A(34), lambda t: P1("ln1_w", t), lambda t: P1("ln1_b", t), Ht, "ln_h")
            layer_norm(3, Ht, at_kb(0), A(34), lambda t: mod[:, 32 + t:33 + t], lambda t: mod[:, 24 + t:25 + t], at_kb(0), "ln_u")
            norm_lo(1, "ln")
            ts(H[:], H[:], ALPHA, None, ALU.mult)
            ffn(88, 88, 0)
            residual(132, 132, 8, 3, lambda c: mod[:, bass.ds(c + 40, 1)])
            drain()
            layer_norm(4, Ht, at_kb(0), A(34), lambda t: P1("ln2_w", t), lambda t: P1("ln2_b", t), Ht, "ln_h")

            with dve.Fori(0, LAYERS) as l:
                f0, c0 = l * FILLS_L + FILLS_1, l * (CHUNKS_L // 4) + CHUNKS_1 // 4

                def rms_norm(k, name):
                    n = 2 * l + k
                    dve.wait_ge(sem("rms_rstd"), n + 1)
                    for t in range(DT):
                        ins = stt(A(0, T, t * T), Ht(t, 1), P2(l, name, t), A(34), ALU.mult, ALU.mult)
                        if t % 2:
                            ins.then_inc(sem("rms_u"), 1)
                    norm_lo(n, "rms")

                rms_norm(0, "norm1")
                def shift(t, j, done):
                    z, d = A(16, T, t * T), A(60, T, j * T)
                    dve.wait_ge(chunk_out[j], done)
                    tt(d[:, 1:T], z[:, 0:T - 1], z[:, 1:T], ALU.subtract)
                    ts(d[:, 0:1], z[:, 0:1], -1.0, None, ALU.mult)
                    drain()
                    stt(z, d, P2(l, "mu", t), z, ALU.mult, ALU.add).then_inc(sem("rw_mix"), 1)

                for j in (2, 3):
                    shift(j - 2, j, c0 + 1)
                with dve.Fori(0, 3) as i:
                    drain()
                    for j in range(4):
                        shift(4 * i + j + 2, j, c0 + i + 2)
                dve.wait_ge(sem("rp_ss"), l + 1)
                ts(rp("rn", 4 * T), bank(4, 4 * T), 1e-24, None, ALU.max).then_inc(sem("rp_mx"), 1)
                dve.wait_ge(sem("rp_rn"), l + 1)
                nc.vector.reciprocal(rp("rn", 4 * T), rp("rn", 4 * T))
                with dve.Fori(0, PAIRS) as p:
                    n = l * PAIRS + p + 1
                    R, K, V = A(16, T, p * T), A(24, T, p * T), A(32, T, p * T)
                    SG, AA = A(76, T, p * T), A(44, T, p * T)
                    drain()
                    dve.wait_ge(sem("rw_lev"), 12 * l + 12)
                    nc.vector.tensor_tensor_scan(rp("cs", T), C("chunk_start", T), SG, 0.0, ALU.mult, ALU.add)
                    drain()
                    tt(rp("cx", T), rp("cs", T), SG, ALU.subtract).then_inc(sem("rp_cs"), 1)
                    stt(rp("kk", T), K, P2(l, "k_k", p), A(0, T, p * T), ALU.mult, ALU.mult)
                    drain()
                    tt(rp("kb", T), rp("kk", T), AA, ALU.mult)
                    ts(AA, AA, -1.0, P2(l, "k_a", p), ALU.add, ALU.mult)
                    drain()
                    stt(AA, AA, 1.0, K, ALU.add, ALU.mult)
                    drain()
                    stt(rp("rk", T), R, P2(l, "r_k", p), AA, ALU.mult, ALU.mult).then_inc(sem("rp_rk"), 1)
                    ar = A(60, 2 * T, p * 2 * T).rearrange("p (c k t) -> p c k t", c=NCH, k=2)
                    dve.wait_ge(sem("rp_e"), n)
                    stt(ar[:, :, 0, :], chunks(rp("kk", T)), -1.0, chunks(rp("ex", T)), ALU.mult, ALU.mult)
                    tt(ar[:, :, 1, :], chunks(R), chunks(rp("e", T)), ALU.mult)
                    cp(rc("el", 8, 8 * p), chunks(rp("e", T))[:, :, CHUNK - 1])
                    tt(SG, rp("kb", T), rp("ei", T), ALU.mult)
                    tt(K, AA, rp("ei", T), ALU.mult)
                    drain()
                    dve.wait_ge(sem("rp_bn"), n)
                    tt(R, bank(5), V, ALU.mult).then_inc(sem("rp_done"), 1)
                nc.vector.memset(rc("state", 512), 0.0).then_inc(sem("rc_st"), 1)
                with dve.Fori(0, NCH) as c:
                    n = l * NCH + c + 1

                    def level(dst, b, mask):
                        return tt(chunks(dst), chunks(bank(b)), bc(mask, 2 * PAIRS), ALU.mult)

                    def plus_identity(name):
                        return tt(chunks(rc(name, 512), 128), chunks(rc(name, 512), 128), bc(C("ident", 128), PAIRS), ALU.add)

                    dve.wait_ge(sem("rc_s1"), n)
                    level(rc("t", 512), 5, C("lower0", 64))
                    level(rc("ak", 512), 6, C("upper", 64))
                    dve.wait_ge(sem("rc_s2"), n)
                    level(rc("u", 512), 4, C("level", 64))
                    level(rc("rbk", 512), 7, C("incl", 64)).then_inc(sem("rc_out"), 1)
                    level(rc("al1", 512), 4, C("level", 64, 64))
                    drain()
                    plus_identity("u")
                    plus_identity("t").then_inc(sem("rc_al"), 1)
                    for v in range(1, 6):
                        if v < 5:
                            level(rc(f"al{(v + 1) % 2}", 512), 4, C("level", 64, 64 * (v + 1)))
                            dve.wait_ge(sem("rc_d"), 4 * n - 4 + v)
                            tt(rc("t", 512), rc("t", 512), bank(6), ALU.add).then_inc(sem("rc_al"), 1)
                        dve.wait_ge(sem("rc_e"), 5 * n - 5 + v)
                        tt(rc("u", 512), rc("u", 512), bank(7), ALU.add).then_inc(sem("rc_uu"), 1)
                    dve.wait_ge(sem("rc_n"), n)
                    tt(rc("state", 512), rc("state", 512), bank(4), ALU.add)
                    drain()
                    dve.wait_ge(sem("rc_yc"), n)
                    el = chunks(rc("el", 32), 8)[:, :, bass.ds(c, 1)].broadcast_to([P, PAIRS, 128])
                    tt(chunks(rc("state", 512), 128), chunks(rc("state", 512), 128), el, ALU.mult).then_inc(sem("rc_st"), 1)
                two_pairs = lambda kb, h: A(kb, 2 * T, 2 * h * T)
                for h in range(2):
                    dve.wait_ge(sem("ro_m"), 2 * l + h + 1)
                    stt(two_pairs(92, h), bank(4 + 2 * h, 2 * T), -1.0 / 64, two_pairs(84, h), ALU.mult, ALU.add).then_inc(sem("ro_c"), 1)
                for h in range(2):
                    y = two_pairs(92, h)
                    dve.wait_ge(sem("ro_r"), 2 * l + h + 1)
                    tt(y, y, two_pairs(24, h), ALU.mult)
                    drain()
                    for p in (2 * h, 2 * h + 1):
                        ts(A(92, T, p * T), A(92, T, p * T), P2(l, "ln_g", p), P2(l, "ln_b", p), ALU.mult, ALU.add)
                    drain()
                    tt(y, y, two_pairs(16, h), ALU.add)
                    drain()
                    tt(y, y, two_pairs(52, h), ALU.mult).then_inc(sem("ro_y"), 1)
                for h in range(2):
                    dve.wait_ge(sem("ro_h"), 2 * l + h + 1)
                    s = slice(2 * h * T, (2 * h + 2) * T)
                    lo(HL[:, s], two_pairs(92, h), HH[:, s]).then_inc(sem("ro_l"), 1)

                def gated(f, c, gate, first, h0):
                    for j in range(8):
                        if j % 2:
                            dve.wait_ge(fill_done, f + j // 2 + 1)
                        else:
                            dve.wait_ge(half_done, l * 12 + h0 + j // 2 + 1)
                        m, g = A(16, T, j * T), A(gate, T, j * T)
                        if first:
                            tt(m, bank(j % 4), g, ALU.mult).then_inc(chunk_out[j % 4], 1)
                        else:
                            tt(g, bank(j % 4), g, ALU.mult).then_inc(chunk_out[j % 4], 1)
                            drain()
                            tt(m, m, g, ALU.add).then_inc(sem("mix_sum"), 1)

                dve.wait_ge(sem("ro_h"), 2 * l + 2)
                dve.wait_ge(sem("gate_b_in"), 16 * l + 16)
                gated(f0 + 48, c0 + 12, 60, True, 0)
                all_out(c0 + 17)
                dve.wait_ge(sem("ak_rs"), l + 1)
                stt(at("kn", T), A(12), P2(l, "kg"), at("rs", T), ALU.mult, ALU.mult).then_inc(sem("ak_n"), 1)
                nc.vector.memset(at("sc", 128), MASKED)
                nc.vector.memset(rt("state", 128), 0.0)
                with dve.Fori(0, 2) as j:
                    with dve.Fori(0, 2) as i:
                        n = l * PAIRS + 2 * j + i
                        p = 2 * j + i

                        def scores(hh):
                            dve.wait_ge(sem("at_sc"), 2 * n + hh + 1)
                            stt(at("sc", 128, 128), bank(4, 128, 128), 0.125, C("band", 128, 128), ALU.mult, ALU.add)
                            stt(chunks(at("sc", 768, 256), 256), chunks(bank(4, 768, 256), 256), 0.125, bc(C("band", 256), 3), ALU.mult, ALU.add)
                            drain()
                            nc.vector.reduce_max(small[:, 24:28], chunks(at("sc", 1024), 256), AX.X)
                            drain()
                            ts(small[:, 0:4], small[:, 24:28], P2(l, "sinks", 2 * p + hh), -1.0, ALU.max, ALU.mult).then_inc(sem("at_m"), 1)

                        def normalise(hh):
                            dve.wait_ge(sem("at_p"), 2 * n + hh + 1)
                            tt(small[:, 32:36], small[:, 8:12], small[:, 16:20], ALU.add)
                            drain()
                            nc.vector.reciprocal(small[:, 36:40], small[:, 32:36])
                            drain()
                            pb = chunks(at("pb", 1024), 256)
                            tt(pb, pb, each(small[:, 36:40], 256), ALU.mult).then_inc(sem("at_pn"), 1)

                        q, k = A(60, T, p * T), A(68, T, p * T)
                        drain()
                        dve.wait_ge(sem("ak_kv"), l + 1)
                        dve.wait_ge(sem("table_in"), 16 * l + 16)
                        dve.wait_ge(sem("rq_in"), 16 * l + 16)
                        cp(at("kj", T), at("kd", T, j * T))
                        cp(chunks(at("vj", 256)), chunks(at("vt", T), 128)[:, :, bass.ds(64 * j, 64)]).then_inc(sem("at_in"), 1)
                        cp(rt("vs", T), A(76, T, p * T)).then_inc(sem("rt_in"), 1)
                        tt(rt("qr", T), q, TB("cos", T), ALU.mult)
                        stt(rt("kr", T), k, 0.125, TB("cos", T), ALU.mult, ALU.mult)
                        dve.wait_ge(sem("at_rs"), n + 1)
                        stt(at("qs", T), A(52, T, p * T), P2(l, "qg"), at("rs", T), ALU.mult, ALU.mult).then_inc(sem("at_q"), 1)
                        dve.wait_ge(sem("rt_rot"), n + 1)
                        tt(rt("t1", T), bank(0), TB("sin", T), ALU.mult)
                        stt(rt("t2", T), bank(1), 0.125, TB("sin", T), ALU.mult, ALU.mult)
                        drain()
                        tt(rt("qr", T), rt("qr", T), rt("t1", T), ALU.add)
                        tt(rt("kr", T), rt("kr", T), rt("t2", T), ALU.add)
                        drain()
                        tt(chunks(rt("qx", T), 128), chunks(rt("qr", T), 128), bc(TB("xi", 128, 128 * p), 4), ALU.mult)
                        tt(chunks(rt("kz", T), 128), chunks(rt("kr", T), 128), bc(TB("zeta", 128, 128 * p), 4), ALU.mult).then_inc(sem("rt_qk"), 1)
                        scores(0)
                        dve.wait_ge(sem("rt_sc"), n + 1)
                        for hh in range(2):
                            tt(chunks(rt("st", T, T * hh), 128), chunks(bank(hh), 128), bc(TB("dmat", 128, 128 * (2 * p + hh)), 4), ALU.mult)
                        dve.wait_ge(sem("rt_kv"), n + 1)
                        tt(chunks(rt("t1", 384), 128), chunks(bank(3, 384), 128), bc(C("blk1", 128), 3), ALU.mult)
                        drain()
                        for b in range(NBLK - 1):
                            ins = stt(rt("state", 128, 128 * b + 128), rt("state", 128, 128 * b), C("cd", 1, p), rt("t1", 128, 128 * b), ALU.mult, ALU.add)
                            if b < NBLK - 2:
                                drain()
                        ins.then_inc(sem("rt_r"), 1)
                        normalise(0)
                        scores(1)
                        dve.wait_ge(sem("rt_rs"), n + 1)
                        tt(rt("t2", T), bank(2), rt("rs", T), ALU.mult)
                        drain()
                        tt(q, rt("t2", T), A(84, T, p * T), ALU.mult).then_inc(sem("rt_done"), 1)
                        normalise(1)
                        dve.wait_ge(sem("at_o"), 2 * n + 2)
                dve.wait_ge(sem("at_ao"), l * PAIRS + PAIRS)
                dve.wait_ge(sem("at_yh"), 2 * l + 1)
                lo(HL[:, 0:4 * T], A(52, 4 * T), HH[:, 0:4 * T]).then_inc(sem("at_y"), 1)
                drain()
                dve.wait_ge(sem("at_yh"), 2 * l + 2)
                lo(HL[:, 4 * T:8 * T], A(60, 4 * T), HH[:, 4 * T:8 * T]).then_inc(sem("at_y"), 1)
                dve.wait_ge(sem("gate_a_in"), 16 * l + 16)
                gated(f0 + 64, c0 + 17, 68, False, 4)
                dve.wait_ge(sem("gate_c_in"), 16 * l + 16)
                gated(f0 + 68, c0 + 19, 84, False, 8)
                for j in range(8):
                    dve.wait_ge(sem("mix_hi"), 8 * l + 8 + j + 1)
                    lo(XL[:, j * T:(j + 1) * T], A(16, T, j * T), XH[:, j * T:(j + 1) * T]).then_inc(sem("mix_lo"), 1)
                residual(f0 + 72, c0 + 21, 8, 1)
                rms_norm(1, "norm2")
                ffn(f0 + 80, c0 + 23, l * FT + FT)
                residual(f0 + 124, c0 + 34, 8, 3)


def columns_of(v):
    return v.reshape(-1, P).T


def shape_constants():
    con = np.zeros((P, N_CONST), np.float32)

    def put(name, a):
        con[:, CONST[name]:CONST[name] + a.shape[1]] = a

    r = np.arange(P)
    half, i64 = r % 64, np.arange(64)
    put("ident", np.eye(P))
    put("ones", np.ones((P, P)))
    put("blk1", (r[:, None] // 64 == r[None, :] // 64))
    put("chunk_start", np.broadcast_to(np.arange(T)[None] % CHUNK != 0, (P, T)))
    put("upper", half[:, None] < i64[None])
    put("incl", half[:, None] <= i64[None])
    put("lower0", (half[:, None] // 2 == i64[None] // 2) & (half[:, None] % 2 == 1) & (i64[None] % 2 == 0))
    levels = [(half[:, None] // (2 * b) == i64[None] // (2 * b)) & (half[:, None] // b % 2 == 0) & (i64[None] // b % 2 == 1)
              for b in (1, 2, 4, 8, 16, 32)]
    put("level", np.concatenate(levels, axis=1))
    key = np.arange(2 * BLK)
    seen = (key[None] > r[:, None]) & (key[None] <= r[:, None] + BLK)
    put("band", np.where(seen, 0.0, MASKED))
    put("dup", np.concatenate([r[:, None] == 64 * j + half[None] for j in range(2)], axis=1))
    put("eps", np.broadcast_to(np.float32([[1e-5, 1e-6, 64e-5, 0.0]]), (P, 4)))

    table = np.zeros((P, N_TABLE), np.float32)

    def put_t(name, a):
        table[:, TABLE[name]:TABLE[name] + a.shape[1]] = a

    inv = np.float32(1.0) / np.power(np.float32(10000.0), np.arange(32, dtype=np.float32) * np.float32(2.0) / np.float32(64))
    angle = np.arange(T, dtype=np.float32)[None] * inv[r % 32][:, None].astype(np.float32)
    put_t("cos", np.cos(angle))
    put_t("sin", np.sin(angle))
    lg = np.log1p(-np.power(2.0, -5.0 - np.arange(HEADS)))
    pos = np.arange(BLK)
    diff = pos[None] - pos[:, None]
    put_t("dmat", np.concatenate([np.where(diff >= 0, np.exp(g * np.maximum(diff, 0)), 0.0) for g in lg], axis=1))
    of = lambda p: lg[2 * p + r // 64][:, None]
    put_t("xi", np.concatenate([np.exp(of(p) * (pos[None] + 1.0)) for p in range(PAIRS)], axis=1))
    put_t("zeta", np.concatenate([np.exp(of(p) * (BLK - 1.0 - pos[None])) for p in range(PAIRS)], axis=1))
    put("cd", np.concatenate([np.exp(of(p) * BLK) for p in range(PAIRS)], axis=1))
    rot = np.zeros((P, P))
    for m in range(P):
        rot[m + 32 if m % 64 < 32 else m - 32, m] = -1.0 if m % 64 < 32 else 1.0
    put_t("rot", rot)
    return con, table


def kernel(**inputs):
    import concourse.bacc as bacc
    from concourse.bass_utils import run_bass_kernel_spmd

    a = {k: np.asarray(v) for k, v in inputs.items()}

    def fills_of(w):
        k, n = w.shape
        t = w.reshape(k // P, P, n // P, P).transpose(2, 1, 0, 3)
        if k == D:
            return t.reshape(n // P, P, 8 * P)
        if k == D // 2:
            return t.reshape(n // P // 2, 2, P, 4 * P).transpose(0, 2, 1, 3).reshape(n // P // 2, P, 8 * P)
        t = np.pad(t, ((0, 0), (0, 0), (0, 24 - k // P), (0, 0)))
        return t.reshape(n // P, P, 3, 8 * P).transpose(0, 2, 1, 3).reshape(n // P * 3, P, 8 * P)

    def turns(parts, order):
        out, at = [], [0] * len(parts)
        while at[0] < len(parts[0]):
            for k, m in enumerate(order):
                out.append(parts[k][at[k]:at[k] + m])
                at[k] += m
        return np.concatenate(out)

    w_in = fills_of(a["w_in"][0])
    zq, zf, zi, zg, zu, zv, ga, gb = (w_in[8 * k:8 * k + 8] for k in range(8))
    ffn = fills_of(a["w_ffn_in"][0])
    fills = [turns([zq, zg, zf, zi], [1, 1, 1, 1]), turns([zu, zv], [2, 2]), ga, fills_of(a["w_proj_a"][0]), gb,
             fills_of(a["w_proj_b"][0]), fills_of(a["w_out"][0]), turns([ffn[:FT], ffn[FT:]], [1, 1]), fills_of(a["w_ffn_out"][0])]
    for l in range(LAYERS):
        w = fills_of(a["w_in_2"][l])
        aq, ak, av, rw, ret = w[0:4], w[4:5], w[5:6], w[6:20], w[20:36]
        gates = [w[36 + 8 * k:44 + 8 * k] for k in range(3)]
        gated = turns([gates[0], gates[1], gates[2], np.concatenate([aq, ret[:4]])], [1, 1, 1, 1])
        fills += [ak, av, rw, gated, fills_of(a["w_rwkv_o_2"][l]), ret[4:], fills_of(a["w_attn_o_2"][l]),
                  fills_of(a["w_ret_o_2"][l]), fills_of(a["w_out_2"][l]),
                  turns([fills_of(a["w_ffn_gate_2"][l]), fills_of(a["w_ffn_up_2"][l])], [1, 1]), fills_of(a["w_ffn_down_2"][l])]
    fills.append(np.zeros((LEAD, P, 8 * P), np.float32))
    fills = np.concatenate(fills)
    assert fills.shape[0] == FILLS

    con, table = shape_constants()
    ln = lambda name: columns_of(a[name][0])
    par1 = np.concatenate([columns_of(a["c"][0]), ln("b_ada"), columns_of(a["hgrn_lb_logits"][0]), columns_of(a["hgrn_lb_logits"][1]),
                           ln("hgrn_norm_w"), ln("gmlp_ln_w"), ln("gmlp_ln_b"), columns_of(a["b_gate"][0].reshape(-1)),
                           ln("ln1_w"), ln("ln1_b"), ln("ln2_w"), ln("ln2_b")], axis=1)
    twice = lambda v: np.concatenate([v, v])[:, None]
    par2 = np.concatenate([np.concatenate(
        [columns_of(a["norm1_g_2"][l]), columns_of(a["norm2_g_2"][l]), twice(a["attn_q_norm_g_2"][l]), twice(a["attn_k_norm_g_2"][l]),
         np.broadcast_to(a["attn_sinks_2"][l][None], (P, HEADS)), columns_of(a["rwkv_shift_mu_2"][l])]
        + [columns_of(a[f"rwkv_{n}_2"][l].reshape(-1)) for n in ("w0", "a0", "k_k", "k_a", "r_k", "lnx_g", "lnx_b")], axis=1)
        for l in range(LAYERS)], axis=1)
    arrays = {
        "x": a["x"][0].reshape(T, DT, P).transpose(2, 1, 0).reshape(P, DT * T),
        "w_ada": a["w_ada"][0].reshape(DT, P, 12, 4, P).transpose(2, 1, 3, 0, 4).reshape(12, P, 16 * KB),
        "fills": fills, "con": con, "table": table, "par1": par1, "par2": par2,
        "gm_ws": a["gmlp_ws"][0].transpose(2, 0, 1).reshape(P, 8 * P),
        "gm_bs": a["gmlp_bs"][0].reshape(1, 8 * P),
        "lora": np.concatenate([np.concatenate([a["rwkv_w2_2"], a["rwkv_a2_2"]], axis=1), a["rwkv_g2_2"]], axis=2),
    }
    arrays = {k: np.ascontiguousarray(v) for k, v in arrays.items()}
    nc = bacc.Bacc("TRN2", target_bir_lowering=False, num_devices=1)
    dram = {k: nc.dram_tensor("in_" + k, v.shape, F32, kind="ExternalInput").ap() for k, v in arrays.items()}
    out = nc.dram_tensor("out", (P, DT * T), F32, kind="ExternalOutput").ap()
    scratch = nc.dram_tensor("scratch", (LAYERS * 32, P, T), F32, kind="Internal").ap()
    build(nc, dram, out, scratch)
    r = run_bass_kernel_spmd(nc, [{"in_" + k: v for k, v in arrays.items()}], core_ids=[0])
    got = np.asarray(r.results[0]["out"])
    return np.ascontiguousarray(got.reshape(P, DT, T).transpose(2, 1, 0).reshape(1, T, D))
```

```python
from contextlib import ExitStack

import numpy as np
import concourse.bass as bass
from concourse import mybir

F32, F32R = mybir.dt.float32, mybir.dt.float32r
ALU, ACT, AX = mybir.AluOpType, mybir.ActivationFunctionType, mybir.AxisListType

P = 128
T = 512
D = 1024
DT = D // P
FF = 2816
FT = FF // P
LAYERS = 2
HEADS = 8
CHUNK = 64
NCH = T // CHUNK
SUB = 16
BLK = 128
NBLK = T // BLK
PAIRS = 4
ALPHA = 2.0 ** 0.25
RWKV_DECAY = float(np.exp(np.float32(-0.5)))
KB = 256

FILLS_1 = 32 + 16 + 4 * 8 + 8 + 44 + 24
FILLS_L = 16 + 32 + 4 + 12 + 4 + 4 + 8 + 44 + 24
LEAD = 4
FILLS = FILLS_1 + LAYERS * FILLS_L + LEAD
SQ_KB, ACC_KB = 88, 90
FILLS_HG = 34
ORDER = "FFAAAAFFAAAA"
FILL_AT = [k for k, x in enumerate(ORDER) if x == "F"]
ADA_AT = [k for k, x in enumerate(ORDER) if x == "A"]
ADA_FIRST = 16
ADA_LATER = 32
CHUNKS_1 = 32 + 16 + 4 * 8 + 8 + 44 + 8
CHUNKS_L = 16 + 32 + 8 + 12 + 8 + 8 + 8 + 44 + 8

def columns(sizes):
    at, out = 0, {}
    for name, n in sizes:
        out[name] = at
        at += n
    return out, at

CONST, N_CONST = columns([("ident", 128), ("ones", 128), ("blk1", 128), ("chunk_start", T), ("upper", 64), ("incl", 64),
                          ("lower0", 64), ("level", 6 * 64), ("eye64", 64), ("band", 256),
                          ("dup", 256), ("cd", 4), ("eps", 4)])
TABLE, N_TABLE = columns([("cos", T), ("sin", T), ("dmat", 8 * 128), ("xi", 4 * 128), ("zeta", 4 * 128), ("rot", 128)])
PAR1, N_PAR1 = columns([("c", 8), ("b_ada", 48), ("lb0", 8), ("lb1", 8), ("hg_w", 1), ("gm_w", 8), ("gm_b", 8),
                        ("b_gate", 16), ("ln1_w", 8), ("ln1_b", 8), ("ln2_w", 8), ("ln2_b", 8)])
PAR2, N_PAR2 = columns([("norm1", 8), ("norm2", 8), ("qg", 1), ("kg", 1), ("sinks", 8), ("mu", 14), ("w0", 4), ("a0", 4),
                        ("k_k", 4), ("k_a", 4), ("r_k", 4), ("ln_g", 4), ("ln_b", 4)])
MASKED = -1.0e30

HG = {"ks": 76, "state": 84, "val_t": 88, "kdec_t": 90, "k": 32, "lf": 34, "cum": 36, "qs": 38, "e1": 40, "qi": 42,
      "kdec": 104.5, "st": 106.5, "val": 34, "o": 38, "sq": 32, "rstd": 36}
RP = {"rn": 0, "kk": 8, "kb": 10, "cs": 40, "cx": 42, "ei": 84, "ex": 86, "e": 92, "rk": 94}
RC = {"a": 0, "b": 2, "k": 4, "v": 6, "ak": 8, "b_t": 10, "k_t": 40, "v_t": 42, "u": 44, "t_c": 46, "u_c": 47, "p": 48, "us": 50,
      "state": 92, "al": 94, "state_c": 96, "p_c": 97, "rbk": 98, "el": 100, "spill": 101, "us_c": 107, "v_c": 108}
AT = {"sq": 0, "rs": 2, "kn": 4, "vt": 6, "kd": 8, "sc": 40, "pb": 44, "pt": 48, "kj": 104.5, "qs": 106.5, "vj": 108.5}
RT = {"qr": 0, "kr": 2, "qx": 4, "kz": 6, "vs": 8, "t1": 10, "t2": 12, "rs": 14, "kz_t": 16, "v_t": 18, "st": 20, "state": 24, "sq": 26}
ARENA_KB = 109.5


def build(nc, dram, out, scratch):
    ctx = ExitStack()
    with ctx:
        def sb(name, cols, dt=F32):
            return ctx.enter_context(nc.sbuf_tensor(name, [P, cols], dt))

        sems = {}

        def sem(name):
            if name not in sems:
                sems[name] = ctx.enter_context(nc.semaphore(name))
            return sems[name]

        FILL = 8 * 128
        w_raw = sb("w_raw", 2 * FILL)
        w_hi = sb("w_hi", 4 * FILL, F32R)
        w_lo = sb("w_lo", 4 * FILL, F32R)
        H = sb("H", DT * T)
        x_at = nc.sbuf_base
        XH = sb("XH", DT * T, F32R)
        XL = sb("XL", DT * T, F32R)
        con = sb("con", N_CONST)
        par1 = sb("par1", N_PAR1)
        par2 = sb("par2", LAYERS * N_PAR2)
        mod = sb("mod", 48)
        cond = sb("cond", 8)
        lbs = sb("lbs", 16)
        lbt = sb("lbt", 32)
        small = sb("small", 64)
        arena = sb("arena", int(ARENA_KB * KB))
        arena_at = nc.sbuf_base - int(ARENA_KB * KB) * 4
        HH = nc.alloc_sbuf_tensor_at("HH", [P, FT * T], F32R, offset=arena_at)
        HL = nc.alloc_sbuf_tensor_at("HL", [P, FT * T], F32R, offset=arena_at + 4 * FT * T)
        X32 = nc.alloc_sbuf_tensor_at("X32", [P, 2 * DT * T], F32, offset=x_at)
        psum = ctx.enter_context(nc.psum_tensor("psum", [P, 8 * 512], F32))

        def A(kb, n=T, at=0):
            lo = int(kb * KB)
            if isinstance(at, int):
                return arena[:, lo + at:lo + at + n]
            return arena[:, bass.ds(lo + at, n)]

        def tile(t, n, at):
            return t[:, at:at + n] if isinstance(at, int) else t[:, bass.ds(at, n)]

        def C(name, n, at=0):
            return tile(con, n, CONST[name] + at)

        def TB(name, n, at=0):
            return A(92, n, TABLE[name] + at)

        def P1(name, at=0, n=1):
            return tile(par1, n, PAR1[name] + at)

        def P2(l, name, at=0, n=1):
            return tile(par2, n, l * N_PAR2 + PAR2[name] + at)

        def bank(b, n=512, at=0):
            return psum[:, 512 * b + at:512 * b + at + n]

        def region(table):
            return lambda name, n, at=0: A(table[name], n, at)

        hg, rp, rc, at = (region(table) for table in (HG, RP, RC, AT))

        def rt(name, n, at=0):
            lo = RT[name] * KB + at
            return X32[:, lo:lo + n]

        def chunks(ap, c=CHUNK):
            return ap.rearrange("p (a c) -> p a c", c=c)

        def bc(ap, n):
            return ap.unsqueeze(1).broadcast_to([ap.shape[0], n, ap.shape[1]])

        def each(ap, n):
            return ap.unsqueeze(2).broadcast_to([ap.shape[0], ap.shape[1], n])

        w_loaded = [sem(f"w_loaded{s}") for s in range(2)]
        hi_ready = sem("hi_ready")
        lo_ready = sem("lo_ready")
        fill_done = sem("fill_done")
        half_done = sem("half_done")
        chunk_out = [sem(f"chunk_out{b}") for b in range(4)]

        spilled = [sem(f"spilled{j}") for j in range(4)]

        def quarter(c):
            return c // 4 if isinstance(c, int) else c

        def arrived(r, k):
            return 8 * r + 16 * (k // 2) + 16

        block = ctx.enter_context(nc.Block())

        @block.sync
        def _(sp):
            sp.dma_start(con[:], dram["con"]).then_inc(sem("const_in"), 16)
            sp.dma_start(par1[:], dram["par1"]).then_inc(sem("const_in"), 16)
            sp.dma_start(par2[:], dram["par2"]).then_inc(sem("const_in"), 16)
            sp.dma_start(H[:], dram["x"]).then_inc(sem("x_in"), 16)
            for k in range(4):
                sp.dma_start(A(40 + 16 * k, 16 * KB), dram["w_ada"][k]).then_inc(sem(f"ada_in{min(k, 1)}"), 16)
            for f in range(2):
                sp.dma_start(w_raw[:, f * FILL:(f + 1) * FILL], dram["fills"][f]).then_inc(w_loaded[f], 16)
            def entry(r, s):
                sp.dma_start(w_raw[:, s * FILL:(s + 1) * FILL],
                             dram["fills"][bass.ds(r, 1)].rearrange("a p n -> (a p) n")).then_inc(w_loaded[s], 16)

            with sp.Fori(0, FILLS_HG // 2) as i:
                for s in range(2):
                    sp.wait_ge(lo_ready, 2 * i + s + 1)
                    entry(2 * i + s + 2, s)
            with sp.Fori(0, HEADS // 2) as i:
                for k in range(12):
                    if k in FILL_AT:
                        sp.wait_ge(lo_ready, FILLS_HG + 4 * i + FILL_AT.index(k) + 1)
                    else:
                        sp.wait_ge(sem("ada_done"), 8 * i + ADA_AT.index(k) + 1)
                    entry(FILLS_HG + 2 + 12 * i + k, k % 2)
            after = FILLS_HG + 4 * HEADS // 2
            with sp.Fori(0, (FILLS - after) // 2 - 1) as i:
                for s in range(2):
                    sp.wait_ge(lo_ready, after + 2 * i + s + 1)
                    entry(after + ADA_LATER + 2 * i + s + 2, s)
            for b in range(4):
                sp.wait_ge(chunk_out[b], (CHUNKS_1 + LAYERS * CHUNKS_L) // 4)
            sp.dma_start(out, H[:]).then_inc(sem("stored"), 16)
            sp.wait_ge(sem("stored"), 16)

        @block.gpsimd
        def _(pool):
            def lo_part(f, j):
                pool.wait_ge(hi_ready, f + 1)
                nc.gpsimd.tensor_tensor(w_lo[:, j * FILL:(j + 1) * FILL], w_raw[:, (j % 2) * FILL:(j % 2 + 1) * FILL],
                                        w_hi[:, j * FILL:(j + 1) * FILL].bitcast(F32), ALU.subtract).then_inc(lo_ready, 1)

            def lo_parts(f, n):
                with pool.Fori(0, n // 4) as i:
                    for k in range(4):
                        lo_part(f + 4 * i + k, (3 + k) % 4)

            for f in range(3):
                lo_part(f, f)
            lo_parts(3, FILLS_1)
            mask = C("blk1", 128).rearrange("p (k t) -> p k t", k=2).unsqueeze(1).broadcast_to([P, PAIRS, 2, 64])
            with pool.Fori(0, LAYERS) as l:
                f0 = l * FILLS_L + FILLS_1
                lo_parts(f0 + 3, 16)
                pool.wait_ge(sem("rp_done"), l * PAIRS + PAIRS)
                nc.gpsimd.tensor_tensor(small[:, 62:63], small[:, 61:62], small[:, 61:62], ALU.add)
                with pool.Fori(0, NCH) as c:
                    n = l * NCH + c + 1
                    for name, kb, step in (("b", 76, 1), ("k", 24, 1), ("v", 32, 1), ("a", 60, 2)):
                        src = A(kb, 4 * step * T).rearrange("p (a t) -> p a t", a=PAIRS)[:, :, bass.ds(c * step * CHUNK, CHUNK)]
                        ins = nc.gpsimd.tensor_tensor(rc(name, 512).rearrange("p (a k t) -> p a k t", a=PAIRS, k=2),
                                                      src.unsqueeze(2).broadcast_to([P, PAIRS, 2, CHUNK]), mask, ALU.mult)
                    ins.then_inc(sem("rc_in"), 1)
                    for k in range(4):
                        lo_part(f0 + 19 + 4 * c + k, (3 + k) % 4)
                    pool.wait_ge(sem("rc_w"), n)
                    nc.gpsimd.tensor_tensor(small[:, 62:63], small[:, 61:62], small[:, 61:62], ALU.add)
                lo_parts(f0 + 51, FILLS_L - 48)

        @block.tensor
        def _(pe):
            mm = nc.tensor.matmul

            def blocks(slot, xh, xl, out_ap, cols, tiles, first, last, ready=None):
                n = len(cols)
                for k in range(n):
                    if ready:
                        ready(k)
                    w = slot * FILL + cols[k] * 128
                    x0 = tiles[k] * T
                    ops = [(w_hi, xh), (w_lo, xh), (w_hi, xl)]
                    for o, (wt, xt) in enumerate(ops):
                        ins = mm(out_ap, wt[:, w:w + 128], xt[:, x0:x0 + T],
                                 start=first and k == 0 and o == 0, stop=last and k == n - 1 and o == 2)
                return ins

            def by_pairs(name, n):
                def ready(k):
                    if k % 2 == 0:
                        pe.wait_ge(sem(name), n + k // 2 + 1)
                return ready

            def gemm(f, c, n, xh=XH, xl=XL, ready=None):
                if isinstance(c, int) and c == 0:
                    for j in range(4):
                        pe.wait_ge(lo_ready, j + 1)
                        blocks(j, xh, xl, bank(j), range(8), range(8), True, True, None if j else ready).then_inc(fill_done, 1)
                    f, c, n = 4, 4, n - 4
                with pe.Fori(0, n // 4) as i:
                    for j in range(4):
                        pe.wait_ge(lo_ready, f + 4 * i + j + 1)
                        pe.wait_ge(chunk_out[j], quarter(c) + i)
                        blocks(j, xh, xl, bank(j), range(8), range(8), True, True, None if j else ready).then_inc(fill_done, 1)

            def gemm512(f, c, tile0):
                for j in range(4):
                    pe.wait_ge(lo_ready, f + j + 1)
                    for h in range(2):
                        b = (2 * j + h) % 4
                        pe.wait_ge(chunk_out[b], quarter(c) + j // 2)
                        blocks(j, HH, HL, bank(b), range(4 * h, 4 * h + 4), range(tile0, tile0 + 4), True, True)\
                            .then_inc(fill_done if h else half_done, 1)

            def gemm2816(f, c, value):
                with pe.Fori(0, 2) as i:
                    for j in range(12):
                        q, part = divmod(j, 3)
                        if j == 0:
                            pe.wait_ge(sem("ffn_lo"), value)
                        pe.wait_ge(lo_ready, f + 12 * i + j + 1)
                        if part == 0:
                            pe.wait_ge(chunk_out[q], quarter(c) + i)
                        n = min(8, FT - 8 * part)
                        blocks(j % 4, HH, HL, bank(q), range(n), range(8 * part, 8 * part + n), part == 0, part == 2)\
                            .then_inc(fill_done, 1)

            def sum_of_squares(n):
                pe.wait_ge(sem("acc"), 2 * n + 6)
                mm(bank(5), C("ones", 128), A(ACC_KB), start=True, stop=True).then_inc(sem("rms_var"), 1)

            def layer_norm(n, src, sq, ready=None, acc=0):
                if acc:
                    pe.wait_ge(sem("acc"), acc)
                    ins = mm(bank(4), C("ones", 128), A(ACC_KB), start=True, stop=True)
                else:
                    for t in range(DT):
                        if ready:
                            ready(t)
                        ins = mm(bank(4), C("ones", 128), src(t), start=t == 0, stop=t == DT - 1)
                ins.then_inc(sem("ln_sum"), 1)
                for t in range(DT):
                    if t % 2 == 0:
                        pe.wait_ge(sem("ln_sq"), 4 * n + t // 2 + 1)
                    ins = mm(bank(5), C("ones", 128), sq(t), start=t == 0, stop=t == DT - 1)
                ins.then_inc(sem("ln_var"), 1)

            def all_out(c):
                for b in range(4):
                    pe.wait_ge(chunk_out[b], quarter(c))

            def transposes(b, src, n=4):
                for k in range(n):
                    ins = nc.tensor.transpose(bank(b, 128, 128 * k), src(k), C("ident", 128))
                return ins

            pe.wait_ge(sem("x_in"), 16)
            layer_norm(0, lambda t: H[:, t * T:(t + 1) * T], lambda t: A(16, T, t * T))
            pe.wait_ge(sem("cond"), 1)
            pe.wait_ge(sem("ada_in0"), 16)
            for t in range(4):
                for kt in range(DT):
                    mm(bank(6, 1, t), A(40, 128, (t * DT + kt) * 128), cond[:, kt:kt + 1], start=kt == 0, stop=kt == DT - 1)
            pe.wait_ge(sem("cond"), 2)
            for t in range(4, ADA_FIRST):
                ins = mm(bank(6, 1, t), A(40, 128, t * DT * 128), C("ones", 1), start=True, stop=True)
            ins.then_inc(sem("ada_used"), 1)
            gemm(0, 0, 32, ready=by_pairs("ln_x", 0))
            def hgrn_head(i, hh):
                h = 2 * i + hh

                def half_fill(k):
                    j, part = divmod(k, 2)
                    if part == 0:
                        pe.wait_ge(lo_ready, 32 + 4 * i + j + 1)
                        pe.wait_ge(chunk_out[j], 8 + i)
                    ins = blocks(j, XH, XL, bank(j), range(4 * part, 4 * part + 4), range(4 * part, 4 * part + 4), part == 0, part == 1)
                    if part:
                        ins.then_inc(fill_done, 1)

                def condition(a):
                    at_ = ADA_AT[a]
                    pe.wait_ge(w_loaded[at_ % 2], arrived(FILLS_HG + 12 * i, at_))
                    for kt in range(DT):
                        ins = mm(psum[:, bass.ds(512 * 6 + 256 + 8 * i + a, 1)], w_raw[:, at_ % 2 * FILL + kt * 128:at_ % 2 * FILL + kt * 128 + 128],
                                 cond[:, kt:kt + 1], start=kt == 0, stop=kt == DT - 1)
                    ins.then_inc(sem("ada_done"), 1)

                pe.wait_ge(sem("hg_q"), h + 1)
                transposes(4, lambda k: hg("kdec", 128, 128 * k))
                transposes(5, lambda k: hg("val", 128, 128 * k)).then_inc(sem("hg_tr"), 1)
                half_fill(4 * hh)
                pe.wait_ge(sem("hg_k"), h + 1)
                for c in range(NCH):
                    for s in range(4):
                        ins = mm(bank(6, SUB, 64 * (c // 2) + SUB * s)[64 * (c % 2):64 * (c % 2) + 64],
                                 hg("ks", 64, (4 * c + s) * 64), hg("qs", SUB, c * CHUNK + s * SUB), start=True, stop=True)
                ins.then_inc(sem("hg_sc"), 1)
                pe.wait_ge(sem("hg_tm"), h + 1)
                for c in range(NCH - 1):
                    p0, t0 = 64 * (c % 2), 128 * (c // 2)
                    ins = mm(bank(4 if c % 2 else 7, 128, t0), hg("kdec_t", 128, t0)[p0:p0 + 64], hg("val_t", 128, t0)[p0:p0 + 64],
                             start=True, stop=True)
                ins.then_inc(sem("hg_u"), 1)
                pe.wait_ge(sem("hg_st"), h + 1)
                half_fill(4 * hh + 1)
                pe.wait_ge(sem("hg_s"), h + 1)
                for b in range(NBLK):
                    mm(bank(5, 128, 128 * b), hg("val_t", 128, 128 * b), hg("st", 128, 128 * b), start=True, stop=False)
                    for c in (2 * b, 2 * b + 1):
                        ins = mm(bank(5, 64, 64 * c), hg("state", 128, 128 * c), hg("qi", 64, 64 * c), start=False, stop=c % 2 == 1)
                ins.then_inc(sem("hg_o"), 1)
                if hh:
                    half_fill(6)
                pe.wait_ge(sem("hg_sq"), h + 1)
                mm(bank(7), C("ones", 128), hg("sq", T), start=True, stop=True).then_inc(sem("hg_var"), 1)
                for k in (7,) if hh else (2, 3):
                    half_fill(k)
                for a in range(4 * hh, 4 * hh + 4):
                    condition(a)

            with pe.Fori(0, HEADS // 2) as i:
                for hh in range(2):
                    hgrn_head(i, hh)
            layer_norm(1, lambda t: A(60, T, t * T), lambda t: A(76, T, t * T), ready=by_pairs("gm_gelu", 0))
            pe.wait_ge(sem("ln_h"), 4)
            pe.wait_ge(sem("gm_mask"), 1)
            def gmlp_group(i, j):
                g = 4 * i + j

                def half_fill(part):
                    if part == 0:
                        pe.wait_ge(lo_ready, 48 + g + 1)
                        pe.wait_ge(chunk_out[j], 12 + i)
                    ins = blocks(j, XH, XL, bank(j), range(4 * part, 4 * part + 4), range(4 * part, 4 * part + 4), part == 0, part == 1)
                    if part:
                        ins.then_inc(fill_done, 1)

                pe.wait_ge(sem("gm_vs"), g + 1)
                transposes(4, lambda k: A(40, 128, 128 * k)).then_inc(sem("gm_tr"), 1)
                half_fill(0)
                pe.wait_ge(sem("gm_vt"), g + 1)
                for b in range(NBLK):
                    ins = mm(bank(5, 128, 128 * b), A(42, 128, 128 * b), A(32, 128, 128 * g), start=True, stop=True)
                ins.then_inc(sem("gm_sv"), 1)
                half_fill(1)

            with pe.Fori(0, 2) as i:
                for j in range(4):
                    gmlp_group(i, j)
            pe.wait_ge(sem("hg_y"), HEADS)
            gemm(56, 56, 8, HH, HL)
            gemm(64, 64, 8)
            gemm(72, 72, 8, HH, HL, ready=by_pairs("gm_lo", 0))
            gemm(80, 80, 8, ready=lambda k: pe.wait_ge(sem("mix_lo"), k + 1))
            layer_norm(2, None, lambda t: A(16, T, t * T), acc=2)
            layer_norm(3, lambda t: H[:, t * T:(t + 1) * T], lambda t: A(16, T, t * T), ready=by_pairs("ln_h", 4))
            gemm(88, 88, 44, ready=by_pairs("ln_x", 4))
            gemm2816(132, 132, FT)
            layer_norm(4, None, lambda t: A(16, T, t * T), acc=4)

            with pe.Fori(0, LAYERS) as l:
                f0, c0 = l * FILLS_L + FILLS_1, l * (CHUNKS_L // 4) + CHUNKS_1 // 4
                sum_of_squares(2 * l)
                gemm(f0, c0, 16, ready=by_pairs("rms_x", 8 * l))
                pe.wait_ge(sem("rp_k2"), l + 1)
                for p in range(PAIRS):
                    ins = mm(bank(4 + p), C("blk1", 128), rp("rn", T, p * T), start=True, stop=True)
                ins.then_inc(sem("rp_ss"), 1)
                pe.wait_ge(sem("rw_act"), l + 1)
                pe.wait_ge(sem("lora_in"), 16 * l + 16)
                for n in range(4):
                    mm(bank(n), A(88, 128, 128 * n)[0:64], A(16, T, 12 * T)[0:64], start=True, stop=True).then_inc(sem("rw_lora"), 1)
                pe.wait_ge(sem("rp_mx"), l + 1)
                for n in range(4):
                    mm(bank(4 + n), A(88, 128, 128 * n)[64:128], A(16, T, 12 * T)[64:128], start=True, stop=True).then_inc(sem("rw_lora"), 1)
                for n in range(4):
                    pe.wait_ge(sem("rw_lev"), 12 * l + n + 1)
                    mm(bank(n), A(88, 128, 512 + 128 * n), A(16, T, 13 * T), start=True, stop=True).then_inc(sem("rw_lora"), 1)
                with pe.Fori(0, PAIRS) as p:
                    pe.wait_ge(sem("rp_rk"), 4 * l + p + 1)
                    mm(bank(5), C("blk1", 128), rp("rk", T), start=True, stop=True).then_inc(sem("rp_bn"), 1)
                with pe.Fori(0, NCH) as c:
                    n = l * NCH + c + 1
                    pairs = range(PAIRS)

                    def half_fill(k):
                        j, h = divmod(k, 2)
                        if h == 0:
                            pe.wait_ge(lo_ready, f0 + 16 + 4 * c + j + 1)
                            pe.wait_ge(chunk_out[j], c0 + 4 + c)
                        ins = blocks(j, XH, XL, bank(j), range(4 * h, 4 * h + 4), range(4 * h, 4 * h + 4), h == 0, h == 1)
                        if h:
                            ins.then_inc(fill_done, 1)

                    def bd(name, p):
                        return rc(name, 128, 128 * p)

                    def product(b, *terms):
                        for p in pairs:
                            for k, (left, right) in enumerate(terms):
                                n = 64 if right.endswith("_c") else 128
                                ins = mm(bank(b, n, n * p), bd(left, p), rc(right, n, n * p), start=k == 0, stop=k == len(terms) - 1)
                        return ins

                    def r(p):
                        return A(60, 64, 2 * T * p + 64 + c * 128)

                    pe.wait_ge(sem("rc_in"), n)
                    for p in pairs:
                        mm(bank(5, 64, 64 * p), bd("a", p), A(76, 64, T * p + 64 * c), start=True, stop=True)
                    product(6, ("k", "a")).then_inc(sem("rc_s1"), 1)
                    pe.wait_ge(sem("rc_st"), n + l)
                    product(4, ("b", "a"))
                    for p in pairs:
                        mm(bank(7, 64, 128 * p), bd("b", p), r(p), start=True, stop=True)
                        ins = mm(bank(7, 64, 128 * p + 64), bd("k", p), r(p), start=True, stop=True)
                    ins.then_inc(sem("rc_s2"), 1)
                    half_fill(0)
                    pe.wait_ge(sem("rc_out"), n)
                    transposes(5, lambda p: bd("b", p))
                    transposes(6, lambda p: bd("k", p))
                    transposes(7, lambda p: bd("v", p)).then_inc(sem("rc_tr"), 1)
                    pe.wait_ge(sem("rc_trc"), n)
                    for v in range(1, 6):
                        pe.wait_ge(sem("rc_al"), 5 * n - 5 + v)
                        product(5, ("al", "t_c")).then_inc(sem("rc_p"), 1)
                        half_fill(v)
                        pe.wait_ge(sem("rc_pc"), 5 * n - 5 + v)
                        if v > 1:
                            pe.wait_ge(sem("rc_uu"), 5 * n - 6 + v)
                        if v < 5:
                            product(6, ("u", "p_c")).then_inc(sem("rc_d"), 1)
                        product(7, ("p", "u_c")).then_inc(sem("rc_e"), 1)
                    product(5, ("a", "state_c"), ("ak", "v_c")).then_inc(sem("rc_w"), 1)
                    half_fill(6)
                    pe.wait_ge(sem("rc_wc"), n)
                    pe.wait_ge(sem("rc_uu"), 5 * n)
                    product(6, ("u", "p_c")).then_inc(sem("rc_u"), 1)
                    half_fill(7)
                    pe.wait_ge(sem("rc_uc"), n)
                    for p in pairs:
                        y = bank(7, 64, 64 * p)
                        mm(y, bd("state", p), r(p), start=True, stop=False)
                        mm(y, bd("us", p), rc("rbk", 64, 128 * p), start=False, stop=False)
                        ins = mm(y, bd("v_t", p), rc("rbk", 64, 128 * p + 64), start=False, stop=True)
                    ins.then_inc(sem("rc_y"), 1)
                    product(4, ("b_t", "us_c"), ("k_t", "v_c")).then_inc(sem("rc_n"), 1)
                pe.wait_ge(sem("rc_st"), (l + 1) * (NCH + 1))
                for h in range(2):
                    for p in (2 * h, 2 * h + 1):
                        ins = mm(bank(4 + p), C("blk1", 128), A(84, T, p * T), start=True, stop=True)
                    ins.then_inc(sem("ro_m"), 1)
                all_out(c0 + 12)
                for h in range(2):
                    pe.wait_ge(sem("ro_s"), 2 * l + h + 1)
                    for p in (2 * h, 2 * h + 1):
                        ins = mm(bank(p), C("blk1", 128), A(100, T, p * T), start=True, stop=True)
                    ins.then_inc(sem("ro_v"), 1)
                pe.wait_ge(sem("ro_l"), 2 * l + 2)
                gemm512(f0 + 48, c0 + 12, 0)
                gemm(f0 + 52, c0 + 14, 12)
                pe.wait_ge(sem("ak_sq"), l + 1)
                mm(bank(4), C("blk1", 128), at("sq", T), start=True, stop=True).then_inc(sem("ak_ss"), 1)
                transposes(5, lambda k: A(14, 128, 128 * k)).then_inc(sem("av_tr"), 1)
                pe.wait_ge(sem("ak_n"), l + 1)
                for j in range(2):
                    ins = mm(bank(6 + j), C("dup", 128, 128 * j), at("kn", T), start=True, stop=True)
                ins.then_inc(sem("ak_dup"), 1)
                with pe.Fori(0, PAIRS) as p:
                    n = l * PAIRS + p
                    halves = (slice(0, 64), slice(64, 128))

                    def scores(hh):
                        for b in range(NBLK):
                            k0, k1 = max(0, BLK * (b - 1)), BLK * (b + 1)
                            ins = mm(bank(4, k1 - k0, 256 * b + 256 - (k1 - k0)), at("qs", 128, 128 * b)[halves[hh]],
                                     at("kj", k1 - k0, k0)[halves[hh]], start=True, stop=True)
                        ins.then_inc(sem("at_sc"), 1)

                    def probs_t(hh):
                        for s in range(1, 8):
                            ins = nc.tensor.transpose(bank(6 - 2 * hh, 128, 128 * s), at("pb", 128, 128 * s), C("ident", 128))
                        ins.then_inc(sem("at_pt"), 1)

                    def weighted(hh):
                        for b in range(NBLK):
                            o = bank(6, 128, 128 * b)[halves[hh]]
                            if b:
                                mm(o, at("vj", 64, 64 * (b - 1)), at("pt", 128, 256 * b), start=True, stop=False)
                            ins = mm(o, at("vj", 64, 64 * b), at("pt", 128, 256 * b + 128), start=b == 0, stop=True)
                        ins.then_inc(sem("at_o"), 1)

                    pe.wait_ge(sem("table_in"), 16 * l + 16)
                    pe.wait_ge(sem("rq_in"), 16 * l + 16)
                    pe.wait_ge(sem("at_sq"), n + 1)
                    mm(bank(7), C("blk1", 128), at("sq", T), start=True, stop=True).then_inc(sem("at_ss"), 1)
                    pe.wait_ge(sem("rt_in"), n + 1)
                    mm(bank(0), TB("rot", 128), A(60, T, p * T), start=True, stop=True)
                    mm(bank(1), TB("rot", 128), A(68, T, p * T), start=True, stop=True).then_inc(sem("rt_rot"), 1)
                    pe.wait_ge(sem("at_q"), n + 1)
                    scores(0)
                    pe.wait_ge(sem("rt_qk"), n + 1)
                    transposes(2, lambda k: rt("kz", 128, 128 * k))
                    transposes(3, lambda k: rt("vs", 128, 128 * k)).then_inc(sem("rt_tr"), 1)
                    for hh in range(2):
                        for b in range(NBLK):
                            ins = mm(bank(hh, 128, 128 * b), rt("kr", 128, 128 * b)[halves[hh]], rt("qr", 128, 128 * b)[halves[hh]], start=True, stop=True)
                    ins.then_inc(sem("rt_sc"), 1)
                    pe.wait_ge(sem("at_m"), 2 * n + 1)
                    scores(1)
                    pe.wait_ge(sem("rt_tm"), n + 1)
                    for b in range(NBLK - 1):
                        ins = mm(bank(3, 128, 128 * b), rt("kz_t", 128, 128 * b), rt("v_t", 128, 128 * b), start=True, stop=True)
                    ins.then_inc(sem("rt_kv"), 1)
                    pe.wait_ge(sem("at_pn"), 2 * n + 1)
                    probs_t(0)
                    pe.wait_ge(sem("at_ptc"), 2 * n + 1)
                    weighted(0)
                    pe.wait_ge(sem("rt_r"), n + 1)
                    for b in range(NBLK):
                        mm(bank(2, 128, 128 * b), rt("state", 128, 128 * b), rt("qx", 128, 128 * b), start=True, stop=False)
                        for hh in range(2):
                            ins = mm(bank(2, 128, 128 * b)[halves[hh]], rt("v_t", 64, 128 * b + 64 * hh), rt("st", 128, 512 * hh + 128 * b),
                                     start=False, stop=True)
                    ins.then_inc(sem("rt_o"), 1)
                    pe.wait_ge(sem("at_pn"), 2 * n + 2)
                    probs_t(1)
                    pe.wait_ge(sem("rt_sq"), n + 1)
                    mm(bank(0), C("blk1", 128), rt("sq", T), start=True, stop=True).then_inc(sem("rt_var"), 1)
                    pe.wait_ge(sem("at_ptc"), 2 * n + 2)
                    weighted(1)
                pe.wait_ge(sem("at_y"), 2 * l + 1)
                gemm512(f0 + 64, c0 + 17, 0)
                pe.wait_ge(sem("at_y"), 2 * l + 2)
                gemm512(f0 + 68, c0 + 19, 4)
                gemm(f0 + 72, c0 + 21, 8, ready=lambda k: pe.wait_ge(sem("mix_lo"), 8 * l + 8 + k + 1))
                sum_of_squares(2 * l + 1)
                gemm(f0 + 80, c0 + 23, 44, ready=by_pairs("rms_x", 8 * l + 4))
                gemm2816(f0 + 124, c0 + 34, l * FT + 2 * FT)

        @block.scalar
        def _(act):
            fn = nc.scalar.activation

            def hi(f, j, r=None):
                s = (j + LEAD) % 4
                if r is None:
                    r = f + LEAD + ADA_LATER
                act.wait_ge(w_loaded[s % 2], arrived(r, j))
                act.wait_ge(fill_done, f + j + 1)
                fn(w_hi[:, s * FILL:(s + 1) * FILL], w_raw[:, (s % 2) * FILL:(s % 2 + 1) * FILL], ACT.Copy).then_inc(hi_ready, 1)

            def hi_hgrn(i, j):
                act.wait_ge(w_loaded[j % 2], arrived(FILLS_HG + 12 * i, FILL_AT[j]))
                act.wait_ge(fill_done, FILLS_HG - LEAD + 4 * i + j + 1)
                s = (FILLS_HG + j) % 4
                fn(w_hi[:, s * FILL:(s + 1) * FILL], w_raw[:, j % 2 * FILL:(j % 2 + 1) * FILL], ACT.Copy).then_inc(hi_ready, 1)

            def gemm(f, c, n, take=None):
                with act.Fori(0, n // 4) as i:
                    for j in range(4):
                        if take:
                            act.wait_ge(fill_done, f + 4 * i + j + 1)
                            take(i, j, chunk_out[j])
                        hi(f + 4 * i, j, f + 4 * i + LEAD + (0 if isinstance(f, int) and f < 32 else ADA_LATER))

            def gemm512(f):
                for j in range(4):
                    hi(f, j)

            def gemm2816(f):
                with act.Fori(0, 2) as i:
                    for j in range(12):
                        hi(f + 12 * i + j // 4 * 4, j % 4)

            def ln_exp_tables():
                act.preload_act_table_set("natural_log_exp_and_others")

            def rstd(name, b, scale, eps, out_ap, done):
                fn(out_ap, bank(b), ACT.Ln, scale=scale, bias=C("eps", 1, eps))
                nc.scalar.drain()
                fn(out_ap, out_ap, ACT.Exp, scale=-0.5).then_inc(sem(done), 1)

            def norm_tail(n, name, eps):
                act.wait_ge(sem(name + "_var"), n + 1)
                rstd(name, 5, 1.0 / D, eps, A(34), name + "_rstd")

            def norm_hi(n, name):
                for q in range(4):
                    act.wait_ge(sem(name + "_u"), 4 * n + q + 1)
                    fn(XH[:, 2 * q * T:(2 * q + 2) * T], A(0, 2 * T, 2 * q * T), ACT.Copy).then_inc(sem(name + "_hi"), 1)

            def layer_norm(n, xc, sq):
                ln_exp_tables()
                for q in range(4):
                    act.wait_ge(sem("ln_xc"), 4 * n + q + 1)
                    fn(sq(2 * q), xc(2 * q), ACT.Square).then_inc(sem("ln_sq"), 1)
                norm_tail(n, "ln", 0)

            def ffn(f, c, n0):
                act.preload_act_table(ACT.Silu)
                with act.Fori(0, FT // 2) as i:
                    for j in range(4):
                        if j % 2 == 0:
                            act.wait_ge(fill_done, f + 4 * i + j + 1)
                            fn(A(88, T, j // 2 * T), bank(j), ACT.Silu).then_inc(chunk_out[j], 1)
                        else:
                            act.wait_ge(chunk_out[j], quarter(c) + i + 1)
                            fn(HH[:, bass.ds((2 * i + j // 2) * T, T)], A(105, T, j // 2 * T), ACT.Copy).then_inc(sem("ffn_hi"), 1)
                        hi(f + 4 * i, j)

            def all_out(c):
                for b in range(4):
                    act.wait_ge(chunk_out[b], quarter(c))

            def first_hi(f):
                act.wait_ge(w_loaded[f % 2], 16 * (f // 2) + 16)
                fn(w_hi[:, f * FILL:(f + 1) * FILL], w_raw[:, (f % 2) * FILL:(f % 2 + 1) * FILL], ACT.Copy).then_inc(hi_ready, 1)

            act.wait_ge(sem("const_in"), 48)
            fn(cond[:], P1("c", 0, 8), ACT.Silu).then_inc(sem("cond"), 1)
            act.wait_ge(sem("lb_max"), 1)
            fn(lbt[:, 8:24], lbt[:, 8:24], ACT.Exp).then_inc(sem("lb_exp"), 1)
            two = lambda kb: (lambda t: A(kb, 2 * T, t * T))
            layer_norm(0, two(0), two(16))
            for f in range(4):
                first_hi(f)
            norm_hi(0, "ln")
            def take_hgrn(i, j, done):
                kb, func = ((0, ACT.Silu), (16, ACT.Silu), (44, ACT.Sigmoid), (60, ACT.Copy))[j]
                fn(A(kb, T, i * T), bank(j), func).then_inc(done, 1)
            gemm(0, 0, 28, take_hgrn)
            for j in range(4):
                act.wait_ge(fill_done, 28 + j + 1)
                take_hgrn(7, j, chunk_out[j])
                if j < FILLS_HG - 28 - LEAD:
                    hi(28, j, 28 + LEAD)
            ln_exp_tables()
            def hgrn_head(i, hh):
                h = 2 * i + hh
                act.wait_ge(sem("hg_f"), h + 1)
                fn(hg("lf", T), hg("lf", T), ACT.Ln).then_inc(sem("hg_lf"), 1)
                act.wait_ge(sem("hg_ex"), h + 1)
                fn(hg("qs", T), hg("qs", T), ACT.Exp)
                fn(hg("kdec", T), hg("kdec", T), ACT.Exp)
                fn(hg("e1", T), hg("cum", T), ACT.Exp).then_inc(sem("hg_exp"), 1)
                act.wait_ge(sem("hg_ks"), h + 1)
                ks = hg("ks", 2048).rearrange("p (c i s) -> p c i s", c=NCH, i=4)
                for s in range(4):
                    n = SUB * (s + 1)
                    ins = fn(ks[:, :, s, :n], ks[:, :, s, :n], ACT.Exp)
                ins.then_inc(sem("hg_kse"), 1)
                act.wait_ge(sem("hg_tr"), h + 1)
                fn(hg("kdec_t", T), bank(4), ACT.Copy)
                fn(hg("val_t", T), bank(5), ACT.Copy).then_inc(sem("hg_tm"), 1)
                hi_hgrn(i, 2 * hh)
                hi_hgrn(i, 2 * hh + 1)
                act.wait_ge(sem("hg_o"), h + 1)
                fn(hg("sq", T), bank(5), ACT.Square).then_inc(sem("hg_sq"), 1)
                act.wait_ge(sem("hg_var"), h + 1)
                rstd("hg", 7, 1.0 / 128, 1, hg("rstd", T), "hg_rstd")
                act.wait_ge(sem("hg_out"), h + 1)
                fn(HH[:, bass.ds(h * T, T)], hg("o", T), ACT.Copy).then_inc(sem("hg_hi"), 1)

            with act.Fori(0, HEADS // 2) as i:
                for hh in range(2):
                    hgrn_head(i, hh)
                for j in range(4):
                    act.wait_ge(fill_done, 32 + 4 * i + j + 1)
                    fn(A(16 if j < 2 else 60, T, (2 * i + j % 2) * T), bank(j), ACT.Copy).then_inc(chunk_out[j], 1)
            for j in range(2, 4):
                hi(44, j)
            act.wait_ge(sem("hg_y"), HEADS)
            act.dma_start(A(32, 8 * 128), dram["gm_ws"]).then_inc(sem("gm_in"), 16)
            act.dma_start(A(36, 8 * 128), dram["gm_bs"].broadcast_to([P, 8 * 128])).then_inc(sem("gm_in"), 16)
            all_out(48)
            for kb in (60, 16):
                for q in range(4):
                    fn(A(kb, 2 * T, 2 * q * T), A(kb, 2 * T, 2 * q * T), ACT.Gelu).then_inc(sem("gm_gelu"), 1)
            ln_exp_tables()
            for q in range(4):
                act.wait_ge(sem("ln_xc"), 4 + q + 1)
                fn(A(76, 2 * T, 2 * q * T), A(60, 2 * T, 2 * q * T), ACT.Square).then_inc(sem("ln_sq"), 1)
            act.wait_ge(sem("ln_var"), 2)
            rstd("ln", 5, 1.0 / D, 0, A(105), "ln_rstd")
            act.preload_act_table(ACT.Sigmoid)
            with act.Fori(0, 2) as i:
                for j in range(4):
                    act.wait_ge(sem("gm_tr"), 4 * i + j + 1)
                    fn(A(42), bank(4), ACT.Copy).then_inc(sem("gm_vt"), 1)
                    act.wait_ge(fill_done, 48 + 4 * i + j + 1)
                    fn(A(60, T, (4 * i + j) * T), bank(j), ACT.Sigmoid, bias=P1("b_gate", 4 * i + j)).then_inc(chunk_out[j], 1)
                    hi(48 + 4 * i, j)
            gemm(56, 56, 8)
            gemm(64, 64, 8, lambda i, j, done: fn(A(76, T, (4 * i + j) * T), bank(j), ACT.Sigmoid, bias=P1("b_gate", 4 * i + j + 8)).then_inc(done, 1))
            all_out(64)
            act.wait_ge(sem("gm_u"), 8)
            for q in range(4):
                fn(HH[:, 2 * q * T:(2 * q + 2) * T], A(16, 2 * T, 2 * q * T), ACT.Copy).then_inc(sem("gm_hi"), 1)
            def sum_hi(n0):
                def take(i, j):
                    act.wait_ge(sem("mix_sum"), n0 + 4 * i + j + 1)
                    fn(XH[:, bass.ds((4 * i + j) * T, T)], A(60, T, (4 * i + j) * T), ACT.Copy).then_inc(sem("mix_hi"), 1)
                return take
            take = sum_hi(0)
            with act.Fori(0, 2) as i:
                for j in range(4):
                    hi(72 + 4 * i, j)
                    take(i, j)
            gemm(80, 80, 8)
            layer_norm(2, two(0), two(16))
            layer_norm(3, two(0), two(16))
            norm_hi(1, "ln")
            ffn(88, 88, 0)
            gemm2816(132)
            layer_norm(4, two(0), two(16))
            for q in range(4):
                act.wait_ge(sem("ln_h"), 8 + q + 1)
                fn(A(16, 2 * T, 2 * q * T), H[:, 2 * q * T:(2 * q + 2) * T], ACT.Square).then_inc(sem("ln_sq"), 1)

            with act.Fori(0, LAYERS) as l:
                f0, c0 = l * FILLS_L + FILLS_1, l * (CHUNKS_L // 4) + CHUNKS_1 // 4

                def rms_norm(k):
                    ln_exp_tables()
                    norm_tail(2 * l + k, "rms", 1)
                    norm_hi(2 * l + k, "rms")

                def take_at(kb):
                    return lambda i, j, done: fn(A(kb, T, (4 * i + j) * T), bank(j), ACT.Copy).then_inc(done, 1)

                rms_norm(0)
                act.dma_start(A(88, 1024), dram["lora"][bass.ds(l, 1)].rearrange("a p n -> (a p) n")).then_inc(sem("lora_in"), 16)
                gemm(f0, c0, 16, take_at(12))
                act.wait_ge(sem("rw_mix"), 14 * l + 8)
                for p in range(PAIRS):
                    ins = fn(rp("rn", T, p * T), A(24, T, p * T), ACT.Square, scale=P2(l, "k_k", p))
                ins.then_inc(sem("rp_k2"), 1)
                act.wait_ge(sem("rw_mix"), 14 * l + 14)
                fn(A(16, T, 12 * T)[0:64], A(16, T, 12 * T)[0:64], ACT.Tanh)
                fn(A(16, T, 13 * T), A(16, T, 13 * T), ACT.Sigmoid).then_inc(sem("rw_act"), 1)
                act.wait_ge(sem("rp_mx"), l + 1)
                fn(rp("rn", 4 * T), rp("rn", 4 * T), ACT.Sqrt).then_inc(sem("rp_rn"), 1)
                for n in range(12):
                    act.wait_ge(sem("rw_lora"), 12 * l + n + 1)
                    if n < 4:
                        ins = fn(A(76, T, n * T), bank(n), ACT.Sigmoid, bias=P2(l, "w0", n))
                    elif n < 8:
                        ins = fn(A(44, T, (n - 4) * T), bank(n), ACT.Sigmoid, bias=P2(l, "a0", n - 4))
                    else:
                        ins = fn(A(52, T, (n - 8) * T), bank(n - 8), ACT.Copy)
                    ins.then_inc(sem("rw_lev"), 1)
                ln_exp_tables()
                with act.Fori(0, PAIRS) as p:
                    n = l * PAIRS + p + 1
                    act.wait_ge(sem("rp_cs"), n)
                    fn(rp("e", T), rp("cs", T), ACT.Exp, scale=-RWKV_DECAY)
                    fn(rp("ei", T), rp("cs", T), ACT.Exp, scale=RWKV_DECAY)
                    fn(rp("ex", T), rp("cx", T), ACT.Exp, scale=-RWKV_DECAY).then_inc(sem("rp_e"), 1)
                act.preload_act_table(ACT.Sigmoid)
                with act.Fori(0, NCH) as c:
                    n = l * NCH + c + 1

                    def take(j):
                        act.wait_ge(fill_done, f0 + 16 + 4 * c + j + 1)
                        buffer = rc("spill", T, T * (j if j < 3 else 1))
                        if j == 3:
                            act.wait_ge(spilled[1], 16 * n)
                        fn(buffer, bank(j), ACT.Copy if j == 3 else ACT.Sigmoid).then_inc(chunk_out[j], 1)
                        hi(f0 + 16 + 4 * c, j)
                        act.wait_ge(chunk_out[j], c0 + 4 + c + 1)
                        act.dma_start(scratch[bass.ds(l * 32 + 8 * j + c, 1)].rearrange("a p n -> (a p) n"),
                                      buffer).then_inc(spilled[j], 16)

                    def both_blocks(name, b, block):
                        for h in range(2):
                            r = slice(64 * h, 64 * h + 64)
                            ins = fn(chunks(rc(name, 512), 128)[r, :, 64 * h:64 * h + 64], block(h)[r], ACT.Copy)
                        return ins

                    act.wait_ge(sem("rc_tr"), n)
                    fn(rc("b_t", T), bank(5), ACT.Copy)
                    fn(rc("k_t", T), bank(6), ACT.Copy)
                    fn(rc("v_t", T), bank(7), ACT.Copy)
                    for h in range(2):
                        r = slice(64 * h, 64 * h + 64)
                        ins = fn(chunks(rc("v_c", 256))[r], chunks(bank(7), 128)[r, :, 64 * h:64 * h + 64], ACT.Copy)
                    ins.then_inc(sem("rc_trc"), 1)
                    for v in range(1, 6):
                        act.wait_ge(sem("rc_p"), 5 * n - 5 + v)
                        fn(rc("p_c", 256), bank(5, 256), ACT.Copy)
                        both_blocks("p", 5, lambda h: chunks(bank(5, 256))).then_inc(sem("rc_pc"), 1)
                        if v in (2, 4):
                            take(v // 2 - 1)
                    take(2)
                    act.wait_ge(sem("rc_w"), n)
                    fn(rc("p_c", 256), bank(5, 256), ACT.Copy).then_inc(sem("rc_wc"), 1)
                    act.wait_ge(sem("rc_u"), n)
                    fn(rc("us_c", 256), bank(6, 256), ACT.Copy)
                    both_blocks("us", 6, lambda h: chunks(bank(6, 256))).then_inc(sem("rc_uc"), 1)
                    take(3)
                    act.wait_ge(sem("rc_y"), n)
                    fn(A(84, 4 * T).rearrange("p (a t) -> p a t", a=PAIRS)[:, :, bass.ds(c * CHUNK, CHUNK)],
                       chunks(bank(7, 256)), ACT.Copy).then_inc(sem("rc_yc"), 1)
                    for j in range(4):
                        act.wait_ge(spilled[j], 16 * n)

                def from_scratch(dst, tile, tiles, done):
                    act.dma_start(dst.rearrange("p (a n) -> p a n", n=T),
                                  scratch[bass.ds(l * 32 + tile, tiles)].rearrange("a p n -> p a n")).then_inc(sem(done), 16)

                act.wait_ge(sem("rc_y"), l * NCH + NCH)
                from_scratch(A(60, 8 * T), 8, 8, "gate_b_in")
                ln_exp_tables()
                two_pairs = lambda kb, h: A(kb, 2 * T, 2 * h * T)
                for h in range(2):
                    act.wait_ge(sem("ro_c"), 2 * l + h + 1)
                    fn(two_pairs(100, h), two_pairs(92, h), ACT.Square).then_inc(sem("ro_s"), 1)
                for h in range(2):
                    act.wait_ge(sem("ro_v"), 2 * l + h + 1)
                    fn(two_pairs(24, h), bank(2 * h, 2 * T), ACT.Ln, scale=1.0 / 64, bias=C("eps", 1, 2))
                    nc.scalar.drain()
                    fn(two_pairs(24, h), two_pairs(24, h), ACT.Exp, scale=-0.5).then_inc(sem("ro_r"), 1)
                for h in range(2):
                    act.wait_ge(sem("ro_y"), 2 * l + h + 1)
                    fn(HH[:, 2 * h * T:(2 * h + 2) * T], two_pairs(92, h), ACT.Copy).then_inc(sem("ro_h"), 1)
                act.wait_ge(sem("ro_l"), 2 * l + 2)
                act.dma_start(A(92, N_TABLE), dram["table"]).then_inc(sem("table_in"), 16)
                from_scratch(A(52, 4 * T), 24, 4, "aq_in")
                gemm512(f0 + 48)
                all_out(c0 + 14)
                from_scratch(A(60, 4 * T), 28, 4, "rq_in")
                gemm(f0 + 52, c0 + 14, 12, take_at(68))
                all_out(c0 + 17)
                fn(A(84, 4 * T), A(84, 4 * T), ACT.Silu)
                ln_exp_tables()
                act.wait_ge(sem("aq_in"), 16 * l + 16)
                fn(at("sq", T), A(12), ACT.Square).then_inc(sem("ak_sq"), 1)
                act.wait_ge(sem("ak_ss"), l + 1)
                rstd("ak", 4, 1.0 / 64, 1, at("rs", T), "ak_rs")
                act.wait_ge(sem("av_tr"), l + 1)
                fn(at("vt", T), bank(5), ACT.Copy)
                act.wait_ge(sem("ak_dup"), l + 1)
                fn(at("kd", 2 * T), bank(6, 2 * T), ACT.Copy).then_inc(sem("ak_kv"), 1)
                with act.Fori(0, PAIRS) as p:
                    n = l * PAIRS + p

                    def exps(hh):
                        act.wait_ge(sem("at_m"), 2 * n + hh + 1)
                        for b in range(NBLK):
                            fn(at("pb", 256, 256 * b), at("sc", 256, 256 * b), ACT.Exp, bias=small[:, b:b + 1], accum_out=small[:, 8 + b:9 + b])
                        fn(small[:, 16:20], small[:, 0:4], ACT.Exp, bias=P2(l, "sinks", 2 * p + hh)).then_inc(sem("at_p"), 1)

                    def probs_out(hh):
                        act.wait_ge(sem("at_pt"), 2 * n + hh + 1)
                        fn(at("pt", 896, 128), bank(6 - 2 * hh, 896, 128), ACT.Copy).then_inc(sem("at_ptc"), 1)

                    fn(at("sq", T), A(52, T, p * T), ACT.Square).then_inc(sem("at_sq"), 1)
                    act.wait_ge(sem("at_ss"), n + 1)
                    rstd("at", 7, 1.0 / 64, 1, at("rs", T), "at_rs")
                    act.wait_ge(sem("rt_tr"), n + 1)
                    fn(rt("kz_t", T), bank(2), ACT.Copy)
                    fn(rt("v_t", T), bank(3), ACT.Copy).then_inc(sem("rt_tm"), 1)
                    exps(0)
                    probs_out(0)
                    exps(1)
                    act.wait_ge(sem("rt_o"), n + 1)
                    fn(rt("sq", T), bank(2), ACT.Square).then_inc(sem("rt_sq"), 1)
                    probs_out(1)
                    act.wait_ge(sem("rt_var"), n + 1)
                    rstd("rt", 0, 1.0 / 64, 1, rt("rs", T), "rt_rs")
                    act.wait_ge(sem("at_o"), 2 * n + 2)
                    fn(small[:, 60:61], small[:, 60:61], ACT.Copy)
                    fn(A(52, T, p * T), bank(6), ACT.Copy).then_inc(sem("at_ao"), 1)
                act.wait_ge(sem("at_ao"), l * PAIRS + PAIRS)
                fn(HH[:, 0:4 * T], A(52, 4 * T), ACT.Copy).then_inc(sem("at_yh"), 1)
                act.wait_ge(sem("rt_done"), l * PAIRS + PAIRS)
                fn(HH[:, 4 * T:8 * T], A(60, 4 * T), ACT.Copy).then_inc(sem("at_yh"), 1)
                from_scratch(A(68, 8 * T), 0, 8, "gates_in")
                from_scratch(A(84, 8 * T), 16, 8, "gates_in")
                gemm512(f0 + 64)
                gemm512(f0 + 68)
                for j in range(8):
                    act.wait_ge(sem("mix_sum"), 16 * l + 16 + j + 1)
                    fn(XH[:, j * T:(j + 1) * T], A(16, T, j * T), ACT.Copy).then_inc(sem("mix_hi"), 1)
                gemm(f0 + 72, c0 + 21, 8)
                rms_norm(1)
                ffn(f0 + 80, c0 + 23, l * FT + FT)
                gemm2816(f0 + 124)

        @block.vector
        def _(dve):
            tt, ts, stt, cp = nc.vector.tensor_tensor, nc.vector.tensor_scalar, nc.vector.scalar_tensor_tensor, nc.vector.tensor_copy

            def drain():
                nc.vector.drain()

            def lo(dst, src, hi_part):
                return tt(dst, src, hi_part.bitcast(F32), ALU.subtract)

            def all_out(c):
                for b in range(4):
                    dve.wait_ge(chunk_out[b], quarter(c))

            def norm_lo(n, name):
                for q in range(4):
                    dve.wait_ge(sem(name + "_hi"), 4 * n + q + 1)
                    s = slice(2 * q * T, (2 * q + 2) * T)
                    lo(XL[:, s], A(0, 2 * T, 2 * q * T), XH[:, s]).then_inc(sem(name + "_x"), 1)

            def layer_norm(n, src, xc, rs, scale, bias, dst, done, modulation=None):
                dve.wait_ge(sem("ln_sum"), n + 1)
                for q in range(4):
                    stt(chunks(xc(2 * q, 2), T), bc(bank(4), 2), -1.0 / D, chunks(src(2 * q, 2), T), ALU.mult, ALU.add).then_inc(sem("ln_xc"), 1)
                if modulation:
                    weighted_rows()
                dve.wait_ge(sem("ln_rstd"), n + 1)
                for q in range(4):
                    tt(chunks(xc(2 * q, 2), T), chunks(xc(2 * q, 2), T), bc(rs, 2), ALU.mult)
                if modulation:
                    modulation()
                drain()
                for t in range(DT):
                    ins = ts(dst(t, 1), xc(t, 1), scale(t), bias(t), ALU.mult, ALU.add)
                    if t % 2:
                        ins.then_inc(sem(done), 1)

            def ffn(f, c, n0):
                with dve.Fori(0, FT // 2) as i:
                    for j in (1, 3):
                        k = j // 2
                        dve.wait_ge(chunk_out[j - 1], quarter(c) + i + 1)
                        dve.wait_ge(fill_done, f + 4 * i + j + 1)
                        tt(A(105, T, k * T), bank(j), A(88, T, k * T), ALU.mult).then_inc(chunk_out[j], 1)
                        dve.wait_ge(sem("ffn_hi"), n0 + 2 * i + k + 1)
                        at_ = bass.ds((2 * i + k) * T, T)
                        lo(HL[:, at_], A(105, T, k * T), HH[:, at_]).then_inc(sem("ffn_lo"), 1)

            def residual(f, c, n, step, scale=None):
                nc.vector.memset(A(ACC_KB), 0.0)
                with dve.Fori(0, 2) as i:
                    for j in range(4):
                        dve.wait_ge(fill_done, f + step * (4 * i + j + 1))
                        h = H[:, bass.ds((4 * i + j) * T, T)]
                        if scale:
                            stt(h, bank(j), scale(4 * i + j), h, ALU.mult, ALU.add).then_inc(chunk_out[j], 1)
                        else:
                            tt(h, bank(j), h, ALU.add).then_inc(chunk_out[j], 1)
                            drain()
                            tt(A(SQ_KB), h, h, ALU.mult)
                        drain()
                        ins = tt(A(ACC_KB), A(ACC_KB), h if scale else A(SQ_KB), ALU.add)
                    ins.then_inc(sem("acc"), 1)

            def Ht(t, n):
                return H[:, t * T:(t + n) * T]

            def at_kb(kb):
                return lambda t, n: A(kb, n * T, t * T)

            nc.vector.memset(small[:], 0.0)
            dve.wait_ge(sem("const_in"), 48)
            tt(lbt[:, 0:8], P1("lb0", 0, 8), P1("lb1", 0, 8), ALU.max)
            drain()
            tt(lbt[:, 8:16], P1("lb0", 0, 8), lbt[:, 0:8], ALU.subtract)
            tt(lbt[:, 16:24], P1("lb1", 0, 8), lbt[:, 0:8], ALU.subtract).then_inc(sem("lb_max"), 1)
            dve.wait_ge(sem("lb_exp"), 1)
            tt(lbt[:, 0:8], lbt[:, 8:16], lbt[:, 16:24], ALU.add)
            drain()
            nc.vector.reciprocal(lbt[:, 24:32], lbt[:, 0:8])
            drain()
            tt(lbs[:, 0:8], lbt[:, 8:16], lbt[:, 24:32], ALU.mult)
            drain()
            ts(lbs[:, 8:16], lbs[:, 0:8], -1.0, 1.0, ALU.mult, ALU.add)
            def weighted_rows():
                w = A(40 + 16, (ADA_FIRST - 4) * D).rearrange("p (t k c) -> p t k c", k=DT, c=128)
                dve.wait_ge(sem("cond"), 1)
                dve.wait_ge(sem("ada_in1"), 48)
                ts(w[:, :, 0, :], w[:, :, 0, :], cond[:, 0:1], None, ALU.mult)
                for kt in range(1, DT):
                    drain()
                    ins = stt(w[:, :, 0, :], w[:, :, kt, :], cond[:, kt:kt + 1], w[:, :, 0, :], ALU.mult, ALU.add)
                ins.then_inc(sem("cond"), 1)

            def modulation():
                dve.wait_ge(sem("ada_used"), 1)
                tt(mod[:, 0:ADA_FIRST], bank(6, ADA_FIRST), P1("b_ada", 0, ADA_FIRST), ALU.add)
                drain()
                ts(mod[:, 8:16], mod[:, 8:16], 1.0, None, ALU.add)

            layer_norm(0, Ht, at_kb(0), A(34), lambda t: mod[:, 8 + t:9 + t], lambda t: mod[:, t:t + 1], at_kb(0), "ln_u", modulation)
            norm_lo(0, "ln")
            ts(H[:], H[:], ALPHA, None, ALU.mult)
            nc.vector.memset(hg("ks", 2048), 0.0)
            nc.vector.memset(hg("state", 128), 0.0)
            nc.vector.memset(hg("st", 512), 0.0)
            all_out(32)
            with dve.Fori(0, HEADS) as h:
                drain()
                ts(hg("lf", T), A(44, T, h * T), lbs[:, bass.ds(h + 8, 1)], lbs[:, bass.ds(h, 1)], ALU.mult, ALU.add)
                drain()
                ts(hg("k", T), hg("lf", T), -1.0, 1.0, ALU.mult, ALU.add).then_inc(sem("hg_f"), 1)
                dve.wait_ge(sem("hg_lf"), h + 1)
                nc.vector.tensor_tensor_scan(hg("cum", T), C("chunk_start", T), hg("lf", T), 0.0, ALU.mult, ALU.add)
                drain()
                tt(hg("lf", T), hg("cum", T), hg("lf", T), ALU.subtract)
                drain()
                ref = chunks(hg("lf", T), SUB)[:, :, 0]
                tt(chunks(hg("qs", T), SUB), chunks(hg("cum", T), SUB), each(ref, SUB), ALU.subtract)
                last = chunks(hg("cum", T))[:, :, CHUNK - 1]
                tt(chunks(hg("kdec", T)), each(last, CHUNK), chunks(hg("cum", T)), ALU.subtract).then_inc(sem("hg_ex"), 1)
                ks = hg("ks", 2048).rearrange("p (c i s) -> p c i s", c=NCH, i=4)
                for s in range(4):
                    n = SUB * (s + 1)
                    ins = tt(ks[:, :, s, :n], each(chunks(hg("lf", T))[:, :, SUB * s], n), chunks(hg("cum", T))[:, :, :n], ALU.subtract)
                ins.then_inc(sem("hg_ks"), 1)
                dve.wait_ge(sem("hg_exp"), h + 1)
                q = A(0, T, h * T)
                tt(hg("qs", T), hg("qs", T), q, ALU.mult)
                tt(hg("qi", T), hg("e1", T), q, ALU.mult)
                tt(hg("kdec", T), hg("kdec", T), hg("k", T), ALU.mult)
                drain()
                cp(hg("val", T), A(60, T, h * T)).then_inc(sem("hg_q"), 1)
                dve.wait_ge(sem("hg_kse"), h + 1)
                kb = chunks(hg("k", T)).unsqueeze(2).broadcast_to([P, NCH, 4, CHUNK])
                tt(ks, ks, kb, ALU.mult).then_inc(sem("hg_k"), 1)
                dve.wait_ge(sem("hg_sc"), h + 1)
                for p0 in (0, 64):
                    r = slice(p0, p0 + 64)
                    ins = tt(chunks(hg("st", T), 128)[r, :, p0:p0 + 64], chunks(bank(6, 256))[r], bc(C("incl", 64)[r], 4), ALU.mult)
                ins.then_inc(sem("hg_st"), 1)
                dve.wait_ge(sem("hg_u"), h + 1)
                for c in range(NCH - 1):
                    e = hg("e1", T)[:, c * CHUNK + CHUNK - 1:c * CHUNK + CHUNK]
                    ins = stt(hg("state", 128, 128 * c + 128), hg("state", 128, 128 * c), e, bank(4 if c % 2 else 7, 128, 128 * (c // 2)), ALU.mult, ALU.add)
                    if c < NCH - 2:
                        drain()
                ins.then_inc(sem("hg_s"), 1)
                dve.wait_ge(sem("hg_rstd"), h + 1)
                tt(hg("o", T), bank(5), hg("rstd", T), ALU.mult)
                drain()
                stt(hg("o", T), hg("o", T), P1("hg_w"), A(16, T, h * T), ALU.mult, ALU.mult).then_inc(sem("hg_out"), 1)
                dve.wait_ge(sem("hg_hi"), h + 1)
                lo(HL[:, bass.ds(h * T, T)], hg("o", T), HH[:, bass.ds(h * T, T)]).then_inc(sem("hg_y"), 1)
            dve.wait_ge(sem("ada_done"), ADA_LATER)
            tt(mod[:, ADA_FIRST:48], bank(6, ADA_LATER, 256), P1("b_ada", ADA_FIRST, ADA_LATER), ALU.add)
            drain()
            ts(mod[:, 32:40], mod[:, 32:40], 1.0, None, ALU.add)
            dve.wait_ge(sem("gm_in"), 32)
            nc.vector.memset(chunks(A(32, 1024), 128)[64:128, :, 0:64], 0.0).then_inc(sem("gm_mask"), 1)
            all_out(48)
            layer_norm(1, at_kb(60), at_kb(60), A(105), lambda t: P1("gm_w", t), lambda t: P1("gm_b", t), at_kb(60), "ln_h")
            with dve.Fori(0, 8) as g:
                drain()
                cp(A(40), A(60, T, g * T)).then_inc(sem("gm_vs"), 1)
                dve.wait_ge(sem("gm_sv"), g + 1)
                tt(chunks(A(40), 128), chunks(bank(5), 128), bc(A(36, 128, g * 128), 4), ALU.add)
                drain()
                dve.wait_ge(sem("gm_gelu"), 8)
                tt(A(16, T, g * T), A(16, T, g * T), A(40), ALU.mult).then_inc(sem("gm_u"), 1)
            all_out(56)
            with dve.Fori(0, 2) as i:
                for j in range(4):
                    dve.wait_ge(fill_done, 56 + 4 * i + j + 1)
                    m = A(60, T, (4 * i + j) * T)
                    tt(m, bank(j), m, ALU.mult).then_inc(chunk_out[j], 1)
            for q in range(4):
                dve.wait_ge(sem("gm_hi"), q + 1)
                s = slice(2 * q * T, (2 * q + 2) * T)
                lo(HL[:, s], A(16, 2 * T, 2 * q * T), HH[:, s]).then_inc(sem("gm_lo"), 1)
            all_out(72)
            with dve.Fori(0, 2) as i:
                for j in range(4):
                    dve.wait_ge(fill_done, 72 + 4 * i + j + 1)
                    k = (4 * i + j) * T
                    tt(A(76, T, k), bank(j), A(76, T, k), ALU.mult).then_inc(chunk_out[j], 1)
                    drain()
                    tt(A(60, T, k), A(60, T, k), A(76, T, k), ALU.add).then_inc(sem("mix_sum"), 1)
                for j in range(4):
                    k = (4 * i + j) * T
                    dve.wait_ge(sem("mix_hi"), 4 * i + j + 1)
                    lo(XL[:, bass.ds(k, T)], A(60, T, k), XH[:, bass.ds(k, T)]).then_inc(sem("mix_lo"), 1)
            residual(80, 80, 8, 1, lambda c: mod[:, bass.ds(c + 16, 1)])
            drain()
            layer_norm(2, Ht, at_kb(0), A(34), lambda t: P1("ln1_w", t), lambda t: P1("ln1_b", t), Ht, "ln_h")
            layer_norm(3, Ht, at_kb(0), A(34), lambda t: mod[:, 32 + t:33 + t], lambda t: mod[:, 24 + t:25 + t], at_kb(0), "ln_u")
            norm_lo(1, "ln")
            ts(H[:], H[:], ALPHA, None, ALU.mult)
            ffn(88, 88, 0)
            residual(132, 132, 8, 3, lambda c: mod[:, bass.ds(c + 40, 1)])
            drain()
            layer_norm(4, Ht, at_kb(0), A(34), lambda t: P1("ln2_w", t), lambda t: P1("ln2_b", t), Ht, "ln_h")
            for h in range(2):
                dve.wait_ge(sem("ln_sq"), 20 + 2 * h + 2)
                tt(A(16 + 8 * h, 2 * T), A(16 + 8 * h, 2 * T), A(20 + 8 * h, 2 * T), ALU.add)
            drain()
            tt(A(16, 2 * T), A(16, 2 * T), A(24, 2 * T), ALU.add)
            drain()
            tt(A(ACC_KB), A(16), A(16, T, T), ALU.add).then_inc(sem("acc"), 2)

            with dve.Fori(0, LAYERS) as l:
                f0, c0 = l * FILLS_L + FILLS_1, l * (CHUNKS_L // 4) + CHUNKS_1 // 4

                def rms_norm(k, name):
                    n = 2 * l + k
                    dve.wait_ge(sem("rms_rstd"), n + 1)
                    for t in range(DT):
                        ins = stt(A(0, T, t * T), Ht(t, 1), P2(l, name, t), A(34), ALU.mult, ALU.mult)
                        if t % 2:
                            ins.then_inc(sem("rms_u"), 1)
                    norm_lo(n, "rms")

                rms_norm(0, "norm1")
                def shift(t, j, done):
                    z, d = A(16, T, t * T), A(60, T, j * T)
                    dve.wait_ge(chunk_out[j], done)
                    tt(d[:, 1:T], z[:, 0:T - 1], z[:, 1:T], ALU.subtract)
                    ts(d[:, 0:1], z[:, 0:1], -1.0, None, ALU.mult)
                    drain()
                    stt(z, d, P2(l, "mu", t), z, ALU.mult, ALU.add).then_inc(sem("rw_mix"), 1)

                for j in (2, 3):
                    shift(j - 2, j, c0 + 1)
                with dve.Fori(0, 3) as i:
                    drain()
                    for j in range(4):
                        shift(4 * i + j + 2, j, c0 + i + 2)
                dve.wait_ge(sem("rp_ss"), l + 1)
                ts(rp("rn", 4 * T), bank(4, 4 * T), 1e-24, None, ALU.max).then_inc(sem("rp_mx"), 1)
                dve.wait_ge(sem("rp_rn"), l + 1)
                nc.vector.reciprocal(rp("rn", 4 * T), rp("rn", 4 * T))
                with dve.Fori(0, PAIRS) as p:
                    n = l * PAIRS + p + 1
                    R, K, V = A(16, T, p * T), A(24, T, p * T), A(32, T, p * T)
                    SG, AA = A(76, T, p * T), A(44, T, p * T)
                    drain()
                    dve.wait_ge(sem("rw_lev"), 12 * l + 12)
                    nc.vector.tensor_tensor_scan(rp("cs", T), C("chunk_start", T), SG, 0.0, ALU.mult, ALU.add)
                    drain()
                    tt(rp("cx", T), rp("cs", T), SG, ALU.subtract).then_inc(sem("rp_cs"), 1)
                    stt(rp("kk", T), K, P2(l, "k_k", p), A(0, T, p * T), ALU.mult, ALU.mult)
                    drain()
                    tt(rp("kb", T), rp("kk", T), AA, ALU.mult)
                    ts(AA, AA, -1.0, P2(l, "k_a", p), ALU.add, ALU.mult)
                    drain()
                    stt(AA, AA, 1.0, K, ALU.add, ALU.mult)
                    drain()
                    stt(rp("rk", T), R, P2(l, "r_k", p), AA, ALU.mult, ALU.mult).then_inc(sem("rp_rk"), 1)
                    ar = A(60, 2 * T, p * 2 * T).rearrange("p (c k t) -> p c k t", c=NCH, k=2)
                    dve.wait_ge(sem("rp_e"), n)
                    stt(ar[:, :, 0, :], chunks(rp("kk", T)), -1.0, chunks(rp("ex", T)), ALU.mult, ALU.mult)
                    tt(ar[:, :, 1, :], chunks(R), chunks(rp("e", T)), ALU.mult)
                    cp(rc("el", 8, 8 * p), chunks(rp("e", T))[:, :, CHUNK - 1])
                    tt(SG, rp("kb", T), rp("ei", T), ALU.mult)
                    tt(K, AA, rp("ei", T), ALU.mult)
                    drain()
                    dve.wait_ge(sem("rp_bn"), n)
                    tt(R, bank(5), V, ALU.mult).then_inc(sem("rp_done"), 1)
                for name in ("p", "us", "u"):
                    nc.vector.memset(rc(name, 512), 0.0)
                nc.vector.memset(rc("state_c", 256), 0.0)
                nc.vector.memset(rc("state", 512), 0.0).then_inc(sem("rc_st"), 1)
                with dve.Fori(0, NCH) as c:
                    n = l * NCH + c + 1

                    def level(dst, b, mask):
                        return tt(chunks(dst), chunks(bank(b)), bc(mask, 2 * PAIRS), ALU.mult)

                    def plus_identity(name):
                        return tt(chunks(rc(name, 256)), chunks(rc(name, 256)), bc(C("eye64", 64), PAIRS), ALU.add)

                    def both_blocks(name, src):
                        for h in range(2):
                            r = slice(64 * h, 64 * h + 64)
                            ins = cp(chunks(rc(name, 512), 128)[r, :, 64 * h:64 * h + 64], chunks(rc(src, 256))[r])
                        return ins

                    drain()
                    dve.wait_ge(sem("rc_s1"), n)
                    tt(chunks(rc("t_c", 256)), chunks(bank(5, 256)), bc(C("lower0", 64), PAIRS), ALU.mult)
                    level(rc("ak", 512), 6, C("upper", 64))
                    dve.wait_ge(sem("rc_s2"), n)
                    for h in range(2):
                        r = slice(64 * h, 64 * h + 64)
                        tt(chunks(rc("u_c", 256))[r], chunks(bank(4), 128)[r, :, 64 * h:64 * h + 64], bc(C("level", 64)[r], PAIRS), ALU.mult)
                    level(rc("rbk", 512), 7, C("incl", 64)).then_inc(sem("rc_out"), 1)
                    level(rc("al", 512), 4, C("level", 64, 64))
                    drain()
                    plus_identity("t_c")
                    plus_identity("u_c")
                    drain()
                    both_blocks("u", "u_c").then_inc(sem("rc_al"), 1)
                    for v in range(1, 6):
                        if v < 5:
                            dve.wait_ge(sem("rc_p"), 5 * n - 5 + v)
                            level(rc("al", 512), 4, C("level", 64, 64 * (v + 1)))
                            dve.wait_ge(sem("rc_d"), 4 * n - 4 + v)
                            tt(rc("t_c", 256), rc("t_c", 256), bank(6, 256), ALU.add).then_inc(sem("rc_al"), 1)
                        dve.wait_ge(sem("rc_e"), 5 * n - 5 + v)
                        tt(rc("u_c", 256), rc("u_c", 256), bank(7, 256), ALU.add)
                        drain()
                        both_blocks("u", "u_c").then_inc(sem("rc_uu"), 1)
                    dve.wait_ge(sem("rc_n"), n)
                    tt(rc("state_c", 256), rc("state_c", 256), bank(4, 256), ALU.add)
                    drain()
                    dve.wait_ge(sem("rc_yc"), n)
                    el = chunks(rc("el", 32), 8)[:, :, bass.ds(c, 1)].broadcast_to([P, PAIRS, 64])
                    tt(chunks(rc("state_c", 256)), chunks(rc("state_c", 256)), el, ALU.mult)
                    drain()
                    both_blocks("state", "state_c").then_inc(sem("rc_st"), 1)
                two_pairs = lambda kb, h: A(kb, 2 * T, 2 * h * T)
                for h in range(2):
                    dve.wait_ge(sem("ro_m"), 2 * l + h + 1)
                    stt(two_pairs(92, h), bank(4 + 2 * h, 2 * T), -1.0 / 64, two_pairs(84, h), ALU.mult, ALU.add).then_inc(sem("ro_c"), 1)
                for h in range(2):
                    y = two_pairs(92, h)
                    dve.wait_ge(sem("ro_r"), 2 * l + h + 1)
                    tt(y, y, two_pairs(24, h), ALU.mult)
                    drain()
                    for p in (2 * h, 2 * h + 1):
                        ts(A(92, T, p * T), A(92, T, p * T), P2(l, "ln_g", p), P2(l, "ln_b", p), ALU.mult, ALU.add)
                    drain()
                    tt(y, y, two_pairs(16, h), ALU.add)
                    drain()
                    tt(y, y, two_pairs(52, h), ALU.mult).then_inc(sem("ro_y"), 1)
                for h in range(2):
                    dve.wait_ge(sem("ro_h"), 2 * l + h + 1)
                    s = slice(2 * h * T, (2 * h + 2) * T)
                    lo(HL[:, s], two_pairs(92, h), HH[:, s]).then_inc(sem("ro_l"), 1)

                def gated(f, c, gate, first, h0):
                    for j in range(8):
                        if j % 2:
                            dve.wait_ge(fill_done, f + j // 2 + 1)
                        else:
                            dve.wait_ge(half_done, l * 12 + h0 + j // 2 + 1)
                        m, g = A(16, T, j * T), A(gate, T, j * T)
                        if first:
                            tt(m, bank(j % 4), g, ALU.mult).then_inc(chunk_out[j % 4], 1)
                        else:
                            tt(g, bank(j % 4), g, ALU.mult).then_inc(chunk_out[j % 4], 1)
                            drain()
                            tt(m, m, g, ALU.add).then_inc(sem("mix_sum"), 1)

                dve.wait_ge(sem("ro_h"), 2 * l + 2)
                dve.wait_ge(sem("gate_b_in"), 16 * l + 16)
                gated(f0 + 48, c0 + 12, 60, True, 0)
                all_out(c0 + 17)
                dve.wait_ge(sem("ak_rs"), l + 1)
                stt(at("kn", T), A(12), P2(l, "kg"), at("rs", T), ALU.mult, ALU.mult).then_inc(sem("ak_n"), 1)
                nc.vector.memset(at("sc", 128), MASKED)
                nc.vector.memset(rt("state", 128), 0.0)
                with dve.Fori(0, 2) as j:
                    with dve.Fori(0, 2) as i:
                        n = l * PAIRS + 2 * j + i
                        p = 2 * j + i

                        def scores(hh):
                            dve.wait_ge(sem("at_sc"), 2 * n + hh + 1)
                            stt(at("sc", 128, 128), bank(4, 128, 128), 0.125, C("band", 128, 128), ALU.mult, ALU.add)
                            stt(chunks(at("sc", 768, 256), 256), chunks(bank(4, 768, 256), 256), 0.125, bc(C("band", 256), 3), ALU.mult, ALU.add)
                            drain()
                            nc.vector.reduce_max(small[:, 24:28], chunks(at("sc", 1024), 256), AX.X)
                            drain()
                            ts(small[:, 0:4], small[:, 24:28], P2(l, "sinks", 2 * p + hh), -1.0, ALU.max, ALU.mult).then_inc(sem("at_m"), 1)

                        def normalise(hh):
                            dve.wait_ge(sem("at_p"), 2 * n + hh + 1)
                            tt(small[:, 32:36], small[:, 8:12], small[:, 16:20], ALU.add)
                            drain()
                            nc.vector.reciprocal(small[:, 36:40], small[:, 32:36])
                            drain()
                            pb = chunks(at("pb", 1024), 256)
                            tt(pb, pb, each(small[:, 36:40], 256), ALU.mult).then_inc(sem("at_pn"), 1)

                        q, k = A(60, T, p * T), A(68, T, p * T)
                        drain()
                        dve.wait_ge(sem("ak_kv"), l + 1)
                        dve.wait_ge(sem("table_in"), 16 * l + 16)
                        dve.wait_ge(sem("rq_in"), 16 * l + 16)
                        cp(at("kj", T), at("kd", T, j * T))
                        cp(chunks(at("vj", 256)), chunks(at("vt", T), 128)[:, :, bass.ds(64 * j, 64)])
                        cp(rt("vs", T), A(76, T, p * T)).then_inc(sem("rt_in"), 1)
                        tt(rt("qr", T), q, TB("cos", T), ALU.mult)
                        stt(rt("kr", T), k, 0.125, TB("cos", T), ALU.mult, ALU.mult)
                        dve.wait_ge(sem("at_rs"), n + 1)
                        stt(at("qs", T), A(52, T, p * T), P2(l, "qg"), at("rs", T), ALU.mult, ALU.mult).then_inc(sem("at_q"), 1)
                        dve.wait_ge(sem("rt_rot"), n + 1)
                        tt(rt("t1", T), bank(0), TB("sin", T), ALU.mult)
                        stt(rt("t2", T), bank(1), 0.125, TB("sin", T), ALU.mult, ALU.mult)
                        drain()
                        tt(rt("qr", T), rt("qr", T), rt("t1", T), ALU.add)
                        tt(rt("kr", T), rt("kr", T), rt("t2", T), ALU.add)
                        drain()
                        tt(chunks(rt("qx", T), 128), chunks(rt("qr", T), 128), bc(TB("xi", 128, 128 * p), 4), ALU.mult)
                        tt(chunks(rt("kz", T), 128), chunks(rt("kr", T), 128), bc(TB("zeta", 128, 128 * p), 4), ALU.mult).then_inc(sem("rt_qk"), 1)
                        scores(0)
                        dve.wait_ge(sem("rt_sc"), n + 1)
                        for hh in range(2):
                            tt(chunks(rt("st", T, T * hh), 128), chunks(bank(hh), 128), bc(TB("dmat", 128, 128 * (2 * p + hh)), 4), ALU.mult)
                        normalise(0)
                        scores(1)
                        dve.wait_ge(sem("rt_kv"), n + 1)
                        tt(chunks(rt("t1", 384), 128), chunks(bank(3, 384), 128), bc(C("blk1", 128), 3), ALU.mult)
                        drain()
                        for b in range(NBLK - 1):
                            ins = stt(rt("state", 128, 128 * b + 128), rt("state", 128, 128 * b), C("cd", 1, p), rt("t1", 128, 128 * b), ALU.mult, ALU.add)
                            if b < NBLK - 2:
                                drain()
                        ins.then_inc(sem("rt_r"), 1)
                        normalise(1)
                        dve.wait_ge(sem("rt_rs"), n + 1)
                        tt(rt("t2", T), bank(2), rt("rs", T), ALU.mult)
                        drain()
                        tt(q, rt("t2", T), A(84, T, p * T), ALU.mult).then_inc(sem("rt_done"), 1)
                        dve.wait_ge(sem("at_o"), 2 * n + 2)
                dve.wait_ge(sem("at_ao"), l * PAIRS + PAIRS)
                dve.wait_ge(sem("at_yh"), 2 * l + 1)
                lo(HL[:, 0:4 * T], A(52, 4 * T), HH[:, 0:4 * T]).then_inc(sem("at_y"), 1)
                drain()
                dve.wait_ge(sem("at_yh"), 2 * l + 2)
                lo(HL[:, 4 * T:8 * T], A(60, 4 * T), HH[:, 4 * T:8 * T]).then_inc(sem("at_y"), 1)
                dve.wait_ge(sem("gates_in"), 32 * l + 32)
                gated(f0 + 64, c0 + 17, 68, False, 4)
                gated(f0 + 68, c0 + 19, 84, False, 8)
                for j in range(8):
                    dve.wait_ge(sem("mix_hi"), 8 * l + 8 + j + 1)
                    lo(XL[:, j * T:(j + 1) * T], A(16, T, j * T), XH[:, j * T:(j + 1) * T]).then_inc(sem("mix_lo"), 1)
                residual(f0 + 72, c0 + 21, 8, 1)
                rms_norm(1, "norm2")
                ffn(f0 + 80, c0 + 23, l * FT + FT)
                residual(f0 + 124, c0 + 34, 8, 3)


def columns_of(v):
    return v.reshape(-1, P).T


def shape_constants():
    con = np.zeros((P, N_CONST), np.float32)

    def put(name, a):
        con[:, CONST[name]:CONST[name] + a.shape[1]] = a

    r = np.arange(P)
    half, i64 = r % 64, np.arange(64)
    put("ident", np.eye(P))
    put("ones", np.ones((P, P)))
    put("blk1", (r[:, None] // 64 == r[None, :] // 64))
    put("chunk_start", np.broadcast_to(np.arange(T)[None] % CHUNK != 0, (P, T)))
    put("upper", half[:, None] < i64[None])
    put("incl", half[:, None] <= i64[None])
    put("lower0", (half[:, None] // 2 == i64[None] // 2) & (half[:, None] % 2 == 1) & (i64[None] % 2 == 0))
    levels = [(half[:, None] // (2 * b) == i64[None] // (2 * b)) & (half[:, None] // b % 2 == 0) & (i64[None] // b % 2 == 1)
              for b in (1, 2, 4, 8, 16, 32)]
    put("level", np.concatenate(levels, axis=1))
    put("eye64", half[:, None] == i64[None])
    key = np.arange(2 * BLK)
    seen = (key[None] > r[:, None]) & (key[None] <= r[:, None] + BLK)
    put("band", np.where(seen, 0.0, MASKED))
    put("dup", np.concatenate([r[:, None] == 64 * j + half[None] for j in range(2)], axis=1))
    put("eps", np.broadcast_to(np.float32([[1e-5, 1e-6, 64e-5, 0.0]]), (P, 4)))

    table = np.zeros((P, N_TABLE), np.float32)

    def put_t(name, a):
        table[:, TABLE[name]:TABLE[name] + a.shape[1]] = a

    inv = np.float32(1.0) / np.power(np.float32(10000.0), np.arange(32, dtype=np.float32) * np.float32(2.0) / np.float32(64))
    angle = np.arange(T, dtype=np.float32)[None] * inv[r % 32][:, None].astype(np.float32)
    put_t("cos", np.cos(angle))
    put_t("sin", np.sin(angle))
    lg = np.log1p(-np.power(2.0, -5.0 - np.arange(HEADS)))
    pos = np.arange(BLK)
    diff = pos[None] - pos[:, None]
    put_t("dmat", np.concatenate([np.where(diff >= 0, np.exp(g * np.maximum(diff, 0)), 0.0) for g in lg], axis=1))
    of = lambda p: lg[2 * p + r // 64][:, None]
    put_t("xi", np.concatenate([np.exp(of(p) * (pos[None] + 1.0)) for p in range(PAIRS)], axis=1))
    put_t("zeta", np.concatenate([np.exp(of(p) * (BLK - 1.0 - pos[None])) for p in range(PAIRS)], axis=1))
    put("cd", np.concatenate([np.exp(of(p) * BLK) for p in range(PAIRS)], axis=1))
    rot = np.zeros((P, P))
    for m in range(P):
        rot[m + 32 if m % 64 < 32 else m - 32, m] = -1.0 if m % 64 < 32 else 1.0
    put_t("rot", rot)
    return con, table


def kernel(**inputs):
    import concourse.bacc as bacc
    from concourse.bass_utils import run_bass_kernel_spmd

    a = {k: np.asarray(v) for k, v in inputs.items()}

    def fills_of(w):
        k, n = w.shape
        t = w.reshape(k // P, P, n // P, P).transpose(2, 1, 0, 3)
        if k == D:
            return t.reshape(n // P, P, 8 * P)
        if k == D // 2:
            return t.reshape(n // P // 2, 2, P, 4 * P).transpose(0, 2, 1, 3).reshape(n // P // 2, P, 8 * P)
        t = np.pad(t, ((0, 0), (0, 0), (0, 24 - k // P), (0, 0)))
        return t.reshape(n // P, P, 3, 8 * P).transpose(0, 2, 1, 3).reshape(n // P * 3, P, 8 * P)

    def turns(parts, order):
        out, at = [], [0] * len(parts)
        while at[0] < len(parts[0]):
            for k, m in enumerate(order):
                out.append(parts[k][at[k]:at[k] + m])
                at[k] += m
        return np.concatenate(out)

    w_in = fills_of(a["w_in"][0])
    zq, zf, zi, zg, zu, zv, ga, gb = (w_in[8 * k:8 * k + 8] for k in range(8))
    ffn = fills_of(a["w_ffn_in"][0])
    fills = [turns([zq, zg, zf, zi], [1, 1, 1, 1]), turns([zu, zv], [2, 2]), ga, fills_of(a["w_proj_a"][0]), gb,
             fills_of(a["w_proj_b"][0]), fills_of(a["w_out"][0]), turns([ffn[:FT], ffn[FT:]], [1, 1]), fills_of(a["w_ffn_out"][0])]
    for l in range(LAYERS):
        w = fills_of(a["w_in_2"][l])
        aq, ak, av, rw, ret = w[0:4], w[4:5], w[5:6], w[6:20], w[20:36]
        gates = [w[36 + 8 * k:44 + 8 * k] for k in range(3)]
        gated = turns([gates[0], gates[1], gates[2], np.concatenate([aq, ret[:4]])], [1, 1, 1, 1])
        fills += [ak, av, rw, gated, fills_of(a["w_rwkv_o_2"][l]), ret[4:], fills_of(a["w_attn_o_2"][l]),
                  fills_of(a["w_ret_o_2"][l]), fills_of(a["w_out_2"][l]),
                  turns([fills_of(a["w_ffn_gate_2"][l]), fills_of(a["w_ffn_up_2"][l])], [1, 1]), fills_of(a["w_ffn_down_2"][l])]
    fills.append(np.zeros((LEAD, P, 8 * P), np.float32))
    fills = np.concatenate(fills)
    assert fills.shape[0] == FILLS
    ada = fills_of(a["w_ada"][0])[ADA_FIRST:]
    parts = {"F": list(fills[FILLS_HG:]), "A": list(ada)}
    stream = [parts[x].pop(0) for _ in range(HEADS // 2) for x in ORDER]
    fills = np.concatenate([fills[:FILLS_HG], np.stack(stream), fills[FILLS_HG + 4 * HEADS // 2:]])

    con, table = shape_constants()
    ln = lambda name: columns_of(a[name][0])
    par1 = np.concatenate([columns_of(a["c"][0]), ln("b_ada"), columns_of(a["hgrn_lb_logits"][0]), columns_of(a["hgrn_lb_logits"][1]),
                           ln("hgrn_norm_w"), ln("gmlp_ln_w"), ln("gmlp_ln_b"), columns_of(a["b_gate"][0].reshape(-1)),
                           ln("ln1_w"), ln("ln1_b"), ln("ln2_w"), ln("ln2_b")], axis=1)
    twice = lambda v: np.concatenate([v, v])[:, None]
    par2 = np.concatenate([np.concatenate(
        [columns_of(a["norm1_g_2"][l]), columns_of(a["norm2_g_2"][l]), twice(a["attn_q_norm_g_2"][l]), twice(a["attn_k_norm_g_2"][l]),
         np.broadcast_to(a["attn_sinks_2"][l][None], (P, HEADS)), columns_of(a["rwkv_shift_mu_2"][l])]
        + [columns_of(a[f"rwkv_{n}_2"][l].reshape(-1)) for n in ("w0", "a0", "k_k", "k_a", "r_k", "lnx_g", "lnx_b")], axis=1)
        for l in range(LAYERS)], axis=1)
    arrays = {
        "x": a["x"][0].reshape(T, DT, P).transpose(2, 1, 0).reshape(P, DT * T),
        "w_ada": a["w_ada"][0][:, :ADA_FIRST * P].reshape(DT, P, 4, 4, P).transpose(2, 1, 3, 0, 4).reshape(4, P, 16 * KB),
        "fills": fills, "con": con, "table": table, "par1": par1, "par2": par2,
        "gm_ws": a["gmlp_ws"][0].transpose(2, 0, 1).reshape(P, 8 * P),
        "gm_bs": a["gmlp_bs"][0].reshape(1, 8 * P),
        "lora": np.concatenate([np.concatenate([a["rwkv_w2_2"], a["rwkv_a2_2"]], axis=1), a["rwkv_g2_2"]], axis=2),
    }
    arrays = {k: np.ascontiguousarray(v) for k, v in arrays.items()}
    nc = bacc.Bacc("TRN2", target_bir_lowering=False, num_devices=1)
    dram = {k: nc.dram_tensor("in_" + k, v.shape, F32, kind="ExternalInput").ap() for k, v in arrays.items()}
    out = nc.dram_tensor("out", (P, DT * T), F32, kind="ExternalOutput").ap()
    scratch = nc.dram_tensor("scratch", (LAYERS * 32, P, T), F32, kind="Internal").ap()
    build(nc, dram, out, scratch)
    r = run_bass_kernel_spmd(nc, [{"in_" + k: v for k, v in arrays.items()}], core_ids=[0])
    got = np.asarray(r.results[0]["out"])
    return np.ascontiguousarray(got.reshape(P, DT, T).transpose(2, 1, 0).reshape(1, T, D))
```
